# Optimizing a Trainium2 kernel written in Bass

```python
import math
import jax, jax.numpy as jnp
from jax import lax
import numpy as np

D_MODEL = 1024
BATCH = 1
SEQ = 256
DEPTH = 1
DEC_BATCH = 8
DEC_SEQ = 1
PAST_LEN = 2048
PAGE_SIZE = 128

SSD_HEADS = 16
SSD_HEADDIM = 64
SSD_D = SSD_HEADS * SSD_HEADDIM
SSD_GROUPS = 2
D_STATE = 128
CONV_W = 4
CONV_DIM = SSD_D + 2 * SSD_GROUPS * D_STATE
SSD_CHUNK = 64
HG_HEADS = 8
HG_DK = 128
HG_DV = 128
HG_D = HG_HEADS * HG_DV
HG_CHUNK = 32
D_MIX = SSD_D + HG_D
IN_SPLITS = (SSD_D, CONV_DIM, SSD_HEADS, HG_HEADS * HG_DK, HG_HEADS * HG_DK, HG_D, HG_D)
IN_COLS = sum(IN_SPLITS)
N_EGROUPS = 4
EXPERTS_PER_GROUP = 4
N_EXPERTS = N_EGROUPS * EXPERTS_PER_GROUP
EXPERT_FF = 512
TOP_K = 2
PLE_DIM = 256
EPS = 1e-6

kernel_name = 'hybrid_ssd_hgrn2_hmoe_decode_step'

def _rms_unit(x):
    x32 = x.astype(jnp.float32)
    return x32 * lax.rsqrt(jnp.mean(x32 * x32, axis=-1, keepdims=True) + EPS)

def rmsnorm(x, w):
    return (_rms_unit(x) * w.astype(jnp.float32)).astype(x.dtype)

def causal_dwconv(x, buf, w, b):
    xp = jnp.concatenate([buf.astype(x.dtype), x], axis=1)
    out = lax.conv_general_dilated(
        xp, w[:, None, :].astype(x.dtype), window_strides=(1,), padding='VALID',
        dimension_numbers=('NWC', 'WIO', 'NWC'), feature_group_count=x.shape[-1])
    return out + b.astype(x.dtype), xp[:, -(CONV_W - 1):]

def _segsum(a):
    T = a.shape[-1]
    ar = jnp.broadcast_to(a[..., :, None], a.shape + (T,))
    ar = jnp.where(jnp.tril(jnp.ones((T, T), bool), -1), ar, 0.0)
    cs = jnp.cumsum(ar, axis=-2)
    return jnp.where(jnp.tril(jnp.ones((T, T), bool)), cs, -jnp.inf)

def _pad_seq(t, pad):
    return jnp.pad(t, [(0, 0), (0, pad)] + [(0, 0)] * (t.ndim - 2))

def ssd_chunked(x, dt, a_head, b_in, c_in, h0):
    bsz, L, H, P = x.shape
    Q = min(SSD_CHUNK, L)
    nc = -(-L // Q)
    pad = nc * Q - L
    rep = H // b_in.shape[2]
    bh = jnp.repeat(b_in, rep, axis=2)
    ch = jnp.repeat(c_in, rep, axis=2)
    N = bh.shape[-1]
    xdt = x * dt[..., None]
    a = dt * a_head
    xdt, a, bh, ch = (_pad_seq(t, pad) for t in (xdt, a, bh, ch))
    xdt = xdt.reshape(bsz, nc, Q, H, P)
    bh = bh.reshape(bsz, nc, Q, H, N)
    ch = ch.reshape(bsz, nc, Q, H, N)
    a = a.reshape(bsz, nc, Q, H).transpose(0, 3, 1, 2)
    a_cs = jnp.cumsum(a, axis=-1)
    lmat = jnp.exp(_segsum(a))
    y_diag = jnp.einsum('bclhn,bcshn,bhcls,bcshp->bclhp', ch, bh, lmat, xdt)
    decay_states = jnp.exp(a_cs[..., -1:] - a_cs)
    states = jnp.einsum('bclhn,bhcl,bclhp->bchpn', bh, decay_states, xdt)
    states = jnp.concatenate([h0[:, None], states], axis=1)
    chunk_a = jnp.pad(a_cs[..., -1], [(0, 0), (0, 0), (1, 0)])
    decay_chunk = jnp.exp(_segsum(chunk_a))
    new_states = jnp.einsum('bhzc,bchpn->bzhpn', decay_chunk, states)
    states_in, h_last = new_states[:, :-1], new_states[:, -1]
    y_off = jnp.einsum('bclhn,bchpn,bhcl->bclhp', ch, states_in, jnp.exp(a_cs))
    y = (y_diag + y_off).reshape(bsz, nc * Q, H, P)[:, :L]
    return y, h_last

def hgrn2_chunked(q, logf, k, v, s0):
    bsz, L, H, K = q.shape
    Q = min(HG_CHUNK, L)
    nc = -(-L // Q)
    pad = nc * Q - L
    q, logf, k, v = (_pad_seq(t, pad) for t in (q, logf, k, v))
    to_chunks = lambda t: t.reshape(bsz, nc, Q, H, t.shape[-1]).swapaxes(0, 1)
    causal = jnp.tril(jnp.ones((Q, Q), bool))[None, :, :, None, None]

    def step(s, inp):
        qc, gc, kc, vc = inp
        gcs = jnp.cumsum(gc, axis=1)
        o_inter = jnp.einsum('blhk,bhkv->blhv', qc * jnp.exp(gcs), s)
        diff = gcs[:, :, None] - gcs[:, None, :]
        decay = jnp.exp(jnp.where(causal, diff, -jnp.inf))
        attn = jnp.einsum('bihk,bjhk,bijhk->bhij', qc, kc, decay)
        o_intra = jnp.einsum('bhij,bjhv->bihv', attn, vc)
        g_last = gcs[:, -1]
        s_new = jnp.exp(g_last)[..., None] * s + jnp.einsum(
            'blhk,blhv->bhkv', kc * jnp.exp(g_last[:, None] - gcs), vc)
        return s_new, o_inter + o_intra

    s_last, o = lax.scan(step, s0, (to_chunks(q), to_chunks(logf), to_chunks(k), to_chunks(v)))
    o = o.swapaxes(0, 1).reshape(bsz, nc * Q, H, v.shape[-1])[:, :L]
    return o, s_last

def token_mixer(h, conv_buf, ssm0, hg0, lb, w_in, conv_w, conv_b, dt_bias, a_log, d_skip,
                ssd_norm_w, hg_norm_w, w_out):
    f32 = jnp.float32
    bsz, L, _ = h.shape
    offs = [int(o) for o in np.cumsum(IN_SPLITS)[:-1]]
    proj = h @ w_in
    z, xbc, dt_raw, q, f_raw, v, g = jnp.split(proj, offs, axis=-1)
    xbc, conv_new = causal_dwconv(xbc, conv_buf, conv_w, conv_b)
    xbc = jax.nn.silu(xbc)
    xs, b_in, c_in = jnp.split(xbc, [SSD_D, SSD_D + SSD_GROUPS * D_STATE], axis=-1)
    xs = xs.astype(f32).reshape(bsz, L, SSD_HEADS, SSD_HEADDIM)
    b_in = b_in.astype(f32).reshape(bsz, L, SSD_GROUPS, D_STATE)
    c_in = c_in.astype(f32).reshape(bsz, L, SSD_GROUPS, D_STATE)
    dt = jax.nn.softplus(dt_raw.astype(f32) + dt_bias.astype(f32))
    a_head = -jnp.exp(a_log.astype(f32))
    y, ssm_new = ssd_chunked(xs, dt, a_head, b_in, c_in, ssm0.astype(f32))
    y = y + d_skip.astype(f32)[:, None] * xs
    y = y.reshape(bsz, L, SSD_D) * jax.nn.silu(z.astype(f32))
    y = _rms_unit(y.reshape(bsz, L, SSD_GROUPS, SSD_D // SSD_GROUPS)).reshape(bsz, L, SSD_D)
    y = y * ssd_norm_w.astype(f32)
    f_raw = f_raw.astype(f32)
    fgate = lb + (1.0 - lb) * jax.nn.sigmoid(f_raw)
    kk = (1.0 - lb) * jax.nn.sigmoid(-f_raw)
    shp = (bsz, L, HG_HEADS, HG_DK)
    o, hg_new = hgrn2_chunked(q.astype(f32).reshape(shp), jnp.log(fgate).reshape(shp),
                              kk.reshape(shp), v.astype(f32).reshape(bsz, L, HG_HEADS, HG_DV),
                              hg0.astype(f32))
    o = _rms_unit(o).reshape(bsz, L, HG_D) * hg_norm_w.astype(f32) * jax.nn.silu(g.astype(f32))
    mixed = jnp.concatenate([y, o], axis=-1).astype(h.dtype)
    return mixed @ w_out, conv_new, ssm_new.astype(h.dtype), hg_new.astype(h.dtype)

def hier_moe(h, w_rg, b_rg, w_re, b_re, w_gate, w_up, w_down):
    f32 = jnp.float32
    bsz, L, D = h.shape
    t = h.reshape(bsz * L, D)
    glog = (t @ w_rg).astype(f32)
    gprob = jax.nn.softmax(glog, axis=-1)
    gsel = jnp.argmax(glog + b_rg.astype(f32), axis=-1)
    gw = jnp.take_along_axis(gprob, gsel[:, None], axis=-1)
    elog = (t @ w_re).astype(f32).reshape(-1, N_EGROUPS, EXPERTS_PER_GROUP)
    elog = jnp.take_along_axis(elog, gsel[:, None, None], axis=1)[:, 0]
    eprob = jax.nn.softmax(elog, axis=-1)
    _, topi = lax.top_k(elog + b_re.astype(f32)[gsel], TOP_K)
    ew = jnp.take_along_axis(eprob, topi, axis=-1)
    ew = ew / jnp.sum(ew, axis=-1, keepdims=True)
    eid = gsel[:, None] * EXPERTS_PER_GROUP + topi
    gates = jnp.sum(jax.nn.one_hot(eid, N_EXPERTS, dtype=f32) * (gw * ew)[..., None], axis=1)
    hg = jnp.einsum('nd,edf->nef', t, w_gate)
    hu = jnp.einsum('nd,edf->nef', t, w_up)
    act = jax.nn.silu(hg) * hu * gates[..., None].astype(t.dtype)
    return jnp.einsum('nef,efd->nd', act, w_down).reshape(bsz, L, D)

def trunk(x, p, ssm_in, conv_in, hg_in, W):
    f32 = jnp.float32
    lb_all = jnp.cumsum(jax.nn.softmax(W['lb_logits'].astype(f32), axis=0), axis=0)
    ssm_out, conv_out, hg_out = [], [], []
    for i in range(DEPTH):
        h = rmsnorm(x, W['norm_mix_w'][i])
        mix, conv_new, ssm_new, hg_new = token_mixer(
            h, conv_in[i], ssm_in[i], hg_in[i], lb_all[i], W['w_in'][i], W['conv_w'][i],
            W['conv_b'][i], W['dt_bias'][i], W['a_log'][i], W['d_skip'][i],
            W['ssd_norm_w'][i], W['hg_norm_w'][i], W['w_out'][i])
        x = x + mix
        x = x + hier_moe(rmsnorm(x, W['norm_ffn_w'][i]), W['w_router_group'][i],
                         W['b_router_group'][i], W['w_router_expert'][i],
                         W['b_router_expert'][i], W['w_exp_gate'][i], W['w_exp_up'][i],
                         W['w_exp_down'][i])
        gate = jax.nn.sigmoid((rmsnorm(x, W['norm_ple_w'][i]) @ W['w_ple_gate'][i]).astype(f32))
        x = x + (gate * (p[i] @ W['w_ple_proj'][i]).astype(f32)).astype(x.dtype)
        ssm_out.append(ssm_new)
        conv_out.append(conv_new)
        hg_out.append(hg_new)
    y = rmsnorm(x, W['final_norm_w'])
    return y, jnp.stack(ssm_out), jnp.stack(conv_out), jnp.stack(hg_out)

def setup_inputs(seed: int = 0) -> dict:
    key = jax.random.key(seed)
    ks = jax.random.split(key, 32)
    f32 = jnp.float32

    def nrm(k, shape, scale):
        return jax.random.normal(k, shape, f32) * scale

    dt0 = jnp.exp(jax.random.uniform(ks[10], (DEPTH, SSD_HEADS), f32,
                                     math.log(1e-3), math.log(1e-1)))
    return {
        'x_prompt': nrm(ks[0], (BATCH, SEQ, D_MODEL), 1.0),
        'x_sample': nrm(ks[1], (DEC_BATCH, DEC_SEQ, D_MODEL), 1.0),
        'state_ssm': nrm(ks[2], (DEPTH, DEC_BATCH, SSD_HEADS, SSD_HEADDIM, D_STATE), 0.5),
        'state_conv': nrm(ks[3], (DEPTH, DEC_BATCH, CONV_W - 1, CONV_DIM), 1.0),
        'state_hgrn': nrm(ks[4], (DEPTH, DEC_BATCH, HG_HEADS, HG_DK, HG_DV), 0.5),
        'p_prompt': nrm(ks[5], (DEPTH, BATCH, SEQ, PLE_DIM), 1.0),
        'p_sample': nrm(ks[6], (DEPTH, DEC_BATCH, DEC_SEQ, PLE_DIM), 1.0),
        'norm_mix_w': 1.0 + nrm(ks[7], (DEPTH, D_MODEL), 0.02),
        'w_in': nrm(ks[8], (DEPTH, D_MODEL, IN_COLS), D_MODEL ** -0.5),
        'conv_w': nrm(ks[9], (DEPTH, CONV_W, CONV_DIM), CONV_W ** -0.5),
        'conv_b': nrm(ks[11], (DEPTH, CONV_DIM), 0.02),
        'dt_bias': dt0 + jnp.log(-jnp.expm1(-dt0)),
        'a_log': jnp.log(jax.random.uniform(ks[12], (DEPTH, SSD_HEADS), f32, 1.0, 16.0)),
        'd_skip': 1.0 + nrm(ks[13], (DEPTH, SSD_HEADS), 0.1),
        'ssd_norm_w': 1.0 + nrm(ks[14], (DEPTH, SSD_D), 0.02),
        'lb_logits': nrm(ks[15], (DEPTH + 1, HG_HEADS * HG_DK), 0.1),
        'hg_norm_w': 1.0 + nrm(ks[16], (DEPTH, HG_D), 0.02),
        'w_out': nrm(ks[17], (DEPTH, D_MIX, D_MODEL), D_MIX ** -0.5),
        'norm_ffn_w': 1.0 + nrm(ks[18], (DEPTH, D_MODEL), 0.02),
        'w_router_group': nrm(ks[19], (DEPTH, D_MODEL, N_EGROUPS), D_MODEL ** -0.5),
        'b_router_group': nrm(ks[20], (DEPTH, N_EGROUPS), 0.01),
        'w_router_expert': nrm(ks[21], (DEPTH, D_MODEL, N_EXPERTS), D_MODEL ** -0.5),
        'b_router_expert': nrm(ks[22], (DEPTH, N_EGROUPS, EXPERTS_PER_GROUP), 0.01),
        'w_exp_gate': nrm(ks[23], (DEPTH, N_EXPERTS, D_MODEL, EXPERT_FF), D_MODEL ** -0.5),
        'w_exp_up': nrm(ks[24], (DEPTH, N_EXPERTS, D_MODEL, EXPERT_FF), D_MODEL ** -0.5),
        'w_exp_down': nrm(ks[25], (DEPTH, N_EXPERTS, EXPERT_FF, D_MODEL), EXPERT_FF ** -0.5),
        'norm_ple_w': 1.0 + nrm(ks[26], (DEPTH, D_MODEL), 0.02),
        'w_ple_gate': nrm(ks[27], (DEPTH, D_MODEL, D_MODEL), D_MODEL ** -0.5),
        'w_ple_proj': nrm(ks[28], (DEPTH, PLE_DIM, D_MODEL), PLE_DIM ** -0.5),
        'final_norm_w': 1.0 + nrm(ks[29], (D_MODEL,), 0.02),
    }

def reference(x_prompt, x_sample, state_ssm, state_conv, state_hgrn, p_prompt, p_sample,
              norm_mix_w, w_in, conv_w, conv_b, dt_bias, a_log, d_skip, ssd_norm_w, lb_logits,
              hg_norm_w, w_out, norm_ffn_w, w_router_group, b_router_group, w_router_expert,
              b_router_expert, w_exp_gate, w_exp_up, w_exp_down, norm_ple_w, w_ple_gate,
              w_ple_proj, final_norm_w):
    W = {
        'norm_mix_w': norm_mix_w, 'w_in': w_in, 'conv_w': conv_w, 'conv_b': conv_b,
        'dt_bias': dt_bias, 'a_log': a_log, 'd_skip': d_skip, 'ssd_norm_w': ssd_norm_w,
        'lb_logits': lb_logits, 'hg_norm_w': hg_norm_w, 'w_out': w_out,
        'norm_ffn_w': norm_ffn_w, 'w_router_group': w_router_group,
        'b_router_group': b_router_group, 'w_router_expert': w_router_expert,
        'b_router_expert': b_router_expert, 'w_exp_gate': w_exp_gate, 'w_exp_up': w_exp_up,
        'w_exp_down': w_exp_down, 'norm_ple_w': norm_ple_w, 'w_ple_gate': w_ple_gate,
        'w_ple_proj': w_ple_proj, 'final_norm_w': final_norm_w,
    }
    bp = x_prompt.shape[0]
    dtp = x_prompt.dtype
    ssm0 = jnp.zeros((DEPTH, bp, SSD_HEADS, SSD_HEADDIM, D_STATE), dtp)
    conv0 = jnp.zeros((DEPTH, bp, CONV_W - 1, CONV_DIM), dtp)
    hg0 = jnp.zeros((DEPTH, bp, HG_HEADS, HG_DK, HG_DV), dtp)
    y_prompt, ssm_p, conv_p, hg_p = trunk(x_prompt, p_prompt, ssm0, conv0, hg0, W)
    y_sample, ssm_s, conv_s, hg_s = trunk(x_sample, p_sample, state_ssm, state_conv,
                                          state_hgrn, W)
    return (y_prompt, y_sample, ssm_p, conv_p, hg_p, ssm_s, conv_s, hg_s)


_drawn_inputs = setup_inputs


def setup_inputs(seed=0):
    import zlib

    import numpy as np

    out = dict(_drawn_inputs(seed))
    spreads = {}
    factors = {'ssd_norm_w': 15.721,
     'hg_norm_w': 27.874,
     'b_router_group': 51.128,
     'b_router_expert': 27.794,
     'norm_ple_w': 200.0,
     'final_norm_w': 25.169,
     'norm_ffn_w': 8.0,
     'p_prompt': 3.196,
     'p_sample': 3.144,
     'w_ple_gate': 4.526,
     'w_ple_proj': 3.156}
    for name, (base, spread) in spreads.items():
        noise = np.random.default_rng([zlib.crc32(name.encode()), seed]).standard_normal(out[name].shape)
        drawn = base * np.exp(spread * noise) if base else spread * noise
        out[name] = __import__('jax').numpy.asarray(drawn.astype(out[name].dtype))
    for name, factor in factors.items():
        out[name] = (out[name] * factor).astype(out[name].dtype)
    return out
```

```python
from contextlib import ExitStack

import concourse.bass as bass
import numpy as np
from concourse import mybir

ALU = mybir.AluOpType
ACT = mybir.ActivationFunctionType
AX = mybir.AxisListType
F32 = mybir.dt.float32

P = 128
D = 1024
NP_, NS = 256, 8
T = NP_ + NS
KT = D // P
H, HD, N = 16, 64, 128
G = 2
SD = H * HD
CONV = SD + 2 * G * N
CT = CONV // P
HH, DK, DV = 8, 128, 128
E, EG, EPG, FF = 16, 4, 4, 512
PLE = 256
EPS = 1e-6
ARENA = 43500
TOK = [(0, 128), (128, 128), (256, 8)]
BIG = 1e30

C_Z, C_X, C_DT, C_Q = 0, SD, SD + CONV, SD + CONV + H
P_X, P_Q, P_F, P_V, P_G, P_Z = 0, 12, 20, 28, 36, 44
NPROJ = 52
LEVELS = 7
K_ID, K_CAUSAL, K_ONES, K_AFTER, K_LM, K_W4 = 0, 128, 256, 512, 640, 640 + 1024
K_N = K_W4 + 4
R_CW, R_CB, R_SN, R_HN, R_MIX, R_FFN, R_PLE, R_FIN, R_LB = 0, 48, 60, 68, 76, 84, 92, 100, 108
R_N = 124


def constants():
    i = np.arange(P)
    row, col = i[:, None], i[None, :]
    c = np.zeros((P, K_N), np.float32)
    c[:, K_ID:K_ID + P] = row == col
    c[:, K_CAUSAL:K_CAUSAL + P] = row <= col
    c[:, K_ONES:K_ONES + P] = 1.0
    c[:, K_ONES + P:K_ONES + 2 * P] = row <= col
    c[:, K_AFTER:K_AFTER + P] = row > col
    for a in range(LEVELS):
        x = row ^ col
        c[:, K_LM + a * P:K_LM + (a + 1) * P] = (x >= 2 ** a) & (x < 2 ** (a + 1)) & (row < col)
    c[:, K_LM + LEVELS * P:K_LM + (LEVELS + 1) * P] = row == col
    c[:, K_W4:K_W4 + 4] = [4, 3, 2, 1]
    return c


class JobList:

    def __init__(self):
        self.at = {}

    def add(self, *name):
        self.at[name] = len(self.at)

    def __getitem__(self, name):
        return self.at[name if isinstance(name, tuple) else (name,)]


def n0(name):
    return slice(name[1] % 4, name[1] % 4 + 1)


def make_jobs():
    a, v = JobList(), JobList()
    for ft in range(KT):
        a.add("xT", ft)
    v.add("prm")
    v.add("prmD")
    v.add("cst")
    v.add("norm", 0)
    for n in range(NPROJ):
        a.add("proj", n)
    v.add("dt")
    for tt in range(2):
        for half in range(2):
            v.add("xs", tt, half)
    v.add("bcs")
    for g in range(G):
        v.add("cb", g)
    v.add("dts")
    for f in range(KT):
        v.add("y", f)
    a.add("btok")
    a.add("w")
    for i in range(3):
        a.add("tail", i)
    for h in range(H):
        a.add("diff", h)
    for i in range(2):
        a.add("st", i)
    for tt in range(2):
        for half in range(2):
            a.add("vtok", tt, half)
    for half in range(2):
        a.add("vs", half)
    for h in range(HH):
        for tt in range(2):
            for b in range(2):
                v.add("lv", h, tt, b)
        v.add("off", h)
        a.add("o", h)
        a.add("klt", h)
        a.add("sth", h)
    v.add("os")
    for g in range(G):
        v.add("yn", g)
    for h in range(HH):
        v.add("on", h)
    for c in range(KT):
        v.add("mix", c)
    v.add("norm", 1)
    v.add("rt")
    while len(v.at) % 4:
        v.add("skip", len(v.at))
    while len(a.at) % 4:
        a.add("skip", len(a.at))
    for e in range(E):
        for b in range(3):
            a.add("gate", e, b)
            a.add("actT", e, b)
            v.add("up", e, b)
            v.add("down", e, b, 0)
            v.add("down", e, b, 1)
    for ft in range(KT):
        v.add("yt", ft)
    v.add("norm", 2)
    for i in range(2):
        a.add("pT", i)
    for c in range(KT):
        a.add("pg", c)
        v.add("pp", c)
    v.add("norm", 3)
    for tt in range(3):
        for half in range(2):
            a.add("out", tt, half)
    return a, v


def build(nc, ins, outs, consts):
    ja, jv = make_jobs()
    ds = bass.ds

    def dram(name, shape):
        return nc.dram_tensor(name, shape, F32, kind="Internal").ap()

    bc_rows = dram("bc_rows", (NS, 2 * G * N))
    v_rows = dram("v_rows", (NS, HH * DV))

    w_in = ins["w_in"][0].rearrange("(k p) c -> p k c", p=P)
    w_out = ins["w_out"][0].rearrange("(k p) c -> p k c", p=P)
    w_pg = ins["w_ple_gate"][0].rearrange("(k p) c -> p k c", p=P)
    w_pp = ins["w_ple_proj"][0].rearrange("(k p) c -> p k c", p=P)

    ctx = ExitStack()
    with ctx:
        def sb(name, shape):
            return ctx.enter_context(nc.sbuf_tensor(name, shape, F32))

        def sem(name):
            return ctx.enter_context(nc.semaphore(name))

        K = sb("K", [P, K_N])
        ident = K[:, K_ID:K_ID + P]
        ones = K[:, K_ONES:K_ONES + P]
        xT = sb("xT", [P, KT, T])
        hT = sb("hT", [P, KT, T])
        sq = sb("sq", [P, KT, T])
        prm = sb("prm", [P, R_N + 8])
        rstd = sb("rstd", [P, 2, T])
        arena = sb("arena", [P, ARENA])
        used = [0]

        def carve(*shape, at=None):
            if at is not None:
                used[0] = at
            n = int(np.prod(shape))
            v = arena[:, used[0]:used[0] + n]
            used[0] += n
            assert used[0] <= ARENA, used[0]
            if len(shape) == 1:
                return v
            names = "abcd"[:len(shape)]
            return v.rearrange(f"p ({' '.join(names)}) -> p {' '.join(names)}",
                               **{c: s for c, s in zip(names, shape)})

        PR = carve(NPROJ, T)
        W = carve(2, 4096)
        CV = carve(CT, T)
        vtok = carve(2, D)
        smalls = carve(900)
        temp = used[0]
        xdt = carve(2, D)
        xw = carve(2, D)
        btok = carve(2, G * N)
        CBm = carve(G, 384)
        AM = carve(2, H, P)
        EM = carve(4, 384)
        stage = carve(KT, P)
        S1 = carve(2, KT, N)
        BCb = carve(2, 2 * G * N)
        U1 = carve(2, N)
        xtok = carve(3, D, at=temp)
        prow = carve(P)
        drow = carve(P)
        crow = carve(CONV)
        convt = carve(CT, NS)
        convu = carve(CT, NS, 3)
        spare = hT[:, :, :].rearrange("p a b -> p (a b)")
        tail, bcs = spare[:, 0:CONV], spare[0:NS, CONV:CONV + 2 * G * N]
        vss = CV[0:NS, KT:CT].rearrange("p a b -> p (a b)")[:, 0:HH * DV]
        QK = carve(2, 8, NP_, at=temp)
        R = carve(2, NP_)
        L = carve(2, NP_)
        KL = carve(2, NP_)
        klt = carve(2, 2, P)
        LVt = carve(2, 8, P)
        AT = carve(2, 384)
        stage_h = carve(HH, DV)
        S2 = carve(2, HH, DV)
        vb = carve(2, HH * DV)
        U2 = carve(2, DV)
        junk = rstd[:, 0, 0:N]
        sq16 = carve(KT, T, at=temp)
        ms8 = carve(KT, T)
        KK = sq
        EW = carve(2, 3, 4096, at=0)
        acc = carve(3, D)
        sil = carve(2, FF)
        act = carve(2, FF)
        actT = carve(2, 4, P)
        WP = carve(2, 4096, at=0)
        ptok = carve(3, PLE)
        pT = carve(2, T)
        wpp = carve(2, D)
        gs = carve(2, T)
        ostage = carve(3, D)

        sm = [0]

        def small(*shape):
            n = int(np.prod(shape))
            v = smalls[:, sm[0]:sm[0] + n]
            sm[0] += n
            assert sm[0] <= 900
            if len(shape) == 1:
                return v
            names = "abcd"[:len(shape)]
            return v.rearrange(f"p ({' '.join(names)}) -> p {' '.join(names)}",
                               **{c: s for c, s in zip(names, shape)})

        wdt = small(KT, H)
        dtb = small(H)
        alog = small(H)
        aneg = small(H)
        dtr = small(3, H)
        dt1 = small(3, H)
        dt2 = small(3, H)
        dt3 = small(3, H)
        dt4 = small(3, H)
        dtv = small(3, H)
        av = small(3, H)
        wdec = small(2, H)
        ea = small(H)
        DX = small(NS, KT)
        EX = small(NS, KT)
        xds = small(NS, KT)
        yss = small(NS, KT)
        lbt = small(2, HH)
        lb = small(HH)
        oml = small(HH)
        lbe = small(3, HH)
        dpair = small(2)
        wr = sb("wr", [P, KT, 20])
        rb = sb("rb", [P, 20])
        rt = sb("rt", [P, 3, 20])
        rs = sb("rs", [P, 24, 3, 4])
        gates = sb("gates", [P, 3, E])
        r1 = sb("r1", [P, 8, 3])
        dtx = sq[0:NS, 0:4, :].rearrange("p a b -> p (a b)")[:, 0:D]
        eax = sq[0:NS, 4:8, :].rearrange("p a b -> p (a b)")[:, 0:D]

        bank = [ctx.enter_context(nc.psum_tensor(f"bank{i}", [P, 512], F32)) for i in range(8)]

        a_full, a_took = sem("a_full"), sem("a_took")
        v_full, v_took = sem("v_full"), sem("v_took")
        ld_k = sem("ld_k")
        ld_x = sem("ld_x")
        ld_p = sem("ld_p")
        ld_s = sem("ld_s")
        ld_r = sem("ld_r")
        w_slot = [sem("w_slot0"), sem("w_slot1")]
        sq_done, sd_done, norm_done = sem("sq_done"), sem("sd_done"), sem("norm_done")
        dve = sem("dve")
        ea_ready = sem("ea_ready")
        conv_done = sem("conv_done")
        silu_done = sem("silu_done")
        sp = sem("softplus")
        dt_ready = sem("dt_ready")
        am_ready = sem("am_ready")
        xw_ready = sem("xw_ready")
        dtx_ready = sem("dtx_ready")
        m_ready = sem("m_ready")
        bcs_out, bcb_in = sem("bcs_out"), [sem("bcb_in0"), sem("bcb_in1")]
        s1_in = [sem("s1_in0"), sem("s1_in1")]
        s1_new, s1_out = sem("s1_new"), [sem("s1_out0"), sem("s1_out1")]
        xds_ready = sem("xds_ready")
        u1_ready, u1_used = sem("u1_ready"), sem("u1_used")
        store = sem("store")
        hg_sig, hg_fk = sem("hg_sig"), sem("hg_fk")
        drow_ready = sem("drow_ready")
        lb_exp, lb_in = sem("lb_exp"), sem("lb_in")
        qk_ready, kl_ready = sem("qk_ready"), sem("kl_ready")
        at_ready = sem("at_ready")
        vs_out, vb_in = sem("vs_out"), [sem("vb_in0"), sem("vb_in1")]
        s2_in = [sem("s2_in0"), sem("s2_in1")]
        s2_new, s2_out = sem("s2_new"), [sem("s2_out0"), sem("s2_out1")]
        s2_pe = sem("s2_pe")
        u2_ready = sem("u2_ready")
        y_raw, gate_silu, sq_m, sd_m, mixed = (sem("y_raw"), sem("gate_silu"), sem("sq_m"), sem("sd_m"),
                                               sem("mixed"))
        r_in, r_exp = sem("r_in"), sem("r_exp")
        e_slot = [sem("e_slot0"), sem("e_slot1")]
        acc_clear = sem("acc_clear")
        ld_pp = sem("ld_pp")
        wp_slot = [sem("wp_slot0"), sem("wp_slot1")]
        o_store = sem("o_store")
        block = ctx.enter_context(nc.Block())

        PROJ0 = ja["proj", 0]

        @block.sync
        def _(eng):
            eng.dma_start(K[:, :], consts).then_inc(ld_k, 16)
            for i, (t0, n) in enumerate(TOK):
                src = ins["x_prompt"][0, t0:t0 + n] if i < 2 else ins["x_sample"][:, 0]
                eng.dma_start(xtok[0:n, i], src).then_inc(ld_x, 16)

            def w_group(slot, group, col, after):
                if after is not None:
                    eng.wait_ge(a_full, after)
                eng.dma_start(W[:, slot].rearrange("p (k c) -> p k c", k=KT),
                              w_in[:, :, col]).then_inc(w_slot[slot], 16)

            for g in range(3):
                w_group(g % 2, g, slice(C_X + 512 * g, C_X + 512 * g + 512),
                        PROJ0 + 4 * (g - 1) if g >= 2 else None)
            with eng.Fori(0, 4) as it:
                for j in range(2):
                    w_group((3 + j) % 2, None, ds(C_Q + 512 * j + it * 1024, 512),
                            it * 8 + (PROJ0 + 4 * (2 + j)))
            for g in range(2):
                w_group((11 + g) % 2, None, slice(C_Z + 512 * g, C_Z + 512 * g + 512),
                        PROJ0 + 4 * (10 + g))
            for g in range(4):
                if g < 2:
                    eng.wait_ge(a_full, PROJ0 + 4 * (12 + g))
                else:
                    eng.wait_ge(v_full, jv["mix", 2 * (g - 2) + 1] + 1)
                eng.dma_start(W[:, (13 + g) % 2].rearrange("p (k c) -> p k c", k=16),
                              w_out[:, :, 256 * g:256 * g + 256]).then_inc(w_slot[(13 + g) % 2], 16)
            eng.wait_ge(v_took, jv["mix", KT - 1] + 1)
            with eng.Fori(0, 4) as it:
                for j in range(4):
                    s = j % 2
                    ex = it * 4 + j
                    eng.wait_ge(v_full, it * 36 + (jv["up", 0, 0] + 9 * (j - 1) if j else jv["up", 0, 0] - 9))
                    for m, name in enumerate(("w_exp_gate", "w_exp_up")):
                        eng.dma_start(EW[:, s, m].rearrange("p (k c) -> p k c", k=KT),
                                      ins[name][0, ds(ex, 1)].rearrange("e (k p) c -> p (e k) c", p=P)
                                      ).then_inc(e_slot[s], 16)
                    eng.dma_start(EW[:, s, 2].rearrange("p (k c) -> p k c", k=4),
                                  ins["w_exp_down"][0, ds(ex, 1)].rearrange("e (k p) c -> p (e k) c", p=P)
                                  ).then_inc(e_slot[s], 16)
            eng.wait_ge(v_took, jv["down", E - 1, 2, 1] + 1)
            eng.dma_start(ptok[:, 0:2], ins["p_prompt"][0, 0].rearrange("(t p) c -> p t c", p=P)).then_inc(ld_pp, 16)
            eng.dma_start(ptok[0:NS, 2], ins["p_sample"][0, :, 0]).then_inc(ld_pp, 16)
            eng.dma_start(wpp[:, :], w_pp).then_inc(ld_pp, 16)
            for g in range(2):
                eng.dma_start(WP[:, g].rearrange("p (k c) -> p k c", k=KT),
                              w_pg[:, :, 512 * g:512 * g + 512]).then_inc(wp_slot[g], 16)
            for tt, (t0, n) in enumerate(TOK):
                eng.wait_ge(a_took, ja["out", tt, 1] + 1)
                dst = outs[0][0, t0:t0 + n] if tt < 2 else outs[1][:, 0]
                eng.dma_start(dst, ostage[0:n, tt]).then_inc(o_store, 16)
            eng.wait_ge(o_store, 48)

        @block.gpsimd
        def _(eng):
            for r, name, rows in ((R_CW, "conv_w", 48), (R_CB, "conv_b", 12), (R_SN, "ssd_norm_w", 8),
                                  (R_HN, "hg_norm_w", 8), (R_MIX, "norm_mix_w", 8), (R_FFN, "norm_ffn_w", 8),
                                  (R_PLE, "norm_ple_w", 8)):
                src = ins[name][0]
                src = (src.rearrange("k (c p) -> (k c) p", p=P) if name == "conv_w"
                       else src.rearrange("(c p) -> c p", p=P))
                eng.dma_start(prow[r:r + rows], src).then_inc(ld_p, 16)
            eng.dma_start(prow[R_FIN:R_FIN + 8], ins["final_norm_w"].rearrange("(c p) -> c p", p=P)).then_inc(ld_p, 16)
            eng.dma_start(prow[R_LB:R_LB + 16], ins["lb_logits"].rearrange("r (c p) -> (r c) p", p=P)).then_inc(ld_p, 16)
            eng.dma_start(dpair[0:KT], ins["d_skip"][0].rearrange("(f h) -> f h", h=2)).then_inc(ld_p, 16)
            eng.dma_start(crow[0:24], ins["state_conv"][0].rearrange("b k c -> (b k) c")).then_inc(ld_p, 16)
            eng.dma_start(wdt, w_in[:, :, C_DT:C_DT + H]).then_inc(ld_s, 16)
            eng.dma_start(dtb, ins["dt_bias"][0:1].to_broadcast([P, H])).then_inc(ld_s, 16)
            eng.dma_start(alog, ins["a_log"][0:1].to_broadcast([P, H])).then_inc(ld_s, 16)
            eng.dma_start(wr[:, :, 0:4], ins["w_router_group"][0].rearrange("(k p) c -> p k c", p=P)).then_inc(ld_r, 16)
            eng.dma_start(wr[:, :, 4:20], ins["w_router_expert"][0].rearrange("(k p) c -> p k c", p=P)).then_inc(ld_r, 16)
            eng.dma_start(rb[:, 0:4], ins["b_router_group"][0:1].to_broadcast([P, 4])).then_inc(ld_r, 16)
            eng.dma_start(rb[:, 4:20], ins["b_router_expert"][0:1].rearrange("o g e -> o (g e)").to_broadcast([P, E])
                          ).then_inc(ld_r, 16)
            eng.dma_start(outs[6][0, :, 0:2], ins["state_conv"][0, :, 1:3]).then_inc(store, 16)
            n_store = 1
            eng.wait_ge(v_took, jv["bcs"] + 1)
            eng.dma_start(bc_rows, bcs[:, :]).then_inc(bcs_out, 16)
            eng.wait_ge(bcs_out, 16)
            for b in range(NS):
                s = b % 2
                if b >= 2:
                    eng.wait_ge(s1_new, KT * (b - 1))
                    eng.wait_ge(s1_out[s], 16 * (b // 2))
                else:
                    eng.wait_ge(dt_ready, 1)
                eng.dma_start(BCb[:, s], bc_rows[b:b + 1].to_broadcast([P, 2 * G * N])).then_inc(bcb_in[s], 16)
                eng.dma_start(S1[:, s], ins["state_ssm"][0, b].rearrange("h p n -> (h p) n")
                              .rearrange("(f q) n -> q f n", q=P)).then_inc(s1_in[s], 16)
                if b >= 1:
                    q = b - 1
                    eng.wait_ge(s1_new, KT * (q + 1))
                    eng.dma_start(outs[5][0, q].rearrange("h p n -> (h p) n").rearrange("(f q) n -> q f n", q=P),
                                  S1[:, q % 2]).then_inc(s1_out[q % 2], 16)
            q = NS - 1
            eng.wait_ge(s1_new, KT * (q + 1))
            eng.dma_start(outs[5][0, q].rearrange("h p n -> (h p) n").rearrange("(f q) n -> q f n", q=P),
                          S1[:, q % 2]).then_inc(s1_out[q % 2], 16)
            for i in range(3):
                eng.wait_ge(a_took, ja["tail", i] + 1)
            eng.dma_start(outs[3][0, 0], tail[0:3]).then_inc(store, 16)
            eng.dma_start(outs[6][0, :, 2], tail[3:11]).then_inc(store, 16)
            eng.wait_ge(a_took, ja["st", 1] + 1)
            eng.dma_start(outs[2][0, 0].rearrange("h p n -> (h p) n").rearrange("(f q) n -> q f n", q=P),
                          stage).then_inc(store, 16)
            n_store += 3
            eng.wait_ge(a_took, ja["vs", 1] + 1)
            eng.dma_start(v_rows, vss[:, :]).then_inc(vs_out, 16)
            eng.wait_ge(vs_out, 16)
            eng.wait_ge(store, 16 * n_store)
            eng.wait_ge(s1_out[0], 16 * 4)
            eng.wait_ge(s1_out[1], 16 * 4)
            eng.wait_ge(v_took, jv["y", KT - 1] + 1)
            for b in range(NS):
                s = b % 2
                if b >= 2:
                    eng.wait_ge(s2_new, HH * (b - 1))
                    eng.wait_ge(s2_pe, b - 1)
                    eng.wait_ge(s2_out[s], 16 * (b // 2))
                eng.dma_start(vb[:, s], v_rows[b:b + 1].to_broadcast([P, HH * DV])).then_inc(vb_in[s], 16)
                eng.dma_start(S2[:, s], ins["state_hgrn"][0, b].rearrange("h k v -> k h v")).then_inc(s2_in[s], 16)
                if b >= 1:
                    q = b - 1
                    eng.wait_ge(s2_new, HH * (q + 1))
                    eng.dma_start(outs[7][0, q].rearrange("h k v -> k h v"), S2[:, q % 2]).then_inc(s2_out[q % 2], 16)
            q = NS - 1
            eng.wait_ge(s2_new, HH * (q + 1))
            eng.dma_start(outs[7][0, q].rearrange("h k v -> k h v"), S2[:, q % 2]).then_inc(s2_out[q % 2], 16)
            eng.wait_ge(a_took, ja["sth", HH - 1] + 1)
            eng.dma_start(outs[4][0, 0].rearrange("h k v -> k h v"), stage_h).then_inc(store, 16)
            n_store += 1
            eng.wait_ge(store, 16 * n_store)
            eng.wait_ge(s2_out[0], 16 * 4)
            eng.wait_ge(s2_out[1], 16 * 4)

        @block.tensor
        def _(eng):
            mm = nc.tensor.matmul

            def bank_a(n):
                if not isinstance(n, int) or n >= 4:
                    eng.wait_ge(a_took, n - 3)

            def open_a(*name):
                n = ja[name]
                bank_a(n)
                return bank[n % 4]

            def open_v(*name):
                n = jv[name]
                if n >= 4:
                    eng.wait_ge(v_took, n - 3)
                return bank[4 + n % 4]

            def norm(k):
                ps = open_v("norm", k)
                eng.wait_ge(sq_done, k + 1)
                for ft in range(KT):
                    last = mm(ps[:, 0:T], ones, sq[:, ft], start=(ft == 0), stop=(ft == KT - 1))
                last.then_inc(v_full, 1)

            eng.wait_ge(ld_k, 16)
            eng.wait_ge(ld_x, 48)
            for ft in range(KT):
                ps = open_a("xT", ft)
                for i, (t0, n) in enumerate(TOK):
                    last = nc.tensor.transpose(ps[:, t0:t0 + n], xtok[0:n, i, ft * P:(ft + 1) * P], ident[0:n, 0:n])
                last.then_inc(a_full, 1)
            eng.wait_ge(ld_p, 16 * 11)
            nc.tensor.transpose(open_v("prm")[:, 0:R_N], prow[0:R_N], ident[0:R_N, 0:R_N]).then_inc(v_full, 1)
            eng.wait_ge(drow_ready, 1)
            nc.tensor.transpose(open_v("prmD")[:, 0:KT], drow[0:KT], ident[0:KT, 0:KT]).then_inc(v_full, 1)
            ps = open_v("cst")
            for c in range(CT):
                last = nc.tensor.transpose(ps[:, 24 * c:24 * c + 24], crow[0:24, c * P:(c + 1) * P], ident[0:24, 0:24])
            last.then_inc(v_full, 1)
            norm(0)

            def proj_group(slot, turn, first):
                eng.wait_ge(w_slot[slot], turn)
                for j in range(4):
                    bank_a(first + (PROJ0 + j))
                    w = W[:, slot].rearrange("p (k c) -> p k c", k=KT)
                    ps = bank[(PROJ0 + j) % 4]
                    for k in range(KT):
                        last = mm(ps[:, 0:T], w[:, k, j * P:(j + 1) * P], hT[:, k], start=(k == 0), stop=(k == KT - 1))
                    last.then_inc(a_full, 1)

            eng.wait_ge(norm_done, KT)
            for g in range(3):
                proj_group(g % 2, 16 * (g // 2 + 1), 4 * g)
            eng.wait_ge(ld_s, 48)
            ps = open_v("dt")
            for i, (t0, n) in enumerate(TOK):
                for k in range(KT):
                    last = mm(ps[0:n, H * i:H * i + H], hT[:, k, t0:t0 + n], wdt[:, k], start=(k == 0), stop=(k == KT - 1))
            last.then_inc(v_full, 1)
            with eng.Fori(0, 4) as it:
                for j in range(2):
                    g = 3 + j
                    proj_group(g % 2, it * 16 + 16 * (g // 2 + 1), it * 8 + 4 * g)
            for g in (11, 12):
                proj_group(g % 2, 16 * (g // 2 + 1), 4 * g)

            eng.wait_ge(silu_done, CT)
            for tt in range(2):
                for half in range(2):
                    ps = open_v("xs", tt, half)
                    for j in range(4):
                        last = nc.tensor.transpose(ps[:, j * P:(j + 1) * P],
                                                   CV[:, 4 * half + j, tt * P:(tt + 1) * P], ident)
                    last.then_inc(v_full, 1)
            ps = open_a("btok")
            for tt in range(2):
                for g in range(G):
                    last = nc.tensor.transpose(ps[:, (2 * tt + g) * P:(2 * tt + g + 1) * P],
                                               CV[:, KT + g, tt * P:(tt + 1) * P], ident)
            last.then_inc(a_full, 1)
            ps = open_v("bcs")
            for j in range(4):
                last = nc.tensor.transpose(ps[0:NS, j * P:(j + 1) * P], CV[:, KT + j, NP_:T], ident)
            last.then_inc(v_full, 1)
            for g in range(G):
                ps = open_v("cb", g)
                mm(ps[:, 0:NP_], CV[:, KT + g, 0:P], CV[:, KT + G + g, 0:NP_], start=True, stop=True)
                mm(ps[:, NP_:384], CV[:, KT + g, P:NP_], CV[:, KT + G + g, P:NP_], start=True, stop=True
                   ).then_inc(v_full, 1)
            ps = open_a("w")
            eng.wait_ge(dt_ready, 1)
            after = K[:, K_AFTER:K_AFTER + P]
            mm(ps[:, 0:H], after, av[:, 0], start=True, stop=False)
            mm(ps[:, 0:H], ones, av[:, 1], start=False, stop=True)
            mm(ps[:, H:2 * H], after, av[:, 1], start=True, stop=True).then_inc(a_full, 1)
            for i in range(3):
                ps = open_a("tail", i)
                for j in range(4):
                    last = nc.tensor.transpose(ps[0:11, j * P:(j + 1) * P], PR[:, 4 * i + j, NP_ - 3:T], ident)
                last.then_inc(a_full, 1)
            eng.wait_ge(dtx_ready, 2)
            ps = open_v("dts")
            for k, src in enumerate((dtx, eax)):
                for f in range(KT):
                    c = (k * KT + f) * NS
                    last = nc.tensor.transpose(ps[:, c:c + NS], src[:, f * P:(f + 1) * P], ident[0:NS, 0:NS])
            last.then_inc(v_full, 1)

            def diff(h):
                ps = open_a("diff", h)
                eng.wait_ge(am_ready, 2)
                causal = K[:, K_CAUSAL:K_CAUSAL + P]
                mm(ps[:, 0:NP_], AM[:, 0, h], K[:, K_CAUSAL:K_CAUSAL + NP_], start=True, stop=False, skip_group_check=True)
                mm(ps[:, P:NP_], av[:, 1, h:h + 1].to_broadcast([P, P]), causal, start=False, stop=True,
                   skip_group_check=True)
                mm(ps[:, NP_:384], AM[:, 1, h], causal, start=True, stop=True, skip_group_check=True).then_inc(a_full, 1)

            def y_head(h):
                ps = bank[4 + jv["y", h // 2] % 4] if h % 2 else open_v("y", h // 2)
                eng.wait_ge(m_ready, h + 1)
                r = slice(HD * (h % 2), HD * (h % 2) + HD)
                c = slice(HD * h, HD * h + HD)
                m = EM[:, h % 4]
                mm(ps[r, 0:NP_], xdt[:, 0, c], m[:, 0:NP_], start=True, stop=False, skip_group_check=True)
                last = mm(ps[r, P:NP_], xdt[:, 1, c], m[:, NP_:384], start=False, stop=True, skip_group_check=True)
                if h % 2:
                    last.then_inc(v_full, 1)

            for h in range(H + 2):
                if h < H:
                    diff(h)
                if h >= 2:
                    y_head(h - 2)
            eng.wait_ge(xw_ready, 2)
            for i in range(2):
                ps = open_a("st", i)
                for j in range(4):
                    f = 4 * i + j
                    for tt in range(2):
                        last = mm(ps[:, j * P:(j + 1) * P], xw[:, tt, f * P:(f + 1) * P],
                                  btok[:, tt, (f // 4) * N:(f // 4 + 1) * N], start=(tt == 0), stop=(tt == 1))
                last.then_inc(a_full, 1)

            for tt in range(2):
                for half in range(2):
                    ps = open_a("vtok", tt, half)
                    for j in range(4):
                        last = nc.tensor.transpose(ps[:, j * P:(j + 1) * P],
                                                   PR[:, P_V + 4 * half + j, tt * P:(tt + 1) * P], ident)
                    last.then_inc(a_full, 1)
            for half in range(2):
                ps = open_a("vs", half)
                for j in range(4):
                    last = nc.tensor.transpose(ps[0:NS, j * P:(j + 1) * P], PR[:, P_V + 4 * half + j, NP_:T], ident)
                last.then_inc(a_full, 1)
            eng.wait_ge(hg_fk, 2 * HH)
            for h in range(HH):
                hl = h % 2
                eng.wait_ge(qk_ready, 16 * (h // 2 + 1))
                for tt in range(2):
                    tk = slice(tt * P, (tt + 1) * P)
                    for b in range(2):
                        ps = open_v("lv", h, tt, b)
                        for j in range(4):
                            a = 4 * b + j
                            if a < LEVELS:
                                x = y = QK[:, hl, a, tk]
                            else:
                                x, y = KK[:, h, tk], PR[:, P_Q + h, tk]
                            last = mm(ps[:, j * P:(j + 1) * P], x, y, start=True, stop=True)
                        last.then_inc(v_full, 1)
                ps = open_v("off", h)
                mm(ps[:, 0:P], QK[:, hl, 7, 0:P], QK[:, hl, 7, P:NP_], start=True, stop=True).then_inc(v_full, 1)
                eng.wait_ge(at_ready, 2 * (h + 1))
                eng.wait_ge(v_took, jv["off", h] + 1)
                ps = open_a("o", h)
                hc = slice(h * P, (h + 1) * P)
                mm(ps[:, 0:NP_], vtok[:, 0, hc], AT[:, hl, 0:NP_], start=True, stop=False, skip_group_check=True)
                mm(ps[:, P:NP_], vtok[:, 1, hc], AT[:, hl, NP_:384], start=False, stop=True, skip_group_check=True
                   ).then_inc(a_full, 1)
                ps = open_a("klt", h)
                eng.wait_ge(kl_ready, h // 2 + 1)
                for tt in range(2):
                    last = nc.tensor.transpose(ps[:, tt * P:(tt + 1) * P], KL[:, hl, tt * P:(tt + 1) * P], ident)
                last.then_inc(a_full, 1)
                ps = open_a("sth", h)
                eng.wait_ge(a_took, ja["klt", h] + 1)
                for tt in range(2):
                    last = mm(ps[:, 0:DV], klt[:, hl, tt], vtok[:, tt, hc], start=(tt == 0), stop=(tt == 1))
                last.then_inc(a_full, 1)
            ps = open_v("os")
            for b in range(NS):
                for h in range(HH):
                    eng.wait_ge(s2_new, HH * b + h + 1)
                    last = mm(ps[:, h * NS + b:h * NS + b + 1], S2[:, b % 2, h], PR[:, P_Q + h, NP_ + b:NP_ + b + 1],
                              start=True, stop=True)
                last.then_inc(s2_pe if b < NS - 1 else v_full, 1)

            for g in range(G):
                ps = open_v("yn", g)
                eng.wait_ge(sq_m, 1)
                for j in range(4):
                    last = mm(ps[:, 0:T], ones, sq16[:, 4 * g + j], start=(j == 0), stop=(j == 3))
                last.then_inc(v_full, 1)
            for h in range(HH):
                ps = open_v("on", h)
                eng.wait_ge(sq_m, 2)
                mm(ps[:, 0:T], ones, sq16[:, h], start=True, stop=True).then_inc(v_full, 1)
            eng.wait_ge(mixed, 16)
            for c in range(KT):
                g = c // 2
                s = (13 + g) % 2
                if c % 2 == 0:
                    eng.wait_ge(w_slot[s], 16 * ((13 + g) // 2 + 1))
                w = W[:, s].rearrange("p (k c) -> p k c", k=16)
                ps = open_v("mix", c)
                for k in range(16):
                    x = PR[:, k] if k < 8 else PR[:, P_F + k - 8]
                    last = mm(ps[:, 0:T], w[:, k, (c % 2) * P:(c % 2) * P + P], x, start=(k == 0), stop=(k == 15))
                last.then_inc(v_full, 1)
            norm(1)

            eng.wait_ge(norm_done, 2 * KT)
            eng.wait_ge(ld_r, 64)
            ps = open_v("rt")
            for i, (t0, n) in enumerate(TOK):
                for k in range(KT):
                    last = mm(ps[0:n, 20 * i:20 * i + 20], hT[:, k, t0:t0 + n], wr[:, k], start=(k == 0), stop=(k == KT - 1))
            last.then_inc(v_full, 1)
            for name in jv.at:
                if name[0] == "skip":
                    mm(open_v(*name)[:, 0:1], ident, ones[:, 0:1], start=True, stop=True).then_inc(v_full, 1)
            for name in ja.at:
                if name[0] == "skip":
                    mm(open_a(*name)[:, 0:1], ident, ones[:, 0:1], start=True, stop=True).then_inc(a_full, 1)

            A0, V0 = ja["gate", 0, 0], jv["up", 0, 0]
            assert A0 % 4 == 0 and V0 % 4 == 0
            with eng.Fori(0, 4) as it:
                for j in range(4):
                    s = j % 2
                    wg = EW[:, s, 0].rearrange("p (k c) -> p k c", k=KT)
                    wu = EW[:, s, 1].rearrange("p (k c) -> p k c", k=KT)
                    wd = EW[:, s, 2].rearrange("p (k c) -> p k c", k=4)
                    eng.wait_ge(e_slot[s], it * 96 + 48 * (j // 2 + 1))
                    for b, (t0, n) in enumerate(TOK):
                        u = 3 * j + b
                        na, nv = 2 * u, 3 * u
                        eng.wait_ge(a_took, it * 24 + (A0 + na - 3))
                        ps = bank[na % 4]
                        for k in range(KT):
                            last = mm(ps[0:n, :], hT[:, k, t0:t0 + n], wg[:, k], start=(k == 0), stop=(k == KT - 1))
                        last.then_inc(a_full, 1)
                        eng.wait_ge(v_took, it * 36 + (V0 + nv - 3))
                        ps = bank[4 + nv % 4]
                        for k in range(KT):
                            last = mm(ps[0:n, :], hT[:, k, t0:t0 + n], wu[:, k], start=(k == 0), stop=(k == KT - 1))
                        last.then_inc(v_full, 1)
                        eng.wait_ge(a_took, it * 24 + (A0 + na - 2))
                        eng.wait_ge(v_took, it * 36 + (V0 + nv + 1))
                        ps = bank[(na + 1) % 4]
                        for k in range(4):
                            last = nc.tensor.transpose(ps[:, k * P:(k + 1) * P], act[:, u % 2, k * P:(k + 1) * P], ident)
                        last.then_inc(a_full, 1)
                        eng.wait_ge(a_took, it * 24 + (A0 + na + 2))
                        for half in range(2):
                            eng.wait_ge(v_took, it * 36 + (V0 + nv + 1 + half - 3))
                            ps = bank[4 + (nv + 1 + half) % 4]
                            for k in range(4):
                                last = mm(ps[0:n, :], actT[:, u % 2, k, 0:n], wd[:, k, 512 * half:512 * half + 512],
                                          start=(k == 0), stop=(k == 3))
                            last.then_inc(v_full, 1)
            for ft in range(KT):
                ps = open_v("yt", ft)
                eng.wait_ge(v_took, jv["down", E - 1, 2, 1] + 1)
                for i, (t0, n) in enumerate(TOK):
                    last = nc.tensor.transpose(ps[:, t0:t0 + n], acc[0:n, i, ft * P:(ft + 1) * P], ident[0:n, 0:n])
                last.then_inc(v_full, 1)
            norm(2)

            eng.wait_ge(ld_pp, 48)
            for c in range(2):
                ps = open_a("pT", c)
                for i, (t0, n) in enumerate(TOK):
                    last = nc.tensor.transpose(ps[:, t0:t0 + n], ptok[0:n, i, c * P:(c + 1) * P], ident[0:n, 0:n])
                last.then_inc(a_full, 1)
            eng.wait_ge(norm_done, 3 * KT)
            for c in range(KT):
                if c % 4 == 0:
                    eng.wait_ge(wp_slot[c // 4], 16)
                w = WP[:, c // 4].rearrange("p (k c) -> p k c", k=KT)
                ps = open_a("pg", c)
                for k in range(KT):
                    last = mm(ps[:, 0:T], w[:, k, (c % 4) * P:(c % 4 + 1) * P], hT[:, k], start=(k == 0), stop=(k == KT - 1))
                last.then_inc(a_full, 1)
                ps = open_v("pp", c)
                eng.wait_ge(a_took, ja["pT", 1] + 1)
                for k in range(2):
                    last = mm(ps[:, 0:T], wpp[:, k, c * P:(c + 1) * P], pT[:, k], start=(k == 0), stop=(k == 1))
                last.then_inc(v_full, 1)
            norm(3)
            eng.wait_ge(norm_done, 4 * KT)
            for i, (t0, n) in enumerate(TOK):
                for half in range(2):
                    ps = open_a("out", i, half)
                    for j in range(4):
                        last = nc.tensor.transpose(ps[0:n, j * P:(j + 1) * P], hT[:, 4 * half + j, t0:t0 + n], ident)
                    last.then_inc(a_full, 1)

        @block.scalar
        def _(eng):
            activation = nc.scalar.activation
            def full(*name):
                n = ja[name]
                eng.wait_ge(a_full, n + 1)
                return bank[n % 4]

            def norm(k):
                eng.wait_ge(norm_in[k][0], norm_in[k][1])
                activation(sq[:, :, :], xT[:, :, :], ACT.Square).then_inc(sq_done, 1)
                eng.wait_ge(v_took, jv["norm", k] + 1)
                activation(rstd[:, 1], rstd[:, 0], ACT.Sqrt).then_inc(sd_done, 1)

            norm_in = {0: (a_took, ja["xT", KT - 1] + 1), 1: (v_took, jv["mix", KT - 1] + 1),
                       2: (v_took, jv["yt", KT - 1] + 1), 3: (v_took, jv["pp", KT - 1] + 1)}
            for ft in range(KT):
                activation(xT[:, ft], full("xT", ft)[:, 0:T], ACT.Copy).then_inc(a_took, 1)
            norm(0)
            eng.wait_ge(lb_in, 2)
            activation(lbt, lbt, ACT.Exp).then_inc(lb_exp, 1)
            eng.wait_ge(ld_s, 48)
            activation(aneg, alog, ACT.Exp).then_inc(lb_exp, 1)
            for n in range(12):
                activation(PR[:, n], full("proj", n)[:, 0:T], ACT.Copy).then_inc(a_took, 1)
            eng.wait_ge(sp, 1)
            activation(dt2, dt1, ACT.Exp, scale=-1.0).then_inc(sp, 1)
            eng.wait_ge(sp, 3)
            activation(dt4, dt3, ACT.Ln).then_inc(sp, 1)
            eng.wait_ge(dt_ready, 1)
            activation(ea[0:NS], av[0:NS, 2], ACT.Exp).then_inc(ea_ready, 1)
            with eng.Fori(0, 4) as it:
                for j in range(8):
                    n = it * 8 + (12 + j)
                    eng.wait_ge(a_full, n + (PROJ0 + 1))
                    activation(PR[:, ds(n, 1)].rearrange("p a t -> p (a t)"), bank[(PROJ0 + 12 + j) % 4][:, 0:T],
                               ACT.Copy).then_inc(a_took, 1)
                for j in range(3):
                    eng.wait_ge(conv_done, it * 3 + (j + 1))
                    c = CV[:, ds(it * 3 + j, 1)].rearrange("p a t -> p (a t)")
                    activation(c, c, ACT.Silu).then_inc(silu_done, 1)
            for n in range(44, NPROJ):
                activation(PR[:, n], full("proj", n)[:, 0:T], ACT.Copy).then_inc(a_took, 1)
            activation(btok[:, :, :].rearrange("p a b -> p (a b)"), full("btok")[:, :], ACT.Copy).then_inc(a_took, 1)
            activation(wdec[:, :, :].rearrange("p a b -> p (a b)"), full("w")[:, 0:2 * H], ACT.Exp).then_inc(a_took, 1)
            for i in range(3):
                activation(tail[0:11, i * 512:(i + 1) * 512], full("tail", i)[0:11, :], ACT.Copy).then_inc(a_took, 1)
            for h in range(H):
                if h >= 4:
                    eng.wait_ge(v_full, jv["y", (h - 4) // 2] + 1)
                activation(EM[:, h % 4], full("diff", h)[:, 0:384], ACT.Exp).then_inc(a_took, 1)
            for i in range(2):
                activation(stage[:, 4 * i:4 * i + 4].rearrange("p a b -> p (a b)"), full("st", i)[:, :],
                           ACT.Copy).then_inc(a_took, 1)
            for tt in range(2):
                for half in range(2):
                    activation(vtok[:, tt, 512 * half:512 * half + 512], full("vtok", tt, half)[:, :],
                               ACT.Copy).then_inc(a_took, 1)
            for half in range(2):
                activation(vss[:, 512 * half:512 * half + 512], full("vs", half)[0:NS, :], ACT.Copy).then_inc(a_took, 1)
            eng.wait_ge(v_full, jv["dts"] + 1)
            fr = PR[:, P_F:P_F + HH]
            activation(KK[:, :, :], fr, ACT.Sigmoid, scale=-1.0).then_inc(hg_sig, 1)
            activation(fr, fr, ACT.Sigmoid).then_inc(hg_sig, 1)
            eng.wait_ge(xds_ready, 1)
            for b in range(NS):
                eng.wait_ge(bcb_in[b % 2], 16 * (b // 2 + 1))
                for f in range(KT):
                    u = b * KT + f
                    if u >= 2:
                        eng.wait_ge(u1_used, u - 1)
                    activation(U1[:, u % 2], BCb[:, b % 2, (f // 4) * N:(f // 4 + 1) * N], ACT.Copy,
                               scale=xds[:, b, f:f + 1]).then_inc(u1_ready, 1)

            def hg_head(h):
                hl = h % 2
                activation(PR[:, P_F + h, 0:NP_], full("o", h)[:, 0:NP_], ACT.Copy).then_inc(a_took, 1)
                activation(klt[:, hl].rearrange("p a b -> p (a b)"), full("klt", h)[:, 0:NP_], ACT.Copy).then_inc(a_took, 1)
                activation(stage_h[:, h], full("sth", h)[:, 0:DV], ACT.Copy).then_inc(a_took, 1)

            eng.wait_ge(hg_fk, 2 * HH)
            for h in range(HH):
                hg_head(h)
            for b in range(NS):
                eng.wait_ge(vb_in[b % 2], 16 * (b // 2 + 1))
                for h in range(HH):
                    u = b * HH + h
                    if u >= 2:
                        eng.wait_ge(s2_new, u - 1)
                    activation(U2[:, u % 2], vb[:, b % 2, h * DV:(h + 1) * DV], ACT.Copy,
                               scale=KK[:, h, NP_ + b:NP_ + b + 1]).then_inc(u2_ready, 1)
            zg = [PR[:, P_Z:P_Z + 8], PR[:, P_G:P_G + 8]]
            for z in zg:
                activation(z, z, ACT.Silu).then_inc(gate_silu, 1)
            eng.wait_ge(y_raw, 1)
            activation(sq16, PR[:, 0:8], ACT.Square).then_inc(sq_m, 1)
            eng.wait_ge(v_took, jv["yn", 1] + 1)
            activation(ms8[:, 2:4], ms8[:, 0:2], ACT.Sqrt).then_inc(sd_m, 1)
            eng.wait_ge(v_took, jv["os"] + 1)
            activation(sq16, PR[:, P_F:P_F + 8], ACT.Square).then_inc(sq_m, 1)
            eng.wait_ge(v_took, jv["on", HH - 1] + 1)
            activation(ms8[:, :], ms8[:, :], ACT.Sqrt).then_inc(sd_m, 1)
            norm(1)
            eng.wait_ge(r_in, 1)
            activation(rs[:, 1], rs[:, 0], ACT.Exp).then_inc(r_exp, 1)
            eng.wait_ge(r_in, 2)
            activation(rs[:, 9], rs[:, 8], ACT.Exp).then_inc(r_exp, 1)
            for name in ja.at:
                if name[0] == "skip":
                    activation(rstd[:, 1, n0(name)], full(*name)[:, 0:1], ACT.Copy).then_inc(a_took, 1)
            A0, V0 = ja["gate", 0, 0], jv["up", 0, 0]
            with eng.Fori(0, 4) as it:
                for j in range(4):
                    for b, (t0, n) in enumerate(TOK):
                        u = 3 * j + b
                        na = 2 * u
                        eng.wait_ge(a_full, it * 24 + (A0 + na + 1))
                        eng.wait_ge(v_took, it * 36 + (V0 + 3 * u - 5))
                        activation(sil[0:n, u % 2], bank[na % 4][0:n, :], ACT.Silu).then_inc(a_took, 1)
                        eng.wait_ge(a_full, it * 24 + (A0 + na + 2))
                        activation(actT[:, u % 2, :, 0:n], bank[(na + 1) % 4][:, :].rearrange("p (k c) -> p k c", k=4)[:, :, 0:n],
                                   ACT.Copy).then_inc(a_took, 1)
            norm(2)
            for c in range(2):
                activation(pT[:, c], full("pT", c)[:, 0:T], ACT.Copy).then_inc(a_took, 1)
            for c in range(KT):
                if c >= 2:
                    eng.wait_ge(v_took, jv["pp", c - 2] + 1)
                activation(gs[:, c % 2], full("pg", c)[:, 0:T], ACT.Sigmoid).then_inc(a_took, 1)
            norm(3)
            for i, (t0, n) in enumerate(TOK):
                for half in range(2):
                    activation(ostage[0:n, i, 512 * half:512 * half + 512], full("out", i, half)[0:n, :],
                               ACT.Copy).then_inc(a_took, 1)

        @block.vector
        def _(eng):
            own = [0]

            def link(ins_):
                own[0] += 1
                ins_.then_inc(dve, 1)
                eng.wait_ge(dve, own[0])

            def full(*name):
                n = jv[name]
                eng.wait_ge(v_full, n + 1)
                return bank[4 + n % 4]

            def took(*name):
                eng.wait_ge(v_took, jv[name] + 1)

            def tt(out, a, b, op=ALU.mult):
                return nc.vector.tensor_tensor(out, a, b, op)

            def ts(out, a, s1, op0, s2=None, op1=None):
                if op1 is None:
                    return nc.vector.tensor_scalar(out, a, s1, None, op0)
                return nc.vector.tensor_scalar(out, a, s1, s2, op0, op1)

            def stt(out, a, s, b, op0, op1):
                return nc.vector.scalar_tensor_tensor(out, a, s, b, op0, op1)

            def col(r):
                return prm[:, r:r + 1]

            def spread(x, n):
                rows = x.shape[0]
                return x.rearrange("p (h o) -> p h o", o=1).to_broadcast([rows, x.shape[1], n])

            def norm(k, row):
                ps = full("norm", k)
                ts(rstd[:, 0], ps[:, 0:T], 1.0 / D, ALU.mult, EPS, ALU.add).then_inc(v_took, 1)
                eng.wait_ge(sd_done, k + 1)
                link(nc.vector.reciprocal(rstd[:, 0], rstd[:, 1]))
                for ft in range(KT):
                    stt(hT[:, ft], xT[:, ft], col(row + ft), rstd[:, 0], ALU.mult, ALU.mult).then_inc(norm_done, 1)

            eng.wait_ge(ld_p, 16 * 11)
            nc.vector.tensor_copy(drow[0:KT].rearrange("f (h p) -> f h p", h=2), spread(dpair[0:KT], HD)
                                  ).then_inc(drow_ready, 1)
            nc.vector.tensor_copy(prm[:, 0:R_N], full("prm")[:, 0:R_N]).then_inc(v_took, 1)
            nc.vector.tensor_copy(prm[:, R_N:R_N + KT], full("prmD")[:, 0:KT]).then_inc(v_took, 1)
            nc.vector.tensor_copy(convu.rearrange("p c b k -> p (c b k)"), full("cst")[:, 0:288]).then_inc(v_took, 1)
            took("cst")
            l0, l1 = prm[:, R_LB:R_LB + HH], prm[:, R_LB + HH:R_LB + 2 * HH]
            link(tt(lbe[:, 0], l0, l1, ALU.max))
            tt(lbt[:, 0], l0, lbe[:, 0], ALU.subtract).then_inc(lb_in, 1)
            tt(lbt[:, 1], l1, lbe[:, 0], ALU.subtract).then_inc(lb_in, 1)
            norm(0, R_MIX)
            eng.wait_ge(lb_exp, 2)
            link(tt(lbe[:, 1], lbt[:, 0], lbt[:, 1], ALU.add))
            link(nc.vector.reciprocal(lbe[:, 2], lbe[:, 1]))
            tt(lb, lbt[:, 0], lbe[:, 2])
            link(tt(oml, lbt[:, 1], lbe[:, 2]))
            link(nc.vector.memset(dtr, 0.0))
            ps = full("dt")
            link(tt(dtr[:, 0:2], ps[:, 0:2 * H].rearrange("p (t h) -> p t h", h=H),
                    dtb.rearrange("p (o h) -> p o h", o=1).to_broadcast([P, 2, H]), ALU.add))
            tt(dtr[0:NS, 2], ps[0:NS, 2 * H:3 * H], dtb[0:NS], ALU.add).then_inc(v_took, 1)
            took("dt")
            link(ts(dt2, dtr, -1.0, ALU.mult))
            tt(dt1, dt2, dtr, ALU.max).then_inc(sp, 1)
            eng.wait_ge(sp, 2)
            ts(dt3, dt2, 1.0, ALU.add).then_inc(sp, 1)
            eng.wait_ge(sp, 4)
            link(ts(dt1, dt3, 1.0, ALU.is_equal))
            link(ts(dt3, dt3, -1.0, ALU.add))
            link(tt(dt3, dt3, dt1, ALU.add))
            link(tt(dt4, dt4, dt1, ALU.add))
            link(nc.vector.reciprocal(dtv, dt3))
            link(tt(dt4, dt4, dt2))
            link(tt(dt4, dt4, dtv))
            link(stt(dtv, dtr, 0.0, dt4, ALU.max, ALU.add))
            stt(av, dtv, -1.0, aneg.rearrange("p (o h) -> p o h", o=1).to_broadcast([P, 3, H]),
                ALU.mult, ALU.mult).then_inc(dt_ready, 1)
            eng.wait_ge(dt_ready, 1)
            for c in range(CT):
                eng.wait_ge(a_took, ja["proj", c] + 1)
                raw, out = PR[:, c], CV[:, c]
                link(ts(out, raw, col(R_CW + 3 * CT + c), ALU.mult, col(R_CB + c), ALU.add))
                for k in range(3):
                    s = 3 - k
                    link(stt(out[:, s:NP_], raw[:, 0:NP_ - s], col(R_CW + k * CT + c), out[:, s:NP_],
                             ALU.mult, ALU.add))
                old = convu[:, c].rearrange("p b k -> p k b")
                for k in range(3):
                    last = stt(out[:, NP_:T], old[:, k], col(R_CW + k * CT + c), out[:, NP_:T], ALU.mult, ALU.add)
                    if k < 2:
                        link(last)
                last.then_inc(conv_done, 1)

            after = K[:, K_AFTER:K_AFTER + P].rearrange("p (o s) -> p o s", o=1).to_broadcast([P, H, P])
            for i in range(2):
                tt(AM[:, i], after, spread(av[:, i], P)).then_inc(am_ready, 1)
            nc.vector.tensor_copy(dtx.rearrange("p (h q) -> p h q", q=HD), spread(dtv[0:NS, 2], HD)).then_inc(dtx_ready, 1)
            eng.wait_ge(ea_ready, 1)
            nc.vector.tensor_copy(eax.rearrange("p (h q) -> p h q", q=HD), spread(ea[0:NS], HD)).then_inc(dtx_ready, 1)
            for i in range(2):
                for half in range(2):
                    tt(xdt[:, i, 512 * half:512 * half + 512].rearrange("p (h q) -> p h q", q=HD),
                       full("xs", i, half)[:, :].rearrange("p (h q) -> p h q", q=HD),
                       spread(dtv[:, i, 8 * half:8 * half + 8], HD)).then_inc(v_took, 1)
            nc.vector.tensor_copy(bcs, full("bcs")[0:NS, :]).then_inc(v_took, 1)
            for g in range(G):
                tt(CBm[:, g], full("cb", g)[:, 0:384], K[:, K_CAUSAL:K_CAUSAL + 384]).then_inc(v_took, 1)
            ps = full("dts")
            link(nc.vector.tensor_copy(DX, ps[:, 0:64].rearrange("p (f b) -> p b f", f=KT)))
            nc.vector.tensor_copy(EX, ps[:, 64:128].rearrange("p (f b) -> p b f", f=KT)).then_inc(v_took, 1)
            took("dts")
            tt(xds, CV[:, 0:KT, NP_:T].rearrange("p f b -> p b f"), DX).then_inc(xds_ready, 1)
            eng.wait_ge(a_took, ja["w"] + 1)
            for i in range(2):
                tt(xw[:, i].rearrange("p (h q) -> p h q", q=HD), xdt[:, i].rearrange("p (h q) -> p h q", q=HD),
                   spread(wdec[:, i], HD)).then_inc(xw_ready, 1)

            def y_take(f):
                stt(PR[:, f, 0:NP_], CV[:, f, 0:NP_], col(R_N + f), full("y", f)[:, 0:NP_], ALU.mult, ALU.add
                    ).then_inc(v_took, 1)

            for h in range(H):
                eng.wait_ge(a_took, ja["diff", h] + 1)
                tt(EM[:, h % 4], EM[:, h % 4], CBm[:, h // 8]).then_inc(m_ready, 1)
                if h % 2 and h >= 3:
                    y_take(h // 2 - 1)
            y_take(KT - 1)
            for b in range(NS):
                eng.wait_ge(s1_in[b % 2], 16 * (b // 2 + 1))
                eng.wait_ge(bcb_in[b % 2], 16 * (b // 2 + 1))
                for f in range(KT):
                    u = b * KT + f
                    eng.wait_ge(u1_ready, u + 1)
                    st = S1[:, b % 2, f]
                    stt(st, st, EX[:, b, f:f + 1], U1[:, u % 2], ALU.mult, ALU.add).then_inc(u1_used, 1)
                    eng.wait_ge(u1_used, u + 1)
                    if u:
                        eng.wait_ge(s1_new, u)
                    nc.vector.tensor_tensor_reduce(
                        junk, st, BCb[:, b % 2, (G + f // 4) * N:(G + f // 4 + 1) * N], 1.0, 0.0,
                        ALU.mult, ALU.add, yss[:, b, f:f + 1]).then_inc(s1_new, 1)
            eng.wait_ge(s1_new, NS * KT)
            link(tt(DX, CV[:, 0:KT, NP_:T].rearrange("p f b -> p b f"),
                    prm[:, R_N:R_N + KT].rearrange("p (o f) -> p o f", o=1).to_broadcast([P, NS, KT])))
            link(tt(PR[:, 0:KT, NP_:T].rearrange("p f b -> p b f"), yss, DX, ALU.add))

            eng.wait_ge(hg_sig, 2)
            for h in range(HH):
                ts(KK[:, h], KK[:, h], oml[:, h:h + 1], ALU.mult).then_inc(hg_fk, 1)
                ts(PR[:, P_F + h], PR[:, P_F + h], oml[:, h:h + 1], ALU.mult, lb[:, h:h + 1], ALU.add).then_inc(hg_fk, 1)
            eng.wait_ge(hg_fk, 2 * HH)
            eng.wait_ge(a_full, ja["st", 1] + 1)

            def halves(x, s):
                y = x.rearrange("p h (n w s) -> p h n w s", w=2, s=s)
                return y[:, :, :, 0], y[:, :, :, 1]

            def last_of(x, s):
                return x[:, :, :, s - 1:s].to_broadcast([P, 2, NP_ // (2 * s), s])

            def tree(pair):
                h = slice(2 * pair, 2 * pair + 2)
                f2 = PR[:, P_F + 2 * pair:P_F + 2 * pair + 2, 0:NP_]
                q2 = PR[:, P_Q + 2 * pair:P_Q + 2 * pair + 2, 0:NP_]
                k2 = KK[:, h, 0:NP_]
                if pair:
                    eng.wait_ge(v_full, jv["off", 2 * pair - 1] + 1)
                    eng.wait_ge(a_full, ja["klt", 2 * pair - 1] + 1)
                link(nc.vector.tensor_copy(R, f2))
                link(nc.vector.memset(L, 1.0))
                for a in range(8):
                    s = 2 ** a
                    ql, qr = halves(q2, s)
                    kl, kr = halves(k2, s)
                    Rl, Rr = halves(R, s)
                    Ll, Lr = halves(L, s)
                    ol, orr = halves(QK[:, :, a], s)
                    tt(ol, kl, Ll).then_inc(qk_ready, 1)
                    tt(orr, qr, Rr).then_inc(qk_ready, 1)
                    link(tt(Ll, Ll, last_of(Rr, s)))
                    if a < 7:
                        link(tt(Rr, Rr, last_of(Rl, s)))
                tt(KL, k2, L).then_inc(kl_ready, 1)

            for h in range(HH):
                if h % 2 == 0:
                    tree(h // 2)
                if h >= 2:
                    eng.wait_ge(a_full, ja["o", h - 2] + 1)
                for i in range(2):
                    for b in range(2):
                        if b == 0 and (h or i):
                            eng.wait_ge(at_ready, 2 * h + i)
                        tt(LVt[:, i, 4 * b:4 * b + 4].rearrange("p a b -> p (a b)"), full("lv", h, i, b)[:, :],
                           K[:, K_LM + 512 * b:K_LM + 512 * b + 512]).then_inc(v_took, 1)
                    took("lv", h, i, 1)
                    nc.vector.tensor_reduce(AT[:, h % 2, 256 * i:256 * i + P], LVt[:, i].rearrange("p a c -> p c a"),
                                            AX.X, ALU.add).then_inc(at_ready, 1)
                nc.vector.tensor_copy(AT[:, h % 2, P:2 * P], full("off", h)[:, 0:P]).then_inc(v_took, 1)
            for b in range(NS):
                eng.wait_ge(s2_in[b % 2], 16 * (b // 2 + 1))
                for h in range(HH):
                    u = b * HH + h
                    eng.wait_ge(u2_ready, u + 1)
                    st = S2[:, b % 2, h]
                    stt(st, st, PR[:, P_F + h, NP_ + b:NP_ + b + 1], U2[:, u % 2], ALU.mult, ALU.add).then_inc(s2_new, 1)
            ps = full("os")
            nc.vector.tensor_copy(PR[:, P_F:P_F + HH, NP_:T], ps[:, 0:64].rearrange("p (h b) -> p h b", h=HH)
                                  ).then_inc(v_took, 1)

            y = PR[:, 0:KT]
            o = PR[:, P_F:P_F + HH]
            eng.wait_ge(gate_silu, 2)
            tt(y, y, PR[:, P_Z:P_Z + KT]).then_inc(y_raw, 1)
            for g in range(G):
                ts(ms8[:, g], full("yn", g)[:, 0:T], 1.0 / (SD // G), ALU.mult, EPS, ALU.add).then_inc(v_took, 1)
            eng.wait_ge(sd_m, 1)
            link(nc.vector.reciprocal(ms8[:, 2:4], ms8[:, 2:4]))
            for f in range(KT):
                stt(y[:, f], y[:, f], col(R_SN + f), ms8[:, 2 + f // 4], ALU.mult, ALU.mult).then_inc(mixed, 1)
            eng.wait_ge(mixed, KT)
            for h in range(HH):
                ts(ms8[:, h], full("on", h)[:, 0:T], 1.0 / DV, ALU.mult, EPS, ALU.add).then_inc(v_took, 1)
            eng.wait_ge(sd_m, 2)
            link(nc.vector.reciprocal(ms8[:, :], ms8[:, :]))
            link(tt(ms8[:, :], ms8[:, :], PR[:, P_G:P_G + HH]))
            for h in range(HH):
                stt(o[:, h], o[:, h], col(R_HN + h), ms8[:, h], ALU.mult, ALU.mult).then_inc(mixed, 1)
            for c in range(KT):
                tt(xT[:, c], xT[:, c], full("mix", c)[:, 0:T], ALU.add).then_inc(v_took, 1)
            norm(1, R_FFN)

            def bc(x, n=4):
                return x.rearrange("p (t o) -> p t o", o=1).to_broadcast([P, 3, n])

            def red(out, x, op):
                link(nc.vector.tensor_reduce(out, x, AX.X, op))

            def first_max(out, x, tmp, m):
                red(m, x, ALU.max)
                link(tt(tmp, x, bc(m), ALU.is_equal))
                link(tt(tmp, tmp, w4))
                red(m, tmp, ALU.max)
                link(tt(out, tmp, bc(m), ALU.is_equal))

            w4 = K[:, K_W4:K_W4 + 4].rearrange("p (o e) -> p o e", o=1).to_broadcast([P, 3, 4])
            link(nc.vector.memset(rt[:, :, :], 0.0))
            link(nc.vector.memset(acc[:, :, :], 0.0))
            ps = full("rt")
            link(nc.vector.tensor_copy(rt[:, 0:2], ps[:, 0:40].rearrange("p (t c) -> p t c", c=20)))
            nc.vector.tensor_copy(rt[0:NS, 2], ps[0:NS, 40:60]).then_inc(v_took, 1)
            took("rt")
            lg = rt[:, :, 0:4]
            red(r1[:, 0], lg, ALU.max)
            tt(rs[:, 0], lg, bc(r1[:, 0]), ALU.subtract).then_inc(r_in, 1)
            link(tt(rs[:, 3], lg, rb[:, 0:4].rearrange("p (o e) -> p o e", o=1).to_broadcast([P, 3, 4]), ALU.add))
            ohg = rs[:, 5]
            first_max(ohg, rs[:, 3], rs[:, 4], r1[:, 3])
            eng.wait_ge(r_exp, 1)
            red(r1[:, 1], rs[:, 1], ALU.add)
            link(nc.vector.reciprocal(r1[:, 2], r1[:, 1]))
            link(tt(rs[:, 2], rs[:, 1], bc(r1[:, 2])))
            link(tt(rs[:, 6], rs[:, 2], ohg))
            red(r1[:, 5], rs[:, 6], ALU.add)
            g4 = gates[:, :, :].rearrange("p t (g e) -> p t g e", g=EG)
            ohb = ohg.rearrange("p t (g o) -> p t g o", o=1).to_broadcast([P, 3, EG, EPG])
            link(tt(g4, rt[:, :, 4:20].rearrange("p t (g e) -> p t g e", g=EG), ohb))
            red(rs[:, 7], g4.rearrange("p t g e -> p t e g"), ALU.add)
            link(tt(g4, rb[:, 4:20].rearrange("p (o g e) -> p o g e", o=1, g=EG).to_broadcast([P, 3, EG, EPG]), ohb))
            red(rs[:, 14], g4.rearrange("p t g e -> p t e g"), ALU.add)
            red(r1[:, 6], rs[:, 7], ALU.max)
            tt(rs[:, 8], rs[:, 7], bc(r1[:, 6]), ALU.subtract).then_inc(r_in, 1)
            link(tt(rs[:, 11], rs[:, 7], rs[:, 14], ALU.add))
            first_max(rs[:, 12], rs[:, 11], rs[:, 4], r1[:, 3])
            link(stt(rs[:, 13], rs[:, 12], -BIG, rs[:, 11], ALU.mult, ALU.add))
            first_max(rs[:, 15], rs[:, 13], rs[:, 4], r1[:, 3])
            link(tt(rs[:, 16], rs[:, 12], rs[:, 15], ALU.add))
            eng.wait_ge(r_exp, 2)
            red(r1[:, 7], rs[:, 9], ALU.add)
            link(nc.vector.reciprocal(r1[:, 0], r1[:, 7]))
            link(tt(rs[:, 10], rs[:, 9], bc(r1[:, 0])))
            link(tt(rs[:, 10], rs[:, 10], rs[:, 16]))
            red(r1[:, 1], rs[:, 10], ALU.add)
            link(nc.vector.reciprocal(r1[:, 2], r1[:, 1]))
            link(tt(r1[:, 2], r1[:, 2], r1[:, 5]))
            link(tt(rs[:, 10], rs[:, 10], bc(r1[:, 2])))
            link(tt(g4, ohb, rs[:, 10].rearrange("p t (o e) -> p t o e", o=1).to_broadcast([P, 3, EG, EPG])))
            for name in jv.at:
                if name[0] == "skip":
                    nc.vector.tensor_copy(rstd[:, 0, n0(name)], full(*name)[:, 0:1]).then_inc(v_took, 1)

            A0, V0 = ja["gate", 0, 0], jv["up", 0, 0]
            with eng.Fori(0, 4) as it:
                for j in range(4):
                    ex = it * 4 + j
                    for b, (t0, n) in enumerate(TOK):
                        u = 3 * j + b
                        na, nv = 2 * u, 3 * u
                        eng.wait_ge(v_full, it * 36 + (V0 + nv + 1))
                        eng.wait_ge(a_took, it * 24 + (A0 + na + 1))
                        stt(act[0:n, u % 2], sil[0:n, u % 2], gates[0:n, b, ds(ex, 1)], bank[4 + nv % 4][0:n, :],
                            ALU.mult, ALU.mult).then_inc(v_took, 1)
                        for half in range(2):
                            eng.wait_ge(v_full, it * 36 + (V0 + nv + half + 2))
                            c = acc[0:n, b, 512 * half:512 * half + 512]
                            tt(c, c, bank[4 + (nv + half + 1) % 4][0:n, :], ALU.add).then_inc(v_took, 1)
            took("down", E - 1, 2, 1)
            for ft in range(KT):
                tt(xT[:, ft], xT[:, ft], full("yt", ft)[:, 0:T], ALU.add).then_inc(v_took, 1)
            norm(2, R_PLE)

            for c in range(KT):
                ps = full("pp", c)
                eng.wait_ge(a_took, ja["pg", c] + 1)
                link(tt(gs[:, c % 2], gs[:, c % 2], ps[:, 0:T]))
                tt(xT[:, c], xT[:, c], gs[:, c % 2], ALU.add).then_inc(v_took, 1)
            norm(3, R_FIN)


_INS = ["x_prompt", "x_sample", "state_ssm", "state_conv", "state_hgrn", "p_prompt", "p_sample", "norm_mix_w",
        "w_in", "conv_w", "conv_b", "dt_bias", "a_log", "d_skip", "ssd_norm_w", "lb_logits", "hg_norm_w",
        "w_out", "norm_ffn_w", "w_router_group", "b_router_group", "w_router_expert", "b_router_expert",
        "w_exp_gate", "w_exp_up", "w_exp_down", "norm_ple_w", "w_ple_gate", "w_ple_proj", "final_norm_w"]
_OUTS = [(1, NP_, D), (NS, 1, D), (1, 1, H, HD, N), (1, 1, 3, CONV), (1, 1, HH, DK, DV),
         (1, NS, H, HD, N), (1, NS, 3, CONV), (1, NS, HH, DK, DV)]


def kernel(**inputs):
    import concourse.bacc as bacc
    from concourse.bass_utils import run_bass_kernel_spmd

    nc = bacc.Bacc("TRN2", target_bir_lowering=False, num_devices=1)
    arrays, ins = {}, {}
    for name in _INS:
        x = np.ascontiguousarray(inputs[name])
        arrays[f"in_{name}"] = x
        ins[name] = nc.dram_tensor(f"in_{name}", x.shape, mybir.dt.from_np(x.dtype), kind="ExternalInput").ap()
    arrays["constants"] = constants()
    consts = nc.dram_tensor("constants", (P, K_N), F32, kind="ExternalInput").ap()
    outs = [nc.dram_tensor(f"out_{i}", shape, F32, kind="ExternalOutput").ap() for i, shape in enumerate(_OUTS)]
    build(nc, ins, outs, consts)
    r = run_bass_kernel_spmd(nc, [arrays], core_ids=[0])
    return tuple(r.results[0][f"out_{i}"] for i in range(len(_OUTS)))
```

```python
from contextlib import ExitStack

import concourse.bass as bass
import numpy as np
from concourse import mybir

ALU = mybir.AluOpType
ACT = mybir.ActivationFunctionType
AX = mybir.AxisListType
F32 = mybir.dt.float32

P = 128
D = 1024
NP_, NS = 256, 8
T = NP_ + NS
KT = D // P
H, HD, N = 16, 64, 128
G = 2
SD = H * HD
CONV = SD + 2 * G * N
CT = CONV // P
HH, DK, DV = 8, 128, 128
E, EG, EPG, FF = 16, 4, 4, 512
TOP_K = 2
FAR = 1e6
PLE = 256
EPS = 1e-6
ARENA = 43400
TOK = [(0, 128), (128, 128), (256, 8)]
BIG = 1e30

C_Z, C_X, C_DT, C_Q = 0, SD, SD + CONV, SD + CONV + H
P_X, P_Q, P_F, P_V, P_G, P_Z = 0, 12, 20, 28, 36, 44
NPROJ = 52
LEVELS = 7
K_ID, K_CAUSAL, K_ONES, K_AFTER, K_LM, K_W4 = 0, 128, 256, 512, 640, 640 + 1024
K_IOTA = K_W4 + 4
K_TOK = K_IOTA + 384
K_N = K_TOK + 3
R_CW, R_CB, R_SN, R_HN, R_MIX, R_FFN, R_PLE, R_FIN, R_LB = 0, 48, 60, 68, 76, 84, 92, 100, 108
R_N = 124


def constants():
    i = np.arange(P)
    row, col = i[:, None], i[None, :]
    c = np.zeros((P, K_N), np.float32)
    c[:, K_ID:K_ID + P] = row == col
    c[:, K_CAUSAL:K_CAUSAL + P] = row <= col
    c[:, K_ONES:K_ONES + P] = 1.0
    c[:, K_ONES + P:K_ONES + 2 * P] = row <= col
    c[:, K_AFTER:K_AFTER + P] = row > col
    for a in range(LEVELS):
        x = row ^ col
        c[:, K_LM + a * P:K_LM + (a + 1) * P] = (x >= 2 ** a) & (x < 2 ** (a + 1)) & (row < col)
    c[:, K_LM + LEVELS * P:K_LM + (LEVELS + 1) * P] = row == col
    c[:, K_W4:K_W4 + 4] = [4, 3, 2, 1]
    c[:, K_IOTA:K_IOTA + 3 * P] = np.arange(1, 3 * P + 1)
    c[:, K_TOK:K_TOK + 3] = row + P * np.arange(3)
    return c


class JobList:

    def __init__(self):
        self.at = {}

    def add(self, *name):
        self.at[name] = len(self.at)

    def __getitem__(self, name):
        return self.at[name if isinstance(name, tuple) else (name,)]


class ExpertSems:

    def __init__(self, sem, k):
        def pair(name):
            return [sem(f"{k}_{name}{i}") for i in range(2)]

        self.g_full, self.g_took = sem(f"{k}_g_full"), sem(f"{k}_g_took")
        self.u_full, self.u_took = sem(f"{k}_u_full"), sem(f"{k}_u_took")
        self.x_full, self.x_took = sem(f"{k}_x_full"), sem(f"{k}_x_took")
        self.t_full, self.t_took = sem(f"{k}_t_full"), sem(f"{k}_t_took")
        self.d_full, self.d_took = sem(f"{k}_d_full"), sem(f"{k}_d_took")
        self.wg, self.wu, self.wd = pair("wg"), pair("wu"), pair("wd")
        self.rows, self.sent = pair("rows"), pair("sent")


def make_jobs():
    a, v = JobList(), JobList()
    for ft in range(KT):
        a.add("xT", ft)
    v.add("prm")
    v.add("prmD")
    v.add("cst")
    v.add("norm", 0)
    for n in range(NPROJ):
        a.add("proj", n)
    v.add("dt")
    for tt in range(2):
        for half in range(2):
            v.add("xs", tt, half)
    v.add("bcs")
    for g in range(G):
        v.add("cb", g)
    v.add("dts")
    for f in range(KT):
        v.add("y", f)
    a.add("btok")
    a.add("w")
    for i in range(3):
        a.add("tail", i)
    for h in range(H):
        a.add("diff", h)
    for i in range(2):
        a.add("st", i)
    for tt in range(2):
        for half in range(2):
            a.add("vtok", tt, half)
    for half in range(2):
        a.add("vs", half)
    for h in range(HH):
        for tt in range(2):
            for b in range(2):
                v.add("lv", h, tt, b)
        v.add("off", h)
        a.add("o", h)
        a.add("klt", h)
        a.add("sth", h)
    v.add("os")
    for g in range(G):
        v.add("yn", g)
    for h in range(HH):
        v.add("on", h)
    for c in range(KT):
        v.add("mix", c)
    v.add("norm", 1)
    v.add("rt")
    for tt in range(3):
        for half in range(2):
            a.add("ht", tt, half)
    v.add("cnt")
    v.add("tab")
    for ft in range(KT):
        v.add("yt", ft)
    v.add("norm", 2)
    for i in range(2):
        a.add("pT", i)
    for c in range(KT):
        a.add("pg", c)
        v.add("pp", c)
    v.add("norm", 3)
    for tt in range(3):
        for half in range(2):
            a.add("out", tt, half)
    return a, v


def build(nc, ins, outs, consts):
    ja, jv = make_jobs()
    ds = bass.ds

    def dram(name, shape):
        return nc.dram_tensor(name, shape, F32, kind="Internal").ap()

    bc_rows = dram("bc_rows", (NS, 2 * G * N))
    v_rows = dram("v_rows", (NS, HH * DV))

    h_rows = dram("h_rows", (T, D))
    pair_rows = dram("pair_rows", (TOP_K * T, D))

    w_in = ins["w_in"][0].rearrange("(k p) c -> p k c", p=P)
    w_out = ins["w_out"][0].rearrange("(k p) c -> p k c", p=P)
    w_pg = ins["w_ple_gate"][0].rearrange("(k p) c -> p k c", p=P)
    w_pp = ins["w_ple_proj"][0].rearrange("(k p) c -> p k c", p=P)

    ctx = ExitStack()
    with ctx:
        def sb(name, shape):
            return ctx.enter_context(nc.sbuf_tensor(name, shape, F32))

        def sem(name):
            return ctx.enter_context(nc.semaphore(name))

        K = sb("K", [P, K_N])
        ident = K[:, K_ID:K_ID + P]
        ones = K[:, K_ONES:K_ONES + P]
        xT = sb("xT", [P, KT, T])
        hT = sb("hT", [P, KT, T])
        sq = sb("sq", [P, KT, T])
        prm = sb("prm", [P, R_N + 8])
        rstd = sb("rstd", [P, 2, T])
        arena = sb("arena", [P, ARENA])
        used = [0]

        def carve(*shape, at=None):
            if at is not None:
                used[0] = at
            n = int(np.prod(shape))
            v = arena[:, used[0]:used[0] + n]
            used[0] += n
            assert used[0] <= ARENA, used[0]
            if len(shape) == 1:
                return v
            names = "abcd"[:len(shape)]
            return v.rearrange(f"p ({' '.join(names)}) -> p {' '.join(names)}",
                               **{c: s for c, s in zip(names, shape)})

        PR = carve(NPROJ, T)
        W = carve(2, 4096)
        smalls = carve(900)
        early = used[0]
        CV = carve(CT, T)
        vtok = carve(2, D)
        temp = used[0]
        slot0 = early + 2 * KT * T
        xdt = carve(2, D)
        xw = carve(2, D)
        btok = carve(2, G * N)
        CBm = carve(G, 384)
        AM = carve(2, H, P)
        EM = carve(4, 384)
        stage = carve(KT, P)
        S1 = carve(2, KT, N)
        BCb = carve(2, 2 * G * N)
        U1 = carve(2, N)
        xtok = carve(3, D, at=temp)
        prow = carve(P)
        drow = carve(P)
        crow = carve(CONV)
        convt = carve(CT, NS)
        convu = carve(CT, NS, 3)
        spare = hT[:, :, :].rearrange("p a b -> p (a b)")
        tail, bcs = spare[:, 0:CONV], spare[0:NS, CONV:CONV + 2 * G * N]
        vss = CV[0:NS, KT:CT].rearrange("p a b -> p (a b)")[:, 0:HH * DV]
        QK = carve(2, 8, NP_, at=temp)
        R = carve(2, NP_)
        L = carve(2, NP_)
        KL = carve(2, NP_)
        klt = carve(2, 2, P)
        LVt = carve(2, 8, P)
        AT = carve(2, 384)
        stage_h = carve(HH, DV)
        S2 = carve(2, HH, DV)
        vb = carve(2, HH * DV)
        U2 = carve(2, DV)
        junk = rstd[:, 0, 0:N]
        KK = sq
        sq16 = carve(KT, T, at=early)
        ms8 = carve(KT, T)
        assert used[0] <= slot0
        htok = carve(3, D, at=early)
        EW = [carve(3, 4096, at=slot0), carve(3, 4096, at=0)]
        xg = carve(2, D)
        xgT = carve(2, KT, P)
        sil = carve(2, FF)
        act = carve(2, FF)
        actT = carve(2, 4, P)
        ys = carve(2, D)
        assert used[0] <= early
        OH = carve(2, 3, P, at=slot0 + 12288)
        rv = carve(3, E, 4)
        tabf = carve(3 * E, 4)
        Mt = carve(3, E)
        slot1 = carve(3, E)
        pairs = carve(3, 2, D, at=0)
        acc = carve(3, D)
        WP = carve(2, 4096, at=slot0)
        wpp = carve(2, D)
        ptok = carve(3, PLE)
        assert used[0] <= slot0 + 12288
        pT = carve(2, T, at=12288)
        gs = carve(2, T)
        ostage = carve(3, D)

        sm = [0]

        def small(*shape):
            n = int(np.prod(shape))
            v = smalls[:, sm[0]:sm[0] + n]
            sm[0] += n
            assert sm[0] <= 900
            if len(shape) == 1:
                return v
            names = "abcd"[:len(shape)]
            return v.rearrange(f"p ({' '.join(names)}) -> p {' '.join(names)}",
                               **{c: s for c, s in zip(names, shape)})

        wdt = small(KT, H)
        dtb = small(H)
        alog = small(H)
        aneg = small(H)
        dtr = small(3, H)
        dt1 = small(3, H)
        dt2 = small(3, H)
        dt3 = small(3, H)
        dt4 = small(3, H)
        dtv = small(3, H)
        av = small(3, H)
        wdec = small(2, H)
        ea = small(H)
        DX = small(NS, KT)
        EX = small(NS, KT)
        xds = small(NS, KT)
        yss = small(NS, KT)
        lbt = small(2, HH)
        lb = small(HH)
        oml = small(HH)
        lbe = small(3, HH)
        dpair = small(2)
        wr = sb("wr", [P, KT, 20])
        rb = sb("rb", [P, 20])
        rt = sb("rt", [P, 3, 20])
        rs = sb("rs", [P, 18, 3, 4])
        gates = sb("gates", [P, 3, E])
        r1 = sb("r1", [P, 8, 3])
        chips = sb("chips", [P, 2])
        row_of = ctx.enter_context(nc.sbuf_tensor("rows", [P, 2, 3 * E], mybir.dt.uint32))
        most = ctx.enter_context(nc.sbuf_tensor("most", [P, 1], mybir.dt.int32))
        dtx = sq[0:NS, 0:4, :].rearrange("p a b -> p (a b)")[:, 0:D]
        eax = sq[0:NS, 4:8, :].rearrange("p a b -> p (a b)")[:, 0:D]

        bank = [ctx.enter_context(nc.psum_tensor(f"bank{i}", [P, 512], F32)) for i in range(8)]

        a_full, a_took = sem("a_full"), sem("a_took")
        v_full, v_took = sem("v_full"), sem("v_took")
        ld_k = sem("ld_k")
        ld_x = sem("ld_x")
        ld_p = sem("ld_p")
        ld_s = sem("ld_s")
        ld_r = sem("ld_r")
        w_slot = [sem("w_slot0"), sem("w_slot1")]
        sq_done, sd_done, norm_done = sem("sq_done"), sem("sd_done"), sem("norm_done")
        dve, o_dve = sem("dve"), sem("o_dve")
        ea_ready = sem("ea_ready")
        conv_done = sem("conv_done")
        silu_done = sem("silu_done")
        sp = sem("softplus")
        dt_ready = sem("dt_ready")
        am_ready = sem("am_ready")
        xw_ready = sem("xw_ready")
        dtx_ready = sem("dtx_ready")
        m_ready = sem("m_ready")
        bcs_out, bcb_in = sem("bcs_out"), [sem("bcb_in0"), sem("bcb_in1")]
        s1_in = [sem("s1_in0"), sem("s1_in1")]
        s1_new, s1_out = sem("s1_new"), [sem("s1_out0"), sem("s1_out1")]
        xds_ready = sem("xds_ready")
        u1_ready, u1_used = sem("u1_ready"), sem("u1_used")
        store = sem("store")
        hg_sig, hg_fk = sem("hg_sig"), sem("hg_fk")
        drow_ready = sem("drow_ready")
        mixers_done = sem("mixers_done")
        lb_exp, lb_in = sem("lb_exp"), sem("lb_in")
        qk_ready, kl_ready = sem("qk_ready"), sem("kl_ready")
        at_ready = sem("at_ready")
        vs_out, vb_in = sem("vs_out"), [sem("vb_in0"), sem("vb_in1")]
        s2_in = [sem("s2_in0"), sem("s2_in1")]
        s2_new, s2_out = sem("s2_new"), [sem("s2_out0"), sem("s2_out1")]
        s2_pe = sem("s2_pe")
        u2_ready = sem("u2_ready")
        y_raw, gate_silu, sq_m, sd_m, mixed = (sem("y_raw"), sem("gate_silu"), sem("sq_m"), sem("sd_m"),
                                               sem("mixed"))
        r_in, r_exp = sem("r_in"), sem("r_exp")
        hrow_out = sem("hrow_out")
        mt_ready, oh_ready, oh_used, tab_ready = sem("mt_ready"), sem("oh_ready"), sem("oh_used"), sem("tab_ready")
        xg_clear = sem("xg_clear")
        pair_in, acc_ready = sem("pair_in"), sem("acc_ready")
        main, over = ExpertSems(sem, "m"), ExpertSems(sem, "o")
        o_tab, o_tab_took, o_oh_ready, o_oh_used = sem("o_tab"), sem("o_tab_took"), sem("o_oh_ready"), sem("o_oh_used")
        wp_again = sem("wp_again")
        ld_pp = sem("ld_pp")
        o_store = sem("o_store")
        block = ctx.enter_context(nc.Block())

        PROJ0 = ja["proj", 0]

        @block.sync
        def _(eng):
            eng.dma_start(K[:, :], consts).then_inc(ld_k, 16)
            for i, (t0, n) in enumerate(TOK):
                src = ins["x_prompt"][0, t0:t0 + n] if i < 2 else ins["x_sample"][:, 0]
                eng.dma_start(xtok[0:n, i], src).then_inc(ld_x, 16)

            def w_group(slot, group, col, after):
                if after is not None:
                    eng.wait_ge(a_full, after)
                eng.dma_start(W[:, slot].rearrange("p (k c) -> p k c", k=KT),
                              w_in[:, :, col]).then_inc(w_slot[slot], 16)

            for g in range(3):
                w_group(g % 2, g, slice(C_X + 512 * g, C_X + 512 * g + 512),
                        PROJ0 + 4 * (g - 1) if g >= 2 else None)
            with eng.Fori(0, 4) as it:
                for j in range(2):
                    w_group((3 + j) % 2, None, ds(C_Q + 512 * j + it * 1024, 512),
                            it * 8 + (PROJ0 + 4 * (2 + j)))
            for g in range(2):
                w_group((11 + g) % 2, None, slice(C_Z + 512 * g, C_Z + 512 * g + 512),
                        PROJ0 + 4 * (10 + g))
            for g in range(4):
                if g < 2:
                    eng.wait_ge(a_full, PROJ0 + 4 * (12 + g))
                else:
                    eng.wait_ge(v_full, jv["mix", 2 * (g - 2) + 1] + 1)
                eng.dma_start(W[:, (13 + g) % 2].rearrange("p (k c) -> p k c", k=16),
                              w_out[:, :, 256 * g:256 * g + 256]).then_inc(w_slot[(13 + g) % 2], 16)
            def weights(m, t, ex, h, p, first):
                for k, (name, slot, full, used_by) in enumerate((
                        ("w_exp_gate", m.wg, m.g_full, t - 1), ("w_exp_up", m.wu, m.u_full, t - 1),
                        ("w_exp_down", m.wd, m.d_full, t * 2 - 2))):
                    if not first:
                        eng.wait_ge(full, used_by)
                    eng.dma_start(EW[p][:, k].rearrange("p (k c) -> p k c", k=KT if k < 2 else 4),
                                  ins[name][0, ds(ex, 1)].rearrange("e (k p) c -> p (e k) c", p=P)
                                  ).then_inc(slot[p], 16)

            def ple_weights(done):
                eng.dma_start(ptok[:, 0:2], ins["p_prompt"][0, 0].rearrange("(t p) c -> p t c", p=P)).then_inc(done, 16)
                eng.dma_start(ptok[0:NS, 2], ins["p_sample"][0, :, 0]).then_inc(done, 16)
                eng.dma_start(wpp[:, :], w_pp).then_inc(done, 16)
                for g in range(2):
                    eng.dma_start(WP[:, g].rearrange("p (k c) -> p k c", k=KT),
                                  w_pg[:, :, 512 * g:512 * g + 512]).then_inc(done, 16)

            eng.wait_ge(v_full, jv["os"] + 1)
            eng.wait_ge(a_took, ja["sth", HH - 1] + 1)
            eng.wait_ge(mixers_done, 1)
            weights(main, 0, 0, 0, 0, True)
            eng.wait_ge(v_full, jv["mix", KT - 1] + 1)
            weights(main, 1, 1, 0, 1, True)
            with eng.Fori(1, E // 2) as it:
                for p in range(2):
                    weights(main, it * 2 + p, it * 2 + p, it, p, False)
            eng.wait_ge(main.d_full, 2 * (E - 1))
            ple_weights(ld_pp)
            eng.wait_ge(tab_ready, 1)
            crowded = eng.value_load(most[0:1, 0:1], min_val=0, max_val=T)
            with eng.If(crowded > P):
                eng.wait_ge(main.d_full, 2 * E)
                eng.wait_ge(ld_pp, 80)
                for t in range(2):
                    weights(over, t, t, 0, t, True)
                with eng.Fori(1, E // 2) as it:
                    for p in range(2):
                        weights(over, it * 2 + p, it * 2 + p, it, p, False)
                with eng.Fori(E // 2, E) as it:
                    for p in range(2):
                        weights(over, it * 2 + p, it * 2 + (p - E), it, p, False)
                eng.wait_ge(over.d_full, 4 * E)
                ple_weights(wp_again)
                for p in range(2):
                    eng.wait_ge(over.sent[p], 16 * E)
            eng.wait_ge(main.d_full, 2 * E)
            for p in range(2):
                eng.wait_ge(main.sent[p], 16 * (E // 2))
            for k in range(TOP_K):
                r = pair_rows[k * T:(k + 1) * T]
                eng.dma_start(pairs[:, 0:2, k], r[0:NP_].rearrange("(t p) d -> p t d", p=P)).then_inc(pair_in, 16)
                eng.dma_start(pairs[0:NS, 2, k], r[NP_:T]).then_inc(pair_in, 16)
            for tt, (t0, n) in enumerate(TOK):
                eng.wait_ge(a_took, ja["out", tt, 1] + 1)
                dst = outs[0][0, t0:t0 + n] if tt < 2 else outs[1][:, 0]
                eng.dma_start(dst, ostage[0:n, tt]).then_inc(o_store, 16)
            eng.wait_ge(o_store, 48)

        @block.gpsimd
        def _(eng):
            for r, name, rows in ((R_CW, "conv_w", 48), (R_CB, "conv_b", 12), (R_SN, "ssd_norm_w", 8),
                                  (R_HN, "hg_norm_w", 8), (R_MIX, "norm_mix_w", 8), (R_FFN, "norm_ffn_w", 8),
                                  (R_PLE, "norm_ple_w", 8)):
                src = ins[name][0]
                src = (src.rearrange("k (c p) -> (k c) p", p=P) if name == "conv_w"
                       else src.rearrange("(c p) -> c p", p=P))
                eng.dma_start(prow[r:r + rows], src).then_inc(ld_p, 16)
            eng.dma_start(prow[R_FIN:R_FIN + 8], ins["final_norm_w"].rearrange("(c p) -> c p", p=P)).then_inc(ld_p, 16)
            eng.dma_start(prow[R_LB:R_LB + 16], ins["lb_logits"].rearrange("r (c p) -> (r c) p", p=P)).then_inc(ld_p, 16)
            eng.dma_start(dpair[0:KT], ins["d_skip"][0].rearrange("(f h) -> f h", h=2)).then_inc(ld_p, 16)
            eng.dma_start(crow[0:24], ins["state_conv"][0].rearrange("b k c -> (b k) c")).then_inc(ld_p, 16)
            eng.dma_start(wdt, w_in[:, :, C_DT:C_DT + H]).then_inc(ld_s, 16)
            eng.dma_start(dtb, ins["dt_bias"][0:1].to_broadcast([P, H])).then_inc(ld_s, 16)
            eng.dma_start(alog, ins["a_log"][0:1].to_broadcast([P, H])).then_inc(ld_s, 16)
            eng.dma_start(wr[:, :, 0:4], ins["w_router_group"][0].rearrange("(k p) c -> p k c", p=P)).then_inc(ld_r, 16)
            eng.dma_start(wr[:, :, 4:20], ins["w_router_expert"][0].rearrange("(k p) c -> p k c", p=P)).then_inc(ld_r, 16)
            eng.dma_start(rb[:, 0:4], ins["b_router_group"][0:1].to_broadcast([P, 4])).then_inc(ld_r, 16)
            eng.dma_start(rb[:, 4:20], ins["b_router_expert"][0:1].rearrange("o g e -> o (g e)").to_broadcast([P, E])
                          ).then_inc(ld_r, 16)
            eng.dma_start(outs[6][0, :, 0:2], ins["state_conv"][0, :, 1:3]).then_inc(store, 16)
            n_store = 1
            eng.wait_ge(v_took, jv["bcs"] + 1)
            eng.dma_start(bc_rows, bcs[:, :]).then_inc(bcs_out, 16)
            eng.wait_ge(bcs_out, 16)
            for b in range(NS):
                s = b % 2
                if b >= 2:
                    eng.wait_ge(s1_new, KT * (b - 1))
                    eng.wait_ge(s1_out[s], 16 * (b // 2))
                else:
                    eng.wait_ge(dt_ready, 1)
                eng.dma_start(BCb[:, s], bc_rows[b:b + 1].to_broadcast([P, 2 * G * N])).then_inc(bcb_in[s], 16)
                eng.dma_start(S1[:, s], ins["state_ssm"][0, b].rearrange("h p n -> (h p) n")
                              .rearrange("(f q) n -> q f n", q=P)).then_inc(s1_in[s], 16)
                if b >= 1:
                    q = b - 1
                    eng.wait_ge(s1_new, KT * (q + 1))
                    eng.dma_start(outs[5][0, q].rearrange("h p n -> (h p) n").rearrange("(f q) n -> q f n", q=P),
                                  S1[:, q % 2]).then_inc(s1_out[q % 2], 16)
            q = NS - 1
            eng.wait_ge(s1_new, KT * (q + 1))
            eng.dma_start(outs[5][0, q].rearrange("h p n -> (h p) n").rearrange("(f q) n -> q f n", q=P),
                          S1[:, q % 2]).then_inc(s1_out[q % 2], 16)
            for i in range(3):
                eng.wait_ge(a_took, ja["tail", i] + 1)
            eng.dma_start(outs[3][0, 0], tail[0:3]).then_inc(store, 16)
            eng.dma_start(outs[6][0, :, 2], tail[3:11]).then_inc(store, 16)
            eng.wait_ge(a_took, ja["st", 1] + 1)
            eng.dma_start(outs[2][0, 0].rearrange("h p n -> (h p) n").rearrange("(f q) n -> q f n", q=P),
                          stage).then_inc(store, 16)
            n_store += 3
            eng.wait_ge(a_took, ja["vs", 1] + 1)
            eng.dma_start(v_rows, vss[:, :]).then_inc(vs_out, 16)
            eng.wait_ge(vs_out, 16)
            eng.wait_ge(store, 16 * n_store)
            eng.wait_ge(s1_out[0], 16 * 4)
            eng.wait_ge(s1_out[1], 16 * 4)
            eng.wait_ge(v_took, jv["y", KT - 1] + 1)
            for b in range(NS):
                s = b % 2
                if b >= 2:
                    eng.wait_ge(s2_new, HH * (b - 1))
                    eng.wait_ge(s2_pe, b - 1)
                    eng.wait_ge(s2_out[s], 16 * (b // 2))
                eng.dma_start(vb[:, s], v_rows[b:b + 1].to_broadcast([P, HH * DV])).then_inc(vb_in[s], 16)
                eng.dma_start(S2[:, s], ins["state_hgrn"][0, b].rearrange("h k v -> k h v")).then_inc(s2_in[s], 16)
                if b >= 1:
                    q = b - 1
                    eng.wait_ge(s2_new, HH * (q + 1))
                    eng.dma_start(outs[7][0, q].rearrange("h k v -> k h v"), S2[:, q % 2]).then_inc(s2_out[q % 2], 16)
            q = NS - 1
            eng.wait_ge(s2_new, HH * (q + 1))
            eng.dma_start(outs[7][0, q].rearrange("h k v -> k h v"), S2[:, q % 2]).then_inc(s2_out[q % 2], 16)
            eng.wait_ge(a_took, ja["sth", HH - 1] + 1)
            eng.dma_start(outs[4][0, 0].rearrange("h k v -> k h v"), stage_h).then_inc(store, 16)
            n_store += 1
            eng.wait_ge(store, 16 * n_store)
            eng.wait_ge(s2_out[0], 16 * 4)
            eng.wait_ge(s2_out[1], 16 * 4)
            eng.memset(chips[:, 0:1], 0.0).then_inc(mixers_done, 1)
            eng.wait_ge(v_full, jv["mix", KT - 1] + 1)
            for p in range(2):
                eng.memset(xg[:, p], 0.0).then_inc(xg_clear, 1)

            def gather(m, t, base):
                p = t % 2
                if t >= 2:
                    eng.wait_ge(m.x_full, 2 * (t - 2) + 2)
                eng.indirect_dma_start(
                    out=xg[:, p], out_offset=None, in_=h_rows,
                    in_offset=bass.IndirectOffsetOnAxis(ap=row_of[:, 0, base + t:base + t + 1], axis=0),
                    bounds_check=T - 1, oob_is_err=False).then_inc(m.rows[p], 16)

            def scatter(m, t, base):
                p = t % 2
                eng.wait_ge(m.d_took, 2 * (t + 1))
                eng.indirect_dma_start(
                    out=pair_rows, out_offset=bass.IndirectOffsetOnAxis(ap=row_of[:, 1, base + t:base + t + 1], axis=0),
                    in_=ys[:, p], in_offset=None,
                    bounds_check=TOP_K * T - 1, oob_is_err=False).then_inc(m.sent[p], 16)

            def tokens(m, n, base):
                for t in range(n + 4):
                    if t < n:
                        gather(m, t, base)
                    if t >= 4:
                        scatter(m, t - 4, base)

            eng.wait_ge(tab_ready, 1)
            eng.wait_ge(hrow_out, 48)
            eng.wait_ge(xg_clear, 2)
            tokens(main, E, 0)
            crowded = eng.value_load(most[0:1, 0:1], min_val=0, max_val=T)
            with eng.If(crowded > P):
                eng.wait_ge(o_tab_took, 1)
                for p in range(2):
                    eng.wait_ge(main.sent[p], 16 * (E // 2))
                tokens(over, 2 * E, E)
                for p in range(2):
                    eng.wait_ge(over.sent[p], 16 * E)
            for p in range(2):
                eng.wait_ge(main.sent[p], 16 * (E // 2))

        @block.tensor
        def _(eng):
            mm = nc.tensor.matmul

            def bank_a(n):
                if not isinstance(n, int) or n >= 4:
                    eng.wait_ge(a_took, n - 3)

            def open_a(*name):
                n = ja[name]
                bank_a(n)
                return bank[n % 4]

            def open_v(*name):
                n = jv[name]
                if n >= 4:
                    eng.wait_ge(v_took, n - 3)
                return bank[4 + n % 4]

            def norm(k):
                ps = open_v("norm", k)
                eng.wait_ge(sq_done, k + 1)
                for ft in range(KT):
                    last = mm(ps[:, 0:T], ones, sq[:, ft], start=(ft == 0), stop=(ft == KT - 1))
                last.then_inc(v_full, 1)

            eng.wait_ge(ld_k, 16)
            eng.wait_ge(ld_x, 48)
            for ft in range(KT):
                ps = open_a("xT", ft)
                for i, (t0, n) in enumerate(TOK):
                    last = nc.tensor.transpose(ps[:, t0:t0 + n], xtok[0:n, i, ft * P:(ft + 1) * P], ident[0:n, 0:n])
                last.then_inc(a_full, 1)
            eng.wait_ge(ld_p, 16 * 11)
            nc.tensor.transpose(open_v("prm")[:, 0:R_N], prow[0:R_N], ident[0:R_N, 0:R_N]).then_inc(v_full, 1)
            eng.wait_ge(drow_ready, 1)
            nc.tensor.transpose(open_v("prmD")[:, 0:KT], drow[0:KT], ident[0:KT, 0:KT]).then_inc(v_full, 1)
            ps = open_v("cst")
            for c in range(CT):
                last = nc.tensor.transpose(ps[:, 24 * c:24 * c + 24], crow[0:24, c * P:(c + 1) * P], ident[0:24, 0:24])
            last.then_inc(v_full, 1)
            norm(0)

            def proj_group(slot, turn, first):
                eng.wait_ge(w_slot[slot], turn)
                for j in range(4):
                    bank_a(first + (PROJ0 + j))
                    w = W[:, slot].rearrange("p (k c) -> p k c", k=KT)
                    ps = bank[(PROJ0 + j) % 4]
                    for k in range(KT):
                        last = mm(ps[:, 0:T], w[:, k, j * P:(j + 1) * P], hT[:, k], start=(k == 0), stop=(k == KT - 1))
                    last.then_inc(a_full, 1)

            eng.wait_ge(norm_done, KT)
            for g in range(3):
                proj_group(g % 2, 16 * (g // 2 + 1), 4 * g)
            eng.wait_ge(ld_s, 48)
            ps = open_v("dt")
            for i, (t0, n) in enumerate(TOK):
                for k in range(KT):
                    last = mm(ps[0:n, H * i:H * i + H], hT[:, k, t0:t0 + n], wdt[:, k], start=(k == 0), stop=(k == KT - 1))
            last.then_inc(v_full, 1)
            with eng.Fori(0, 4) as it:
                for j in range(2):
                    g = 3 + j
                    proj_group(g % 2, it * 16 + 16 * (g // 2 + 1), it * 8 + 4 * g)
            for g in (11, 12):
                proj_group(g % 2, 16 * (g // 2 + 1), 4 * g)

            eng.wait_ge(silu_done, CT)
            for tt in range(2):
                for half in range(2):
                    ps = open_v("xs", tt, half)
                    for j in range(4):
                        last = nc.tensor.transpose(ps[:, j * P:(j + 1) * P],
                                                   CV[:, 4 * half + j, tt * P:(tt + 1) * P], ident)
                    last.then_inc(v_full, 1)
            ps = open_a("btok")
            for tt in range(2):
                for g in range(G):
                    last = nc.tensor.transpose(ps[:, (2 * tt + g) * P:(2 * tt + g + 1) * P],
                                               CV[:, KT + g, tt * P:(tt + 1) * P], ident)
            last.then_inc(a_full, 1)
            ps = open_v("bcs")
            for j in range(4):
                last = nc.tensor.transpose(ps[0:NS, j * P:(j + 1) * P], CV[:, KT + j, NP_:T], ident)
            last.then_inc(v_full, 1)
            for g in range(G):
                ps = open_v("cb", g)
                mm(ps[:, 0:NP_], CV[:, KT + g, 0:P], CV[:, KT + G + g, 0:NP_], start=True, stop=True)
                mm(ps[:, NP_:384], CV[:, KT + g, P:NP_], CV[:, KT + G + g, P:NP_], start=True, stop=True
                   ).then_inc(v_full, 1)
            ps = open_a("w")
            eng.wait_ge(dt_ready, 1)
            after = K[:, K_AFTER:K_AFTER + P]
            mm(ps[:, 0:H], after, av[:, 0], start=True, stop=False)
            mm(ps[:, 0:H], ones, av[:, 1], start=False, stop=True)
            mm(ps[:, H:2 * H], after, av[:, 1], start=True, stop=True).then_inc(a_full, 1)
            for i in range(3):
                ps = open_a("tail", i)
                for j in range(4):
                    last = nc.tensor.transpose(ps[0:11, j * P:(j + 1) * P], PR[:, 4 * i + j, NP_ - 3:T], ident)
                last.then_inc(a_full, 1)
            eng.wait_ge(dtx_ready, 2)
            ps = open_v("dts")
            for k, src in enumerate((dtx, eax)):
                for f in range(KT):
                    c = (k * KT + f) * NS
                    last = nc.tensor.transpose(ps[:, c:c + NS], src[:, f * P:(f + 1) * P], ident[0:NS, 0:NS])
            last.then_inc(v_full, 1)

            def diff(h):
                ps = open_a("diff", h)
                eng.wait_ge(am_ready, 2)
                causal = K[:, K_CAUSAL:K_CAUSAL + P]
                mm(ps[:, 0:NP_], AM[:, 0, h], K[:, K_CAUSAL:K_CAUSAL + NP_], start=True, stop=False, skip_group_check=True)
                mm(ps[:, P:NP_], av[:, 1, h:h + 1].to_broadcast([P, P]), causal, start=False, stop=True,
                   skip_group_check=True)
                mm(ps[:, NP_:384], AM[:, 1, h], causal, start=True, stop=True, skip_group_check=True).then_inc(a_full, 1)

            def y_head(h):
                ps = bank[4 + jv["y", h // 2] % 4] if h % 2 else open_v("y", h // 2)
                eng.wait_ge(m_ready, h + 1)
                r = slice(HD * (h % 2), HD * (h % 2) + HD)
                c = slice(HD * h, HD * h + HD)
                m = EM[:, h % 4]
                mm(ps[r, 0:NP_], xdt[:, 0, c], m[:, 0:NP_], start=True, stop=False, skip_group_check=True)
                last = mm(ps[r, P:NP_], xdt[:, 1, c], m[:, NP_:384], start=False, stop=True, skip_group_check=True)
                if h % 2:
                    last.then_inc(v_full, 1)

            for h in range(H + 2):
                if h < H:
                    diff(h)
                if h >= 2:
                    y_head(h - 2)
            eng.wait_ge(xw_ready, 2)
            for i in range(2):
                ps = open_a("st", i)
                for j in range(4):
                    f = 4 * i + j
                    for tt in range(2):
                        last = mm(ps[:, j * P:(j + 1) * P], xw[:, tt, f * P:(f + 1) * P],
                                  btok[:, tt, (f // 4) * N:(f // 4 + 1) * N], start=(tt == 0), stop=(tt == 1))
                last.then_inc(a_full, 1)

            for tt in range(2):
                for half in range(2):
                    ps = open_a("vtok", tt, half)
                    for j in range(4):
                        last = nc.tensor.transpose(ps[:, j * P:(j + 1) * P],
                                                   PR[:, P_V + 4 * half + j, tt * P:(tt + 1) * P], ident)
                    last.then_inc(a_full, 1)
            for half in range(2):
                ps = open_a("vs", half)
                for j in range(4):
                    last = nc.tensor.transpose(ps[0:NS, j * P:(j + 1) * P], PR[:, P_V + 4 * half + j, NP_:T], ident)
                last.then_inc(a_full, 1)
            eng.wait_ge(hg_fk, 2 * HH)
            for h in range(HH):
                hl = h % 2
                eng.wait_ge(qk_ready, 16 * (h // 2 + 1))
                for tt in range(2):
                    tk = slice(tt * P, (tt + 1) * P)
                    for b in range(2):
                        ps = open_v("lv", h, tt, b)
                        for j in range(4):
                            a = 4 * b + j
                            if a < LEVELS:
                                x = y = QK[:, hl, a, tk]
                            else:
                                x, y = KK[:, h, tk], PR[:, P_Q + h, tk]
                            last = mm(ps[:, j * P:(j + 1) * P], x, y, start=True, stop=True)
                        last.then_inc(v_full, 1)
                ps = open_v("off", h)
                mm(ps[:, 0:P], QK[:, hl, 7, 0:P], QK[:, hl, 7, P:NP_], start=True, stop=True).then_inc(v_full, 1)
                eng.wait_ge(at_ready, 2 * (h + 1))
                eng.wait_ge(v_took, jv["off", h] + 1)
                ps = open_a("o", h)
                hc = slice(h * P, (h + 1) * P)
                mm(ps[:, 0:NP_], vtok[:, 0, hc], AT[:, hl, 0:NP_], start=True, stop=False, skip_group_check=True)
                mm(ps[:, P:NP_], vtok[:, 1, hc], AT[:, hl, NP_:384], start=False, stop=True, skip_group_check=True
                   ).then_inc(a_full, 1)
                ps = open_a("klt", h)
                eng.wait_ge(kl_ready, h // 2 + 1)
                for tt in range(2):
                    last = nc.tensor.transpose(ps[:, tt * P:(tt + 1) * P], KL[:, hl, tt * P:(tt + 1) * P], ident)
                last.then_inc(a_full, 1)
                ps = open_a("sth", h)
                eng.wait_ge(a_took, ja["klt", h] + 1)
                for tt in range(2):
                    last = mm(ps[:, 0:DV], klt[:, hl, tt], vtok[:, tt, hc], start=(tt == 0), stop=(tt == 1))
                last.then_inc(a_full, 1)
            ps = open_v("os")
            for b in range(NS):
                for h in range(HH):
                    eng.wait_ge(s2_new, HH * b + h + 1)
                    last = mm(ps[:, h * NS + b:h * NS + b + 1], S2[:, b % 2, h], PR[:, P_Q + h, NP_ + b:NP_ + b + 1],
                              start=True, stop=True)
                last.then_inc(s2_pe if b < NS - 1 else v_full, 1)

            for g in range(G):
                ps = open_v("yn", g)
                eng.wait_ge(sq_m, 1)
                for j in range(4):
                    last = mm(ps[:, 0:T], ones, sq16[:, 4 * g + j], start=(j == 0), stop=(j == 3))
                last.then_inc(v_full, 1)
            for h in range(HH):
                ps = open_v("on", h)
                eng.wait_ge(sq_m, 2)
                mm(ps[:, 0:T], ones, sq16[:, h], start=True, stop=True).then_inc(v_full, 1)
            eng.wait_ge(mixed, 16)
            for c in range(KT):
                g = c // 2
                s = (13 + g) % 2
                if c % 2 == 0:
                    eng.wait_ge(w_slot[s], 16 * ((13 + g) // 2 + 1))
                w = W[:, s].rearrange("p (k c) -> p k c", k=16)
                ps = open_v("mix", c)
                for k in range(16):
                    x = PR[:, k] if k < 8 else PR[:, P_F + k - 8]
                    last = mm(ps[:, 0:T], w[:, k, (c % 2) * P:(c % 2) * P + P], x, start=(k == 0), stop=(k == 15))
                last.then_inc(v_full, 1)
            norm(1)

            eng.wait_ge(norm_done, 2 * KT)
            eng.wait_ge(ld_r, 64)
            ps = open_v("rt")
            for i, (t0, n) in enumerate(TOK):
                for k in range(KT):
                    last = mm(ps[0:n, 20 * i:20 * i + 20], hT[:, k, t0:t0 + n], wr[:, k], start=(k == 0), stop=(k == KT - 1))
            last.then_inc(v_full, 1)
            for i, (t0, n) in enumerate(TOK):
                for half in range(2):
                    ps = open_a("ht", i, half)
                    for j in range(4):
                        last = nc.tensor.transpose(ps[0:n, j * P:(j + 1) * P], hT[:, 4 * half + j, t0:t0 + n], ident)
                    last.then_inc(a_full, 1)
            eng.wait_ge(mt_ready, 3)
            ps = open_v("cnt")
            for i in range(4):
                c = slice(E * i, E * i + E)
                for k in range(min(i + 1, 3)):
                    last = mm(ps[:, c], ones if k < i else K[:, K_CAUSAL:K_CAUSAL + P], Mt[:, k],
                              start=(k == 0), stop=(k == min(i, 2)))
            last.then_inc(v_full, 1)

            def table(ps, turns, ready, used_, done):
                for t in range(turns):
                    eng.wait_ge(ready, t + 1)
                    for i in range(3):
                        last = mm(ps[:, 4 * t:4 * t + 4], OH[:, t % 2, i], rv[:, i, t % E], start=(i == 0), stop=(i == 2))
                    last.then_inc(used_ if t < turns - 1 else done, 1)

            table(open_v("tab"), E, oh_ready, oh_used, v_full)

            def gate(m, t, h, p, wait=True):
                wg = EW[p][:, 0].rearrange("p (k c) -> p k c", k=KT)
                eng.wait_ge(m.x_took, t * 2 + 2)
                if wait:
                    eng.wait_ge(m.t_took, t - 1)
                eng.wait_ge(m.wg[p], h * 16 + 16)
                for k in range(KT):
                    last = mm(bank[p][:, :], xgT[:, p, k], wg[:, k], start=(k == 0), stop=(k == KT - 1))
                last.then_inc(m.g_full, 1)

            def turn_rows(m, t, h, p):
                eng.wait_ge(m.rows[p], h * 16 + 16)
                for half in range(2):
                    for j in range(4):
                        c = slice((4 * half + j) * P, (4 * half + j + 1) * P)
                        last = nc.tensor.transpose(bank[2 + half][:, j * P:(j + 1) * P], xg[:, p, c], ident)
                    last.then_inc(m.x_full, 1)

            def up(m, t, h, p, wait=True):
                wu = EW[p][:, 1].rearrange("p (k c) -> p k c", k=KT)
                if wait:
                    eng.wait_ge(m.u_took, t - 1)
                eng.wait_ge(m.wu[p], h * 16 + 16)
                for k in range(KT):
                    last = mm(bank[4 + p][:, :], xgT[:, p, k], wu[:, k], start=(k == 0), stop=(k == KT - 1))
                last.then_inc(m.u_full, 1)

            def down(m, t, h, p, wait=True):
                wd = EW[p][:, 2].rearrange("p (k c) -> p k c", k=4)
                eng.wait_ge(m.t_took, t + 1)
                eng.wait_ge(m.wd[p], h * 16 + 16)
                for half in range(2):
                    if wait:
                        eng.wait_ge(m.d_took, t * 2 - 1 + half)
                    for k in range(4):
                        last = mm(bank[6 + half][:, :], actT[:, p, k], wd[:, k, 512 * half:512 * half + 512],
                                  start=(k == 0), stop=(k == 3))
                    last.then_inc(m.d_full, 1)

            def turn_act(m, t, h, p):
                eng.wait_ge(m.u_took, t + 1)
                for k in range(4):
                    last = nc.tensor.transpose(bank[p][:, k * P:(k + 1) * P], act[:, p, k * P:(k + 1) * P], ident)
                last.then_inc(m.t_full, 1)

            def experts(m, n):
                turn_rows(m, 0, 0, 0)
                gate(m, 0, 0, 0, wait=False)
                turn_rows(m, 1, 0, 1)
                up(m, 0, 0, 0, wait=False)
                turn_act(m, 0, 0, 0)
                gate(m, 1, 0, 1, wait=False)
                turn_rows(m, 2, 1, 0)
                up(m, 1, 0, 1, wait=False)
                down(m, 0, 0, 0, wait=False)
                turn_act(m, 1, 0, 1)
                with eng.Fori(1, n // 2 - 1) as it:
                    t = it * 2
                    gate(m, t, it, 0)
                    turn_rows(m, t + 1, it, 1)
                    up(m, t, it, 0)
                    down(m, t - 1, it - 1, 1)
                    turn_act(m, t, it, 0)
                    gate(m, t + 1, it, 1)
                    turn_rows(m, t + 2, it + 1, 0)
                    up(m, t + 1, it, 1)
                    down(m, t, it, 0)
                    turn_act(m, t + 1, it, 1)
                t, h = n - 2, n // 2 - 1
                gate(m, t, h, 0)
                turn_rows(m, t + 1, h, 1)
                up(m, t, h, 0)
                down(m, t - 1, h - 1, 1)
                turn_act(m, t, h, 0)
                gate(m, t + 1, h, 1)
                up(m, t + 1, h, 1)
                down(m, t, h, 0)
                turn_act(m, t + 1, h, 1)
                down(m, t + 1, h, 1)
                eng.wait_ge(m.d_took, 2 * n)
                eng.wait_ge(m.t_took, n)

            eng.wait_ge(a_took, ja["ht", 2, 1] + 1)
            eng.wait_ge(v_took, jv["tab"] + 1)
            experts(main, E)
            eng.wait_ge(tab_ready, 1)
            crowded = eng.value_load(most[0:1, 0:1], min_val=0, max_val=T)
            with eng.If(crowded > P):
                table(bank[4], 2 * E, o_oh_ready, o_oh_used, o_tab)
                eng.wait_ge(o_tab_took, 1)
                experts(over, 2 * E)
                eng.wait_ge(wp_again, 80)
            for ft in range(KT):
                ps = open_v("yt", ft)
                eng.wait_ge(acc_ready, 3)
                for i, (t0, n) in enumerate(TOK):
                    last = nc.tensor.transpose(ps[:, t0:t0 + n], acc[0:n, i, ft * P:(ft + 1) * P], ident[0:n, 0:n])
                last.then_inc(v_full, 1)
            norm(2)

            eng.wait_ge(ld_pp, 80)
            for c in range(2):
                ps = open_a("pT", c)
                for i, (t0, n) in enumerate(TOK):
                    last = nc.tensor.transpose(ps[:, t0:t0 + n], ptok[0:n, i, c * P:(c + 1) * P], ident[0:n, 0:n])
                last.then_inc(a_full, 1)
            eng.wait_ge(norm_done, 3 * KT)
            for c in range(KT):
                w = WP[:, c // 4].rearrange("p (k c) -> p k c", k=KT)
                ps = open_a("pg", c)
                for k in range(KT):
                    last = mm(ps[:, 0:T], w[:, k, (c % 4) * P:(c % 4 + 1) * P], hT[:, k], start=(k == 0), stop=(k == KT - 1))
                last.then_inc(a_full, 1)
                ps = open_v("pp", c)
                eng.wait_ge(a_took, ja["pT", 1] + 1)
                for k in range(2):
                    last = mm(ps[:, 0:T], wpp[:, k, c * P:(c + 1) * P], pT[:, k], start=(k == 0), stop=(k == 1))
                last.then_inc(v_full, 1)
            norm(3)
            eng.wait_ge(norm_done, 4 * KT)
            for i, (t0, n) in enumerate(TOK):
                for half in range(2):
                    ps = open_a("out", i, half)
                    for j in range(4):
                        last = nc.tensor.transpose(ps[0:n, j * P:(j + 1) * P], hT[:, 4 * half + j, t0:t0 + n], ident)
                    last.then_inc(a_full, 1)

        @block.scalar
        def _(eng):
            activation = nc.scalar.activation
            def full(*name):
                n = ja[name]
                eng.wait_ge(a_full, n + 1)
                return bank[n % 4]

            def norm(k):
                eng.wait_ge(norm_in[k][0], norm_in[k][1])
                activation(sq[:, :, :], xT[:, :, :], ACT.Square).then_inc(sq_done, 1)
                eng.wait_ge(v_took, jv["norm", k] + 1)
                activation(rstd[:, 1], rstd[:, 0], ACT.Sqrt).then_inc(sd_done, 1)

            norm_in = {0: (a_took, ja["xT", KT - 1] + 1), 1: (v_took, jv["mix", KT - 1] + 1),
                       2: (v_took, jv["yt", KT - 1] + 1), 3: (v_took, jv["pp", KT - 1] + 1)}
            for ft in range(KT):
                activation(xT[:, ft], full("xT", ft)[:, 0:T], ACT.Copy).then_inc(a_took, 1)
            norm(0)
            eng.wait_ge(lb_in, 2)
            activation(lbt, lbt, ACT.Exp).then_inc(lb_exp, 1)
            eng.wait_ge(ld_s, 48)
            activation(aneg, alog, ACT.Exp).then_inc(lb_exp, 1)
            for n in range(12):
                activation(PR[:, n], full("proj", n)[:, 0:T], ACT.Copy).then_inc(a_took, 1)
            eng.wait_ge(sp, 1)
            activation(dt2, dt1, ACT.Exp, scale=-1.0).then_inc(sp, 1)
            eng.wait_ge(sp, 3)
            activation(dt4, dt3, ACT.Ln).then_inc(sp, 1)
            eng.wait_ge(dt_ready, 1)
            activation(ea[0:NS], av[0:NS, 2], ACT.Exp).then_inc(ea_ready, 1)
            with eng.Fori(0, 4) as it:
                for j in range(8):
                    n = it * 8 + (12 + j)
                    eng.wait_ge(a_full, n + (PROJ0 + 1))
                    activation(PR[:, ds(n, 1)].rearrange("p a t -> p (a t)"), bank[(PROJ0 + 12 + j) % 4][:, 0:T],
                               ACT.Copy).then_inc(a_took, 1)
                for j in range(3):
                    eng.wait_ge(conv_done, it * 3 + (j + 1))
                    c = CV[:, ds(it * 3 + j, 1)].rearrange("p a t -> p (a t)")
                    activation(c, c, ACT.Silu).then_inc(silu_done, 1)
            for n in range(44, NPROJ):
                activation(PR[:, n], full("proj", n)[:, 0:T], ACT.Copy).then_inc(a_took, 1)
            activation(btok[:, :, :].rearrange("p a b -> p (a b)"), full("btok")[:, :], ACT.Copy).then_inc(a_took, 1)
            activation(wdec[:, :, :].rearrange("p a b -> p (a b)"), full("w")[:, 0:2 * H], ACT.Exp).then_inc(a_took, 1)
            for i in range(3):
                activation(tail[0:11, i * 512:(i + 1) * 512], full("tail", i)[0:11, :], ACT.Copy).then_inc(a_took, 1)
            for h in range(H):
                if h >= 4:
                    eng.wait_ge(v_full, jv["y", (h - 4) // 2] + 1)
                activation(EM[:, h % 4], full("diff", h)[:, 0:384], ACT.Exp).then_inc(a_took, 1)
            for i in range(2):
                activation(stage[:, 4 * i:4 * i + 4].rearrange("p a b -> p (a b)"), full("st", i)[:, :],
                           ACT.Copy).then_inc(a_took, 1)
            for tt in range(2):
                for half in range(2):
                    activation(vtok[:, tt, 512 * half:512 * half + 512], full("vtok", tt, half)[:, :],
                               ACT.Copy).then_inc(a_took, 1)
            for half in range(2):
                activation(vss[:, 512 * half:512 * half + 512], full("vs", half)[0:NS, :], ACT.Copy).then_inc(a_took, 1)
            eng.wait_ge(v_full, jv["dts"] + 1)
            fr = PR[:, P_F:P_F + HH]
            activation(KK[:, :, :], fr, ACT.Sigmoid, scale=-1.0).then_inc(hg_sig, 1)
            activation(fr, fr, ACT.Sigmoid).then_inc(hg_sig, 1)
            eng.wait_ge(xds_ready, 1)
            for b in range(NS):
                eng.wait_ge(bcb_in[b % 2], 16 * (b // 2 + 1))
                for f in range(KT):
                    u = b * KT + f
                    if u >= 2:
                        eng.wait_ge(u1_used, u - 1)
                    activation(U1[:, u % 2], BCb[:, b % 2, (f // 4) * N:(f // 4 + 1) * N], ACT.Copy,
                               scale=xds[:, b, f:f + 1]).then_inc(u1_ready, 1)

            def hg_head(h):
                hl = h % 2
                activation(PR[:, P_F + h, 0:NP_], full("o", h)[:, 0:NP_], ACT.Copy).then_inc(a_took, 1)
                activation(klt[:, hl].rearrange("p a b -> p (a b)"), full("klt", h)[:, 0:NP_], ACT.Copy).then_inc(a_took, 1)
                activation(stage_h[:, h], full("sth", h)[:, 0:DV], ACT.Copy).then_inc(a_took, 1)

            eng.wait_ge(hg_fk, 2 * HH)
            for h in range(HH):
                hg_head(h)
            for b in range(NS):
                eng.wait_ge(vb_in[b % 2], 16 * (b // 2 + 1))
                for h in range(HH):
                    u = b * HH + h
                    if u >= 2:
                        eng.wait_ge(s2_new, u - 1)
                    activation(U2[:, u % 2], vb[:, b % 2, h * DV:(h + 1) * DV], ACT.Copy,
                               scale=KK[:, h, NP_ + b:NP_ + b + 1]).then_inc(u2_ready, 1)
            zg = [PR[:, P_Z:P_Z + 8], PR[:, P_G:P_G + 8]]
            for z in zg:
                activation(z, z, ACT.Silu).then_inc(gate_silu, 1)
            eng.wait_ge(y_raw, 1)
            activation(sq16, PR[:, 0:8], ACT.Square).then_inc(sq_m, 1)
            eng.wait_ge(v_took, jv["yn", 1] + 1)
            activation(ms8[:, 2:4], ms8[:, 0:2], ACT.Sqrt).then_inc(sd_m, 1)
            eng.wait_ge(v_took, jv["os"] + 1)
            activation(sq16, PR[:, P_F:P_F + 8], ACT.Square).then_inc(sq_m, 1)
            eng.wait_ge(v_took, jv["on", HH - 1] + 1)
            activation(ms8[:, :], ms8[:, :], ACT.Sqrt).then_inc(sd_m, 1)
            norm(1)
            def turned_rows(m, t, p):
                for half in range(2):
                    eng.wait_ge(m.x_full, t * 2 + (half + 1))
                    activation(xgT[:, p, 4 * half:4 * half + 4].rearrange("p k c -> p (k c)"), bank[2 + half][:, :],
                               ACT.Copy).then_inc(m.x_took, 1)

            def silu(m, t, p, wait=True):
                eng.wait_ge(m.g_full, t + 1)
                if wait:
                    eng.wait_ge(m.u_took, t - 1)
                activation(sil[:, p], bank[p][:, :], ACT.Silu).then_inc(m.g_took, 1)

            def turned_act(m, t, p):
                eng.wait_ge(m.t_full, t + 1)
                activation(actT[:, p].rearrange("p k c -> p (k c)"), bank[p][:, :], ACT.Copy).then_inc(m.t_took, 1)

            def experts(m, n):
                turned_rows(m, 0, 0)
                for t in range(2):
                    silu(m, t, t, wait=False)
                    turned_rows(m, t + 1, 1 - t)
                    turned_act(m, t, t)
                with eng.Fori(1, n // 2 - 1) as it:
                    for p in range(2):
                        t = it * 2 + p
                        silu(m, t, p)
                        turned_rows(m, t + 1, 1 - p)
                        turned_act(m, t, p)
                silu(m, n - 2, 0)
                turned_rows(m, n - 1, 1)
                turned_act(m, n - 2, 0)
                silu(m, n - 1, 1)
                turned_act(m, n - 1, 1)

            for i, (t0, n) in enumerate(TOK):
                for half in range(2):
                    activation(htok[0:n, i, 512 * half:512 * half + 512], full("ht", i, half)[0:n, :],
                               ACT.Copy).then_inc(a_took, 1)
                eng.wait_ge(a_took, ja["ht", i, 1] + 1)
                eng.dma_start(h_rows[t0:t0 + n], htok[0:n, i]).then_inc(hrow_out, 16)
            eng.wait_ge(r_in, 1)
            activation(rs[:, 1], rs[:, 0], ACT.Exp).then_inc(r_exp, 1)
            eng.wait_ge(r_in, 2)
            activation(rs[:, 9], rs[:, 8], ACT.Exp).then_inc(r_exp, 1)
            experts(main, E)
            eng.wait_ge(tab_ready, 1)
            crowded = eng.value_load(most[0:1, 0:1], min_val=0, max_val=T)
            with eng.If(crowded > P):
                experts(over, 2 * E)
            eng.wait_ge(hrow_out, 48)
            norm(2)
            for c in range(2):
                activation(pT[:, c], full("pT", c)[:, 0:T], ACT.Copy).then_inc(a_took, 1)
            for c in range(KT):
                if c >= 2:
                    eng.wait_ge(v_took, jv["pp", c - 2] + 1)
                activation(gs[:, c % 2], full("pg", c)[:, 0:T], ACT.Sigmoid).then_inc(a_took, 1)
            norm(3)
            for i, (t0, n) in enumerate(TOK):
                for half in range(2):
                    activation(ostage[0:n, i, 512 * half:512 * half + 512], full("out", i, half)[0:n, :],
                               ACT.Copy).then_inc(a_took, 1)

        @block.vector
        def _(eng):
            own = {dve: 0, o_dve: 0}

            def link(ins_, chain=dve):
                own[chain] += 1
                ins_.then_inc(chain, 1)
                eng.wait_ge(chain, own[chain])

            def full(*name):
                n = jv[name]
                eng.wait_ge(v_full, n + 1)
                return bank[4 + n % 4]

            def took(*name):
                eng.wait_ge(v_took, jv[name] + 1)

            def tt(out, a, b, op=ALU.mult):
                return nc.vector.tensor_tensor(out, a, b, op)

            def ts(out, a, s1, op0, s2=None, op1=None):
                if op1 is None:
                    return nc.vector.tensor_scalar(out, a, s1, None, op0)
                return nc.vector.tensor_scalar(out, a, s1, s2, op0, op1)

            def stt(out, a, s, b, op0, op1):
                return nc.vector.scalar_tensor_tensor(out, a, s, b, op0, op1)

            def col(r):
                return prm[:, r:r + 1]

            def spread(x, n):
                rows = x.shape[0]
                return x.rearrange("p (h o) -> p h o", o=1).to_broadcast([rows, x.shape[1], n])

            def norm(k, row):
                ps = full("norm", k)
                ts(rstd[:, 0], ps[:, 0:T], 1.0 / D, ALU.mult, EPS, ALU.add).then_inc(v_took, 1)
                eng.wait_ge(sd_done, k + 1)
                link(nc.vector.reciprocal(rstd[:, 0], rstd[:, 1]))
                for ft in range(KT):
                    stt(hT[:, ft], xT[:, ft], col(row + ft), rstd[:, 0], ALU.mult, ALU.mult).then_inc(norm_done, 1)

            eng.wait_ge(ld_p, 16 * 11)
            nc.vector.tensor_copy(drow[0:KT].rearrange("f (h p) -> f h p", h=2), spread(dpair[0:KT], HD)
                                  ).then_inc(drow_ready, 1)
            nc.vector.tensor_copy(prm[:, 0:R_N], full("prm")[:, 0:R_N]).then_inc(v_took, 1)
            nc.vector.tensor_copy(prm[:, R_N:R_N + KT], full("prmD")[:, 0:KT]).then_inc(v_took, 1)
            nc.vector.tensor_copy(convu.rearrange("p c b k -> p (c b k)"), full("cst")[:, 0:288]).then_inc(v_took, 1)
            took("cst")
            l0, l1 = prm[:, R_LB:R_LB + HH], prm[:, R_LB + HH:R_LB + 2 * HH]
            link(tt(lbe[:, 0], l0, l1, ALU.max))
            tt(lbt[:, 0], l0, lbe[:, 0], ALU.subtract).then_inc(lb_in, 1)
            tt(lbt[:, 1], l1, lbe[:, 0], ALU.subtract).then_inc(lb_in, 1)
            norm(0, R_MIX)
            eng.wait_ge(lb_exp, 2)
            link(tt(lbe[:, 1], lbt[:, 0], lbt[:, 1], ALU.add))
            link(nc.vector.reciprocal(lbe[:, 2], lbe[:, 1]))
            tt(lb, lbt[:, 0], lbe[:, 2])
            link(tt(oml, lbt[:, 1], lbe[:, 2]))
            link(nc.vector.memset(dtr, 0.0))
            ps = full("dt")
            link(tt(dtr[:, 0:2], ps[:, 0:2 * H].rearrange("p (t h) -> p t h", h=H),
                    dtb.rearrange("p (o h) -> p o h", o=1).to_broadcast([P, 2, H]), ALU.add))
            tt(dtr[0:NS, 2], ps[0:NS, 2 * H:3 * H], dtb[0:NS], ALU.add).then_inc(v_took, 1)
            took("dt")
            link(ts(dt2, dtr, -1.0, ALU.mult))
            tt(dt1, dt2, dtr, ALU.max).then_inc(sp, 1)
            eng.wait_ge(sp, 2)
            ts(dt3, dt2, 1.0, ALU.add).then_inc(sp, 1)
            eng.wait_ge(sp, 4)
            link(ts(dt1, dt3, 1.0, ALU.is_equal))
            link(ts(dt3, dt3, -1.0, ALU.add))
            link(tt(dt3, dt3, dt1, ALU.add))
            link(tt(dt4, dt4, dt1, ALU.add))
            link(nc.vector.reciprocal(dtv, dt3))
            link(tt(dt4, dt4, dt2))
            link(tt(dt4, dt4, dtv))
            link(stt(dtv, dtr, 0.0, dt4, ALU.max, ALU.add))
            stt(av, dtv, -1.0, aneg.rearrange("p (o h) -> p o h", o=1).to_broadcast([P, 3, H]),
                ALU.mult, ALU.mult).then_inc(dt_ready, 1)
            eng.wait_ge(dt_ready, 1)
            for c in range(CT):
                eng.wait_ge(a_took, ja["proj", c] + 1)
                raw, out = PR[:, c], CV[:, c]
                link(ts(out, raw, col(R_CW + 3 * CT + c), ALU.mult, col(R_CB + c), ALU.add))
                for k in range(3):
                    s = 3 - k
                    link(stt(out[:, s:NP_], raw[:, 0:NP_ - s], col(R_CW + k * CT + c), out[:, s:NP_],
                             ALU.mult, ALU.add))
                old = convu[:, c].rearrange("p b k -> p k b")
                for k in range(3):
                    last = stt(out[:, NP_:T], old[:, k], col(R_CW + k * CT + c), out[:, NP_:T], ALU.mult, ALU.add)
                    if k < 2:
                        link(last)
                last.then_inc(conv_done, 1)

            after = K[:, K_AFTER:K_AFTER + P].rearrange("p (o s) -> p o s", o=1).to_broadcast([P, H, P])
            for i in range(2):
                tt(AM[:, i], after, spread(av[:, i], P)).then_inc(am_ready, 1)
            nc.vector.tensor_copy(dtx.rearrange("p (h q) -> p h q", q=HD), spread(dtv[0:NS, 2], HD)).then_inc(dtx_ready, 1)
            eng.wait_ge(ea_ready, 1)
            nc.vector.tensor_copy(eax.rearrange("p (h q) -> p h q", q=HD), spread(ea[0:NS], HD)).then_inc(dtx_ready, 1)
            for i in range(2):
                for half in range(2):
                    tt(xdt[:, i, 512 * half:512 * half + 512].rearrange("p (h q) -> p h q", q=HD),
                       full("xs", i, half)[:, :].rearrange("p (h q) -> p h q", q=HD),
                       spread(dtv[:, i, 8 * half:8 * half + 8], HD)).then_inc(v_took, 1)
            nc.vector.tensor_copy(bcs, full("bcs")[0:NS, :]).then_inc(v_took, 1)
            for g in range(G):
                tt(CBm[:, g], full("cb", g)[:, 0:384], K[:, K_CAUSAL:K_CAUSAL + 384]).then_inc(v_took, 1)
            ps = full("dts")
            link(nc.vector.tensor_copy(DX, ps[:, 0:64].rearrange("p (f b) -> p b f", f=KT)))
            nc.vector.tensor_copy(EX, ps[:, 64:128].rearrange("p (f b) -> p b f", f=KT)).then_inc(v_took, 1)
            took("dts")
            tt(xds, CV[:, 0:KT, NP_:T].rearrange("p f b -> p b f"), DX).then_inc(xds_ready, 1)
            eng.wait_ge(a_took, ja["w"] + 1)
            for i in range(2):
                tt(xw[:, i].rearrange("p (h q) -> p h q", q=HD), xdt[:, i].rearrange("p (h q) -> p h q", q=HD),
                   spread(wdec[:, i], HD)).then_inc(xw_ready, 1)

            def y_take(f):
                stt(PR[:, f, 0:NP_], CV[:, f, 0:NP_], col(R_N + f), full("y", f)[:, 0:NP_], ALU.mult, ALU.add
                    ).then_inc(v_took, 1)

            for h in range(H):
                eng.wait_ge(a_took, ja["diff", h] + 1)
                tt(EM[:, h % 4], EM[:, h % 4], CBm[:, h // 8]).then_inc(m_ready, 1)
                if h % 2 and h >= 3:
                    y_take(h // 2 - 1)
            y_take(KT - 1)
            for b in range(NS):
                eng.wait_ge(s1_in[b % 2], 16 * (b // 2 + 1))
                eng.wait_ge(bcb_in[b % 2], 16 * (b // 2 + 1))
                for f in range(KT):
                    u = b * KT + f
                    eng.wait_ge(u1_ready, u + 1)
                    st = S1[:, b % 2, f]
                    stt(st, st, EX[:, b, f:f + 1], U1[:, u % 2], ALU.mult, ALU.add).then_inc(u1_used, 1)
                    eng.wait_ge(u1_used, u + 1)
                    if u:
                        eng.wait_ge(s1_new, u)
                    nc.vector.tensor_tensor_reduce(
                        junk, st, BCb[:, b % 2, (G + f // 4) * N:(G + f // 4 + 1) * N], 1.0, 0.0,
                        ALU.mult, ALU.add, yss[:, b, f:f + 1]).then_inc(s1_new, 1)
            eng.wait_ge(s1_new, NS * KT)
            link(tt(DX, CV[:, 0:KT, NP_:T].rearrange("p f b -> p b f"),
                    prm[:, R_N:R_N + KT].rearrange("p (o f) -> p o f", o=1).to_broadcast([P, NS, KT])))
            link(tt(PR[:, 0:KT, NP_:T].rearrange("p f b -> p b f"), yss, DX, ALU.add))

            eng.wait_ge(hg_sig, 2)
            for h in range(HH):
                ts(KK[:, h], KK[:, h], oml[:, h:h + 1], ALU.mult).then_inc(hg_fk, 1)
                ts(PR[:, P_F + h], PR[:, P_F + h], oml[:, h:h + 1], ALU.mult, lb[:, h:h + 1], ALU.add).then_inc(hg_fk, 1)
            eng.wait_ge(hg_fk, 2 * HH)
            eng.wait_ge(a_full, ja["st", 1] + 1)

            def halves(x, s):
                y = x.rearrange("p h (n w s) -> p h n w s", w=2, s=s)
                return y[:, :, :, 0], y[:, :, :, 1]

            def last_of(x, s):
                return x[:, :, :, s - 1:s].to_broadcast([P, 2, NP_ // (2 * s), s])

            def tree(pair):
                h = slice(2 * pair, 2 * pair + 2)
                f2 = PR[:, P_F + 2 * pair:P_F + 2 * pair + 2, 0:NP_]
                q2 = PR[:, P_Q + 2 * pair:P_Q + 2 * pair + 2, 0:NP_]
                k2 = KK[:, h, 0:NP_]
                if pair:
                    eng.wait_ge(v_full, jv["off", 2 * pair - 1] + 1)
                    eng.wait_ge(a_full, ja["klt", 2 * pair - 1] + 1)
                link(nc.vector.tensor_copy(R, f2))
                link(nc.vector.memset(L, 1.0))
                for a in range(8):
                    s = 2 ** a
                    ql, qr = halves(q2, s)
                    kl, kr = halves(k2, s)
                    Rl, Rr = halves(R, s)
                    Ll, Lr = halves(L, s)
                    ol, orr = halves(QK[:, :, a], s)
                    tt(ol, kl, Ll).then_inc(qk_ready, 1)
                    tt(orr, qr, Rr).then_inc(qk_ready, 1)
                    link(tt(Ll, Ll, last_of(Rr, s)))
                    if a < 7:
                        link(tt(Rr, Rr, last_of(Rl, s)))
                tt(KL, k2, L).then_inc(kl_ready, 1)

            for h in range(HH):
                if h % 2 == 0:
                    tree(h // 2)
                if h >= 2:
                    eng.wait_ge(a_full, ja["o", h - 2] + 1)
                for i in range(2):
                    for b in range(2):
                        if b == 0 and (h or i):
                            eng.wait_ge(at_ready, 2 * h + i)
                        tt(LVt[:, i, 4 * b:4 * b + 4].rearrange("p a b -> p (a b)"), full("lv", h, i, b)[:, :],
                           K[:, K_LM + 512 * b:K_LM + 512 * b + 512]).then_inc(v_took, 1)
                    took("lv", h, i, 1)
                    nc.vector.tensor_reduce(AT[:, h % 2, 256 * i:256 * i + P], LVt[:, i].rearrange("p a c -> p c a"),
                                            AX.X, ALU.add).then_inc(at_ready, 1)
                nc.vector.tensor_copy(AT[:, h % 2, P:2 * P], full("off", h)[:, 0:P]).then_inc(v_took, 1)
            for b in range(NS):
                eng.wait_ge(s2_in[b % 2], 16 * (b // 2 + 1))
                for h in range(HH):
                    u = b * HH + h
                    eng.wait_ge(u2_ready, u + 1)
                    st = S2[:, b % 2, h]
                    stt(st, st, PR[:, P_F + h, NP_ + b:NP_ + b + 1], U2[:, u % 2], ALU.mult, ALU.add).then_inc(s2_new, 1)
            ps = full("os")
            nc.vector.tensor_copy(PR[:, P_F:P_F + HH, NP_:T], ps[:, 0:64].rearrange("p (h b) -> p h b", h=HH)
                                  ).then_inc(v_took, 1)

            y = PR[:, 0:KT]
            o = PR[:, P_F:P_F + HH]
            eng.wait_ge(gate_silu, 2)
            tt(y, y, PR[:, P_Z:P_Z + KT]).then_inc(y_raw, 1)
            for g in range(G):
                ts(ms8[:, g], full("yn", g)[:, 0:T], 1.0 / (SD // G), ALU.mult, EPS, ALU.add).then_inc(v_took, 1)
            eng.wait_ge(sd_m, 1)
            link(nc.vector.reciprocal(ms8[:, 2:4], ms8[:, 2:4]))
            for f in range(KT):
                stt(y[:, f], y[:, f], col(R_SN + f), ms8[:, 2 + f // 4], ALU.mult, ALU.mult).then_inc(mixed, 1)
            eng.wait_ge(mixed, KT)
            for h in range(HH):
                ts(ms8[:, h], full("on", h)[:, 0:T], 1.0 / DV, ALU.mult, EPS, ALU.add).then_inc(v_took, 1)
            eng.wait_ge(sd_m, 2)
            link(nc.vector.reciprocal(ms8[:, :], ms8[:, :]))
            link(tt(ms8[:, :], ms8[:, :], PR[:, P_G:P_G + HH]))
            for h in range(HH):
                stt(o[:, h], o[:, h], col(R_HN + h), ms8[:, h], ALU.mult, ALU.mult).then_inc(mixed, 1)
            for c in range(KT):
                tt(xT[:, c], xT[:, c], full("mix", c)[:, 0:T], ALU.add).then_inc(v_took, 1)
            norm(1, R_FFN)

            def bc(x, n=4):
                return x.rearrange("p (t o) -> p t o", o=1).to_broadcast([P, 3, n])

            def red(out, x, op):
                link(nc.vector.tensor_reduce(out, x, AX.X, op))

            def first_max(out, x, tmp, m):
                red(m, x, ALU.max)
                link(tt(tmp, x, bc(m), ALU.is_equal))
                link(tt(tmp, tmp, w4))
                red(m, tmp, ALU.max)
                link(tt(out, tmp, bc(m), ALU.is_equal))

            w4 = K[:, K_W4:K_W4 + 4].rearrange("p (o e) -> p o e", o=1).to_broadcast([P, 3, 4])
            link(nc.vector.memset(rt[:, :, :], 0.0))
            eng.wait_ge(mixers_done, 1)
            for i in range(3):
                link(nc.vector.memset(Mt[:, i], 0.0))
            ps = full("rt")
            link(nc.vector.tensor_copy(rt[:, 0:2], ps[:, 0:40].rearrange("p (t c) -> p t c", c=20)))
            nc.vector.tensor_copy(rt[0:NS, 2], ps[0:NS, 40:60]).then_inc(v_took, 1)
            took("rt")
            lg = rt[:, :, 0:4]
            red(r1[:, 0], lg, ALU.max)
            tt(rs[:, 0], lg, bc(r1[:, 0]), ALU.subtract).then_inc(r_in, 1)
            link(tt(rs[:, 3], lg, rb[:, 0:4].rearrange("p (o e) -> p o e", o=1).to_broadcast([P, 3, 4]), ALU.add))
            ohg = rs[:, 5]
            first_max(ohg, rs[:, 3], rs[:, 4], r1[:, 3])
            eng.wait_ge(r_exp, 1)
            red(r1[:, 1], rs[:, 1], ALU.add)
            link(nc.vector.reciprocal(r1[:, 2], r1[:, 1]))
            link(tt(rs[:, 2], rs[:, 1], bc(r1[:, 2])))
            link(tt(rs[:, 6], rs[:, 2], ohg))
            red(r1[:, 5], rs[:, 6], ALU.add)
            g4 = gates[:, :, :].rearrange("p t (g e) -> p t g e", g=EG)
            ohb = ohg.rearrange("p t (g o) -> p t g o", o=1).to_broadcast([P, 3, EG, EPG])
            link(tt(g4, rt[:, :, 4:20].rearrange("p t (g e) -> p t g e", g=EG), ohb))
            red(rs[:, 7], g4.rearrange("p t g e -> p t e g"), ALU.add)
            link(tt(g4, rb[:, 4:20].rearrange("p (o g e) -> p o g e", o=1, g=EG).to_broadcast([P, 3, EG, EPG]), ohb))
            red(rs[:, 14], g4.rearrange("p t g e -> p t e g"), ALU.add)
            red(r1[:, 6], rs[:, 7], ALU.max)
            tt(rs[:, 8], rs[:, 7], bc(r1[:, 6]), ALU.subtract).then_inc(r_in, 1)
            link(tt(rs[:, 11], rs[:, 7], rs[:, 14], ALU.add))
            first_max(rs[:, 12], rs[:, 11], rs[:, 4], r1[:, 3])
            link(stt(rs[:, 13], rs[:, 12], -BIG, rs[:, 11], ALU.mult, ALU.add))
            first_max(rs[:, 15], rs[:, 13], rs[:, 4], r1[:, 3])
            link(tt(rs[:, 16], rs[:, 12], rs[:, 15], ALU.add))
            eng.wait_ge(r_exp, 2)
            red(r1[:, 7], rs[:, 9], ALU.add)
            link(nc.vector.reciprocal(r1[:, 0], r1[:, 7]))
            link(tt(rs[:, 10], rs[:, 9], bc(r1[:, 0])))
            link(tt(rs[:, 10], rs[:, 10], rs[:, 16]))
            red(r1[:, 1], rs[:, 10], ALU.add)
            link(nc.vector.reciprocal(r1[:, 2], r1[:, 1]))
            link(tt(r1[:, 2], r1[:, 2], r1[:, 5]))
            link(tt(rs[:, 10], rs[:, 10], bc(r1[:, 2])))
            link(tt(g4, ohb, rs[:, 10].rearrange("p t (o e) -> p t o e", o=1).to_broadcast([P, 3, EG, EPG])))
            chosen = rs[:, 16].rearrange("p t (o e) -> p t o e", o=1).to_broadcast([P, 3, EG, EPG])
            for i, (t0, n) in enumerate(TOK):
                tt(Mt[0:n, i].rearrange("p (g e) -> p g e", g=EG), ohb[0:n, i], chosen[0:n, i]).then_inc(mt_ready, 1)
            tokid = K[:, K_TOK:K_TOK + 3]
            nc.vector.tensor_copy(rv[:, :, :, 0], spread(tokid, E))
            link(nc.vector.tensor_copy(rv[:, :, :, 1], gates[:, :, :]))
            nc.vector.memset(rv[:, :, :, 3], 1.0)
            link(stt(rs[:, 17], rs[:, 15], float(T), bc(tokid), ALU.mult, ALU.add))
            link(nc.vector.tensor_copy(rv[:, :, :, 2].rearrange("p t (g e) -> p t g e", g=EG),
                                       rs[:, 17].rearrange("p t (o e) -> p t o e", o=1).to_broadcast([P, 3, EG, EPG])))
            ps = full("cnt")
            eng.wait_ge(mt_ready, 3)
            tt(slot1[:, :, :], ps[:, 0:3 * E].rearrange("p (t e) -> p t e", e=E), Mt[:, :, :])
            nc.vector.tensor_reduce(most[:, :], ps[:, 3 * E:4 * E], AX.X, ALU.max).then_inc(v_took, 1)
            took("cnt")

            def one_hots(turns, first, ready, used_):
                for t in range(turns):
                    c = (first + t) // E
                    if t >= 2:
                        eng.wait_ge(used_, t - 1)
                    tt(OH[:, t % 2], K[:, K_IOTA + P * c:K_IOTA + P * c + P].rearrange("p (o s) -> p o s", o=1)
                       .to_broadcast([P, 3, P]),
                       slot1[:, :, t % E:t % E + 1].to_broadcast([P, 3, P]), ALU.is_equal).then_inc(ready, 1)

            def tables(ps, turns, first):
                return nc.vector.tensor_copy(tabf[:, first:first + turns].rearrange("p t c -> p (t c)"),
                                             ps[:, 0:4 * turns])

            def row_numbers(turns, first, chain):
                f = tabf[:, first:first + turns]
                link(ts(f[:, :, 3], f[:, :, 3], -FAR, ALU.mult, FAR, ALU.add), chain)
                link(tt(row_of[:, 0, first:first + turns], f[:, :, 0], f[:, :, 3], ALU.add), chain)
                return tt(row_of[:, 1, first:first + turns], f[:, :, 2], f[:, :, 3], ALU.add)

            one_hots(E, 0, oh_ready, oh_used)
            tables(full("tab"), E, 0).then_inc(v_took, 1)
            took("tab")
            row_numbers(E, 0, dve).then_inc(tab_ready, 1)
            eng.wait_ge(tab_ready, 1)

            def mul(m, t, p, base):
                eng.wait_ge(m.u_full, t + 1)
                eng.wait_ge(m.g_took, t + 1)
                stt(act[:, p], sil[:, p], tabf[:, ds(t + base, 1), 1], bank[4 + p][:, :], ALU.mult, ALU.mult
                    ).then_inc(m.u_took, 1)

            def result(m, t, h, p, wait=True):
                for half in range(2):
                    eng.wait_ge(m.d_full, t * 2 + (1 + half))
                    if wait and not half:
                        eng.wait_ge(m.sent[p], h * 16)
                    nc.vector.tensor_copy(ys[:, p, 512 * half:512 * half + 512], bank[6 + half][:, :]).then_inc(m.d_took, 1)

            def experts(m, n, base):
                mul(m, 0, 0, base)
                mul(m, 1, 1, base)
                result(m, 0, 0, 0, wait=False)
                mul(m, 2, 0, base)
                result(m, 1, 0, 1, wait=False)
                mul(m, 3, 1, base)
                result(m, 2, 1, 0)
                with eng.Fori(2, n // 2) as it:
                    t = it * 2
                    mul(m, t, 0, base)
                    result(m, t - 1, it - 1, 1)
                    mul(m, t + 1, 1, base)
                    result(m, t, it, 0)
                result(m, n - 1, n // 2 - 1, 1)

            experts(main, E, 0)
            crowded = eng.value_load(most[0:1, 0:1], min_val=0, max_val=T)
            with eng.If(crowded > P):
                one_hots(2 * E, E, o_oh_ready, o_oh_used)
                eng.wait_ge(o_tab, 1)
                link(tables(bank[4], 2 * E, E), o_dve)
                row_numbers(2 * E, E, o_dve).then_inc(o_tab_took, 1)
                eng.wait_ge(o_tab_took, 1)
                for p in range(2):
                    eng.wait_ge(main.sent[p], 16 * (E // 2))
                experts(over, 2 * E, E)
            eng.wait_ge(pair_in, 64)
            for i, (t0, n) in enumerate(TOK):
                tt(acc[0:n, i], pairs[0:n, i, 0], pairs[0:n, i, 1], ALU.add).then_inc(acc_ready, 1)
            for ft in range(KT):
                tt(xT[:, ft], xT[:, ft], full("yt", ft)[:, 0:T], ALU.add).then_inc(v_took, 1)
            norm(2, R_PLE)

            for c in range(KT):
                ps = full("pp", c)
                eng.wait_ge(a_took, ja["pg", c] + 1)
                link(tt(gs[:, c % 2], gs[:, c % 2], ps[:, 0:T]))
                tt(xT[:, c], xT[:, c], gs[:, c % 2], ALU.add).then_inc(v_took, 1)
            norm(3, R_FIN)


_INS = ["x_prompt", "x_sample", "state_ssm", "state_conv", "state_hgrn", "p_prompt", "p_sample", "norm_mix_w",
        "w_in", "conv_w", "conv_b", "dt_bias", "a_log", "d_skip", "ssd_norm_w", "lb_logits", "hg_norm_w",
        "w_out", "norm_ffn_w", "w_router_group", "b_router_group", "w_router_expert", "b_router_expert",
        "w_exp_gate", "w_exp_up", "w_exp_down", "norm_ple_w", "w_ple_gate", "w_ple_proj", "final_norm_w"]
_OUTS = [(1, NP_, D), (NS, 1, D), (1, 1, H, HD, N), (1, 1, 3, CONV), (1, 1, HH, DK, DV),
         (1, NS, H, HD, N), (1, NS, 3, CONV), (1, NS, HH, DK, DV)]


def kernel(**inputs):
    import concourse.bacc as bacc
    from concourse.bass_utils import run_bass_kernel_spmd

    nc = bacc.Bacc("TRN2", target_bir_lowering=False, num_devices=1)
    arrays, ins = {}, {}
    for name in _INS:
        x = np.ascontiguousarray(inputs[name])
        arrays[f"in_{name}"] = x
        ins[name] = nc.dram_tensor(f"in_{name}", x.shape, mybir.dt.from_np(x.dtype), kind="ExternalInput").ap()
    arrays["constants"] = constants()
    consts = nc.dram_tensor("constants", (P, K_N), F32, kind="ExternalInput").ap()
    outs = [nc.dram_tensor(f"out_{i}", shape, F32, kind="ExternalOutput").ap() for i, shape in enumerate(_OUTS)]
    build(nc, ins, outs, consts)
    r = run_bass_kernel_spmd(nc, [arrays], core_ids=[0])
    return tuple(r.results[0][f"out_{i}"] for i in range(len(_OUTS)))
```

```python
from contextlib import ExitStack

import concourse.bass as bass
import numpy as np
from concourse import mybir

ALU = mybir.AluOpType
ACT = mybir.ActivationFunctionType
AX = mybir.AxisListType
F32 = mybir.dt.float32
BF16 = mybir.dt.bfloat16

P = 128
D = 1024
NP_, NS = 256, 8
T = NP_ + NS
KT = D // P
H, HD, N = 16, 64, 128
G = 2
SD = H * HD
CONV = SD + 2 * G * N
CT = CONV // P
HH, DK, DV = 8, 128, 128
E, EG, EPG, FF = 16, 4, 4, 512
TOP_K = 2
FAR = 1e6
PLE = 256
EPS = 1e-6
ARENA = 43400
TOK = [(0, 128), (128, 128), (256, 8)]
BIG = 1e30

C_Z, C_X, C_DT, C_Q = 0, SD, SD + CONV, SD + CONV + H
P_X, P_Q, P_F, P_V, P_Z, P_G = 0, 12, 20, 28, 36, 44
NPROJ = 52
Y_NORM_AT = 6
LEVELS = 7
TAB0 = 2
OH_SLOTS = 8
RV = 8
K_ID, K_CAUSAL, K_ONES, K_AFTER, K_LM, K_W4 = 0, 128, 256, 512, 640, 640 + 1024
K_IOTA = K_W4 + 4
K_TOK = K_IOTA + 384
K_EPS = K_TOK + 3
K_N = K_EPS + 1
R_CW, R_CB, R_SN, R_HN, R_MIX, R_FFN, R_PLE, R_FIN, R_LB = 0, 48, 60, 68, 76, 84, 92, 100, 108
R_N = 124

def constants():
    i = np.arange(P)
    row, col = i[:, None], i[None, :]
    c = np.zeros((P, K_N), np.float32)
    c[:, K_ID:K_ID + P] = row == col
    c[:, K_CAUSAL:K_CAUSAL + P] = row <= col
    c[:, K_ONES:K_ONES + P] = 1.0
    c[:, K_ONES + P:K_ONES + 2 * P] = row <= col
    c[:, K_AFTER:K_AFTER + P] = row > col
    for a in range(LEVELS):
        x = row ^ col
        c[:, K_LM + a * P:K_LM + (a + 1) * P] = (x >= 2 ** a) & (x < 2 ** (a + 1)) & (row < col)
    c[:, K_LM + LEVELS * P:K_LM + (LEVELS + 1) * P] = row == col
    c[:, K_W4:K_W4 + 4] = [4, 3, 2, 1]
    c[:, K_IOTA:K_IOTA + 3 * P] = np.arange(1, 3 * P + 1)
    c[:, K_TOK:K_TOK + 3] = row + P * np.arange(3)
    c[:, K_EPS] = EPS
    return c

class JobList:

    def __init__(self):
        self.at = {}

    def add(self, *name):
        self.at[name] = len(self.at)

    def __getitem__(self, name):
        return self.at[name if isinstance(name, tuple) else (name,)]

class ExpertSems:

    def __init__(self, sem, k):
        def pair(name):
            return [sem(f"{k}_{name}{i}") for i in range(2)]

        self.g_full, self.g_took = sem(f"{k}_g_full"), sem(f"{k}_g_took")
        self.u_full, self.u_took = sem(f"{k}_u_full"), sem(f"{k}_u_took")
        self.x_full, self.x_took = sem(f"{k}_x_full"), sem(f"{k}_x_took")
        self.t_full, self.t_took = sem(f"{k}_t_full"), sem(f"{k}_t_took")
        self.d_full, self.d_took = sem(f"{k}_d_full"), sem(f"{k}_d_took")
        self.wg, self.wu, self.wd = pair("wg"), pair("wu"), pair("wd")
        self.rows, self.sent = pair("rows"), pair("sent")

def make_jobs():
    a, v = JobList(), JobList()
    for ft in range(KT):
        a.add("xT", ft)
    a.add("norm", 0)
    v.add("prm")
    v.add("prmD")
    v.add("cst")
    for n in range(P_F - 4):
        a.add("proj", n)
    v.add("dt")
    v.add("bcs")
    for g in range(G):
        v.add("cb", g)
    v.add("dts")
    a.add("btok")
    a.add("w")
    for i in range(3):
        a.add("tail", i)
    for tt in range(2):
        for half in range(2):
            v.add("xs", tt, half)
    for n in range(P_F - 4, P_V + 8):
        a.add("proj", n)
    for f in range(KT):
        v.add("y", f)
    for h in range(H):
        a.add("diff", h)
    for i in range(2):
        a.add("st", i)
    for tt in range(2):
        for half in range(2):
            a.add("vtok", tt, half)
    for half in range(2):
        a.add("vs", half)
    for h in range(HH):
        for tt in range(2):
            for b in range(2):
                v.add("lv", h, tt, b)
        v.add("off", h)
        if h:
            v.add("os", h - 1)
        if h == Y_NORM_AT:
            for g in range(G):
                a.add("yn", g)
        a.add("proj", P_Z + 2 * h)
        if h:
            for name in ("klt", "o", "sth"):
                a.add(name, h - 1)
        a.add("proj", P_Z + 2 * h + 1)
    for name in ("klt", "o", "sth"):
        a.add(name, HH - 1)
    v.add("os", HH - 1)
    for h in range(HH):
        a.add("on", h)
    for c in range(KT):
        v.add("mix", c)
    a.add("norm", 1)
    v.add("rt")
    for tt in range(3):
        for half in range(2):
            a.add("ht", tt, half)
    v.add("cnt")
    for i in range(2):
        v.add("tab", i)
    for i in range(2):
        a.add("pT", i)
    for c in range(KT):
        a.add("pp", c)
    for ft in range(KT):
        v.add("yt", ft)
    a.add("norm", 2)
    for c in range(KT):
        a.add("pg", c)
    a.add("norm", 3)
    for tt in range(3):
        for half in range(2):
            a.add("out", tt, half)
    return a, v


def build(nc, ins, outs, consts):
    ja, jv = make_jobs()
    ds = bass.ds

    def dram(name, shape):
        return nc.dram_tensor(name, shape, F32, kind="Internal").ap()

    bc_rows = dram("bc_rows", (NS, 2 * G * N))
    v_rows = dram("v_rows", (NS, HH * DV))

    h_rows = dram("h_rows", (T, D))
    pair_rows = dram("pair_rows", (TOP_K * T, D))

    w_in = ins["w_in"][0].rearrange("(k p) c -> p k c", p=P)
    w_out = ins["w_out"][0].rearrange("(k p) c -> p k c", p=P)
    w_pg = ins["w_ple_gate"][0].rearrange("(k p) c -> p k c", p=P)
    w_pp = ins["w_ple_proj"][0].rearrange("(k p) c -> p k c", p=P)

    ctx = ExitStack()
    with ctx:
        def sb(name, shape):
            return ctx.enter_context(nc.sbuf_tensor(name, shape, F32))

        def sem(name):
            return ctx.enter_context(nc.semaphore(name))

        K = sb("K", [P, K_N])
        ident = K[:, K_ID:K_ID + P]
        ones = K[:, K_ONES:K_ONES + P]
        eps = K[:, K_EPS:K_EPS + 1]
        xT = sb("xT", [P, KT, T])
        hT = sb("hT", [P, KT, T])
        sq = sb("sq", [P, KT, T])
        prm = sb("prm", [P, R_N + 8])
        rstd = sb("rstd", [P, 2, T])
        arena = sb("arena", [P, ARENA])
        used = [0]

        def carve(*shape, at=None):
            if at is not None:
                used[0] = at
            n = int(np.prod(shape))
            v = arena[:, used[0]:used[0] + n]
            used[0] += n
            assert used[0] <= ARENA, used[0]
            if len(shape) == 1:
                return v
            names = "abcd"[:len(shape)]
            return v.rearrange(f"p ({' '.join(names)}) -> p {' '.join(names)}",
                               **{c: s for c, s in zip(names, shape)})

        PR = carve(NPROJ, T)
        W = carve(2, 4096)
        smalls = carve(900)
        early = used[0]
        CV = carve(CT, T)
        vtok = carve(2, D)
        temp = used[0]
        slot0 = early + 2 * KT * T
        xdt = carve(2, D)
        xw = carve(2, D)
        btok = carve(2, G * N)
        CBm = carve(G, 384)
        EM = carve(4, 384)
        stage = carve(KT, P)
        decode = used[0]
        bc01 = carve(2, 2 * G * N)
        U1 = carve(2, KT, N)
        S1 = carve(4, KT, N)
        assert used[0] <= ARENA
        xtok = carve(3, D, at=temp)
        prow = carve(P)
        drow = carve(P)
        crow = carve(CONV)
        convu = carve(CT, NS, 3)
        assert used[0] <= decode
        AM = carve(2, H, P, at=P_Z * T)
        bc23 = carve(2, 2 * G * N, at=(P_V + 4) * T)
        BCb = [bc01[:, 0], bc01[:, 1], bc23[:, 0], bc23[:, 1]]
        rows_a = vtok[:, :, :].rearrange("p a b -> p (a b)")
        tail, bcs = rows_a[:, 0:CONV], rows_a[0:NS, CONV:CONV + 2 * G * N]
        QK = [carve(2, 8, NP_, at=decode)]
        R = carve(2, NP_)
        L = carve(2, NP_)
        S2 = carve(2, HH, DV, at=decode + 5120)
        assert used[0] <= ARENA
        QK.append(carve(2, 8, NP_, at=temp))
        LVt = carve(2, 8, P)
        AT = carve(2, 384)
        klt = carve(2, 2, P)
        assert used[0] <= decode
        KL = [carve(2, NP_, at=KT * T), carve(2, NP_)]
        assert used[0] <= P_Q * T
        stage_h = carve(HH, DV, at=early)
        vb = carve(2, HH * DV)
        assert used[0] <= early + CT * T
        vss = stage_h[0:NS, :, :].rearrange("p a b -> p (a b)")
        KK = sq
        ysq, osq, ms = PR[:, P_Z:P_Z + 8], PR[:, P_V:P_V + 8], PR[:, P_Q:P_Q + 8]
        htok = carve(3, D, at=early)
        EW = [carve(3, 4096, at=slot0), carve(3, 4096, at=0)]
        xg = carve(2, D)
        xgT = carve(2, KT, P)
        sil = carve(2, FF)
        act = carve(2, FF)
        actT = carve(2, 4, P)
        ys = carve(2, D)
        assert used[0] <= early
        rv = carve(3 * E * RV // 2, at=slot0 + 12288).bitcast(BF16).rearrange("p (t e c) -> p t e c", t=3, c=RV)
        tabf = carve(3 * E, RV)
        Mt = carve(3, E)
        slot1 = carve(3, E)
        grest = carve(3, E)
        ple_in = carve(KT, T)
        OH = carve(OH_SLOTS * 3 * P // 2, at=used[0] - KT * T).bitcast(BF16).rearrange(
            "p (u t s) -> p u t s", u=OH_SLOTS, t=3)
        pairs = carve(3, 2, D, at=0)
        acc = carve(3, D)
        WP = carve(2, 4096, at=slot0)
        wpp = carve(2, D)
        ptok = carve(3, PLE)
        assert used[0] <= slot0 + 12288
        pT = carve(2, T, at=12288)
        gs = carve(2, T)
        ostage = carve(3, D)

        sm = [0]

        def small(*shape):
            n = int(np.prod(shape))
            v = smalls[:, sm[0]:sm[0] + n]
            sm[0] += n
            assert sm[0] <= 900
            if len(shape) == 1:
                return v
            names = "abcd"[:len(shape)]
            return v.rearrange(f"p ({' '.join(names)}) -> p {' '.join(names)}",
                               **{c: s for c, s in zip(names, shape)})

        wdt = small(KT, H)
        dtb = small(H)
        alog = small(H)
        aneg = small(H)
        dtr = small(3, H)
        dt1 = small(3, H)
        dt2 = small(3, H)
        dt3 = small(3, H)
        dt4 = small(3, H)
        dtv = small(3, H)
        av = small(3, H)
        wdec = small(2, H)
        ea = small(H)
        DX = small(NS, KT)
        EX = small(NS, KT)
        xds = small(NS, KT)
        yss = small(NS, KT)
        lbt = small(2, HH)
        lb = small(HH)
        oml = small(HH)
        lbe = small(3, HH)
        dpair = small(2)
        wr = sb("wr", [P, KT, 20])
        rb = sb("rb", [P, 20])
        rt = sb("rt", [P, 3, 20])
        rs = sb("rs", [P, 18, 3, 4])
        gates = sb("gates", [P, 3, E])
        r1 = sb("r1", [P, 8, 3])
        chips = sb("chips", [P, 2])
        row_of = ctx.enter_context(nc.sbuf_tensor("rows", [P, 2, 3 * E], mybir.dt.uint32))
        most = ctx.enter_context(nc.sbuf_tensor("most", [P, 1], mybir.dt.int32))
        dtx = sq[0:NS, 0:4, :].rearrange("p a b -> p (a b)")[:, 0:D]
        eax = sq[0:NS, 4:8, :].rearrange("p a b -> p (a b)")[:, 0:D]

        bank = [ctx.enter_context(nc.psum_tensor(f"bank{i}", [P, 512], F32)) for i in range(8)]

        a_full, a_took = sem("a_full"), sem("a_took")
        v_full, v_took = sem("v_full"), sem("v_took")
        ld_k = sem("ld_k")
        ld_x = [sem(f"ld_x{i}") for i in range(3)]
        tail_out, st_out = sem("tail_out"), sem("st_out")
        ld_p, ld_prm = sem("ld_p"), sem("ld_prm")
        ld_s = sem("ld_s")
        ld_r = sem("ld_r")
        w_slot = [sem("w_slot0"), sem("w_slot1")]
        sq_done, norm_done = sem("sq_done"), sem("norm_done")
        dve, o_dve = sem("dve"), sem("o_dve")
        ea_ready = sem("ea_ready")
        conv_done = sem("conv_done")
        silu_done = sem("silu_done")
        sp = sem("softplus")
        dt_ready = sem("dt_ready")
        am_ready = sem("am_ready")
        xw_ready = sem("xw_ready")
        dtx_ready = sem("dtx_ready")
        m_ready = sem("m_ready")
        bcs_out, bcb_in = sem("bcs_out"), [sem(f"bcb_in{i}") for i in range(4)]
        s1_in = [sem(f"s1_in{i}") for i in range(4)]
        s1_new, s1_out = sem("s1_new"), [sem(f"s1_out{i}") for i in range(4)]
        xds_ready = sem("xds_ready")
        u1_ready, u1_used = sem("u1_ready"), sem("u1_used")
        store = sem("store")
        hg_sig, hg_fk = sem("hg_sig"), sem("hg_fk")
        drow_ready = sem("drow_ready")
        mixers_done = sem("mixers_done")
        lb_exp, lb_in = sem("lb_exp"), sem("lb_in")
        qk_ready, kl_ready = sem("qk_ready"), sem("kl_ready")
        at_ready = sem("at_ready")
        vs_out, vb_in = sem("vs_out"), [sem("vb_in0"), sem("vb_in1")]
        s2_in = [sem("s2_in0"), sem("s2_in1")]
        s2_new, s2_out = sem("s2_new"), [sem("s2_out0"), sem("s2_out1")]
        u2_ready = sem("u2_ready")
        y_raw, gate_silu, sq_m, sd_m, mixed = (sem("y_raw"), sem("gate_silu"), sem("sq_m"), sem("sd_m"),
                                               sem("mixed"))
        r_in, r_exp = sem("r_in"), sem("r_exp")
        hrow_out = sem("hrow_out")
        mt_ready, oh_ready, oh_used, tab_ready = sem("mt_ready"), sem("oh_ready"), sem("oh_used"), sem("tab_ready")
        xg_clear = sem("xg_clear")
        pair_in, acc_ready = sem("pair_in"), sem("acc_ready")
        main, over = ExpertSems(sem, "m"), ExpertSems(sem, "o")
        o_tab, o_tab_took, o_oh_ready, o_oh_used = sem("o_tab"), sem("o_tab_took"), sem("o_oh_ready"), sem("o_oh_used")
        wp_again = sem("wp_again")
        ld_pg, ld_pp, x_new = sem("ld_pg"), sem("ld_pp"), sem("x_new")
        o_store = sem("o_store")
        block = ctx.enter_context(nc.Block())


        @block.sync
        def _(eng):
            eng.dma_start(K[:, :], consts).then_inc(ld_k, 16)
            for i, (t0, n) in enumerate(TOK):
                src = ins["x_prompt"][0, t0:t0 + n] if i < 2 else ins["x_sample"][:, 0]
                eng.dma_start(xtok[0:n, i], src).then_inc(ld_x[i], 16)

            starts = ([C_X + 512 * g for g in range(3)] + [C_Q + 512 * g for g in range(6)] +
                      [C_Z + 512 * g for g in range(2)] + [C_Q + 3 * D + 512 * g for g in range(2)])
            eng.wait_ge(ld_prm, 16 * 9)
            for g, c in enumerate(starts):
                if g >= 2:
                    eng.wait_ge(a_full, ja["proj", 4 * g - 5] + 1)
                eng.dma_start(W[:, g % 2].rearrange("p (k c) -> p k c", k=KT), w_in[:, :, c:c + 512]
                              ).then_inc(w_slot[g % 2], 16)

            def w_out_group(g):
                if g < 2:
                    eng.wait_ge(a_full, ja["proj", 4 * (11 + g) + 3] + 1)
                else:
                    eng.wait_ge(v_full, jv["mix", 2 * (g - 2) + 1] + 1)
                eng.dma_start(W[:, (13 + g) % 2].rearrange("p (k c) -> p k c", k=16),
                              w_out[:, :, 256 * g:256 * g + 256]).then_inc(w_slot[(13 + g) % 2], 16)

            for g in range(2):
                w_out_group(g)

            def weights(m, t, ex, h, p, first):
                for k, (name, slot, full, used_by) in enumerate((
                        ("w_exp_gate", m.wg, m.g_full, t - 1), ("w_exp_up", m.wu, m.u_full, t - 1),
                        ("w_exp_down", m.wd, m.d_full, t * 2 - 2))):
                    if not first:
                        eng.wait_ge(full, used_by)
                    eng.dma_start(EW[p][:, k].rearrange("p (k c) -> p k c", k=KT if k < 2 else 4),
                                  ins[name][0, ds(ex, 1)].rearrange("e (k p) c -> p (e k) c", p=P)
                                  ).then_inc(slot[p], 16)

            def ple_gate_weights(done):
                for g in range(2):
                    eng.dma_start(WP[:, g].rearrange("p (k c) -> p k c", k=KT),
                                  w_pg[:, :, 512 * g:512 * g + 512]).then_inc(done, 16)

            def ple_weights(done):
                eng.dma_start(ptok[:, 0:2], ins["p_prompt"][0, 0].rearrange("(t p) c -> p t c", p=P)).then_inc(done, 16)
                eng.dma_start(ptok[0:NS, 2], ins["p_sample"][0, :, 0]).then_inc(done, 16)
                eng.dma_start(wpp[:, :], w_pp).then_inc(done, 16)

            eng.wait_ge(v_full, jv["os", HH - 1] + 1)
            eng.wait_ge(a_took, ja["sth", HH - 1] + 1)
            eng.wait_ge(mixers_done, 1)
            weights(main, 0, 0, 0, 0, True)
            for g in range(2, 4):
                w_out_group(g)
            eng.wait_ge(v_full, jv["mix", KT - 1] + 1)
            weights(main, 1, 1, 0, 1, True)
            with eng.Fori(1, E // 2) as it:
                for p in range(2):
                    weights(main, it * 2 + p, it * 2 + p, it, p, False)
            eng.wait_ge(main.g_full, E - 1)
            eng.wait_ge(main.u_full, E - 1)
            ple_gate_weights(ld_pg)
            eng.wait_ge(main.d_full, 2 * (E - 1))
            ple_weights(ld_pp)
            eng.wait_ge(tab_ready, 1)
            crowded = eng.value_load(most[0:1, 0:1], min_val=0, max_val=T)
            with eng.If(crowded > P):
                eng.wait_ge(main.d_full, 2 * E)
                eng.wait_ge(ld_pp, 48)
                eng.wait_ge(ld_pg, 32)
                for t in range(2):
                    weights(over, t, t, 0, t, True)
                with eng.Fori(1, E // 2) as it:
                    for p in range(2):
                        weights(over, it * 2 + p, it * 2 + p, it, p, False)
                with eng.Fori(E // 2, E) as it:
                    for p in range(2):
                        weights(over, it * 2 + p, it * 2 + (p - E), it, p, False)
                eng.wait_ge(over.d_full, 4 * E)
                ple_gate_weights(wp_again)
                ple_weights(wp_again)
                for p in range(2):
                    eng.wait_ge(over.sent[p], 16 * E)
            eng.wait_ge(main.d_full, 2 * E)
            for p in range(2):
                eng.wait_ge(main.sent[p], 16 * (E // 2))
            for k in range(TOP_K):
                r = pair_rows[k * T:(k + 1) * T]
                eng.dma_start(pairs[:, 0:2, k], r[0:NP_].rearrange("(t p) d -> p t d", p=P)).then_inc(pair_in, 16)
                eng.dma_start(pairs[0:NS, 2, k], r[NP_:T]).then_inc(pair_in, 16)
            for tt, (t0, n) in enumerate(TOK):
                eng.wait_ge(a_took, ja["out", tt, 1] + 1)
                dst = outs[0][0, t0:t0 + n] if tt < 2 else outs[1][:, 0]
                eng.dma_start(dst, ostage[0:n, tt]).then_inc(o_store, 16)
            eng.wait_ge(o_store, 48)

        @block.gpsimd
        def _(eng):
            eng.dma_start(dpair[0:KT], ins["d_skip"][0].rearrange("(f h) -> f h", h=2)).then_inc(ld_p, 16)
            eng.dma_start(crow[0:24], ins["state_conv"][0].rearrange("b k c -> (b k) c")).then_inc(ld_p, 16)
            eng.dma_start(wdt, w_in[:, :, C_DT:C_DT + H]).then_inc(ld_s, 16)
            eng.dma_start(dtb, ins["dt_bias"][0:1].to_broadcast([P, H])).then_inc(ld_s, 16)
            eng.dma_start(alog, ins["a_log"][0:1].to_broadcast([P, H])).then_inc(ld_s, 16)
            eng.dma_start(wr[:, :, 0:4], ins["w_router_group"][0].rearrange("(k p) c -> p k c", p=P)).then_inc(ld_r, 16)
            eng.dma_start(wr[:, :, 4:20], ins["w_router_expert"][0].rearrange("(k p) c -> p k c", p=P)).then_inc(ld_r, 16)
            eng.dma_start(rb[:, 0:4], ins["b_router_group"][0:1].to_broadcast([P, 4])).then_inc(ld_r, 16)
            eng.dma_start(rb[:, 4:20], ins["b_router_expert"][0:1].rearrange("o g e -> o (g e)").to_broadcast([P, E])
                          ).then_inc(ld_r, 16)
            eng.dma_start(outs[6][0, :, 0:2], ins["state_conv"][0, :, 1:3]).then_inc(store, 16)
            n_store = 1

            def s1_load(b):
                eng.dma_start(S1[:, b % 4], ins["state_ssm"][0, b].rearrange("h p n -> (h p) n")
                              .rearrange("(f q) n -> q f n", q=P)).then_inc(s1_in[b % 4], 16)

            def s1_store(b):
                eng.wait_ge(s1_new, KT * (b + 1))
                eng.dma_start(outs[5][0, b].rearrange("h p n -> (h p) n").rearrange("(f q) n -> q f n", q=P),
                              S1[:, b % 4]).then_inc(s1_out[b % 4], 16)

            def bc_load(b):
                eng.dma_start(BCb[b % 4], bc_rows[b:b + 1].to_broadcast([P, 2 * G * N])).then_inc(bcb_in[b % 4], 16)

            for b in range(4):
                s1_load(b)
            eng.wait_ge(v_took, jv["bcs"] + 1)
            eng.dma_start(bc_rows, bcs[:, :]).then_inc(bcs_out, 16)
            eng.wait_ge(bcs_out, 16)
            for b in range(4):
                bc_load(b)
            eng.wait_ge(a_took, ja["tail", 2] + 1)
            eng.dma_start(outs[3][0, 0], tail[0:3]).then_inc(tail_out, 16)
            eng.dma_start(outs[6][0, :, 2], tail[3:11]).then_inc(tail_out, 16)
            for b in range(NS):
                if b + 4 < NS:
                    eng.wait_ge(s1_new, KT * (b + 1))
                    bc_load(b + 4)
                s1_store(b)
                if 1 <= b < NS - 3:
                    eng.wait_ge(s1_out[b - 1], 16)
                    s1_load(b + 3)

            def s2_load(b):
                eng.dma_start(S2[:, b % 2], ins["state_hgrn"][0, b].rearrange("h k v -> k h v")).then_inc(s2_in[b % 2], 16)

            def s2_store(b):
                eng.wait_ge(s2_new, HH * (b + 1))
                eng.dma_start(outs[7][0, b].rearrange("h k v -> k h v"), S2[:, b % 2]).then_inc(s2_out[b % 2], 16)

            def vb_load(b):
                eng.dma_start(vb[:, b % 2], v_rows[b:b + 1].to_broadcast([P, HH * DV])).then_inc(vb_in[b % 2], 16)

            for p in range(4):
                eng.wait_ge(s1_out[p], 16 * 2)
            for b in range(2):
                s2_load(b)
            eng.wait_ge(a_took, ja["st", 1] + 1)
            eng.dma_start(outs[2][0, 0].rearrange("h p n -> (h p) n").rearrange("(f q) n -> q f n", q=P),
                          stage).then_inc(st_out, 16)
            eng.wait_ge(a_took, ja["vs", 1] + 1)
            eng.dma_start(v_rows, vss).then_inc(vs_out, 16)
            eng.wait_ge(vs_out, 16)
            for b in range(2):
                vb_load(b)
            for b in range(NS):
                s2_store(b)
                if b + 2 < NS:
                    vb_load(b + 2)
                    eng.wait_ge(v_full, jv["os", b] + 1)
                    eng.wait_ge(s2_out[b % 2], 16 * (b // 2 + 1))
                    s2_load(b + 2)
            eng.wait_ge(a_took, ja["sth", HH - 1] + 1)
            eng.dma_start(outs[4][0, 0].rearrange("h k v -> k h v"), stage_h).then_inc(store, 16)
            n_store += 1
            eng.wait_ge(store, 16 * n_store)
            eng.wait_ge(tail_out, 32)
            eng.wait_ge(st_out, 16)
            for p in range(2):
                eng.wait_ge(s2_out[p], 16 * 4)
            eng.memset(chips[:, 0:1], 0.0).then_inc(mixers_done, 1)
            eng.wait_ge(v_full, jv["mix", KT - 1] + 1)
            for p in range(2):
                eng.memset(xg[:, p], 0.0).then_inc(xg_clear, 1)

            def gather(m, t, base):
                p = t % 2
                if t >= 2:
                    eng.wait_ge(m.x_full, 2 * (t - 2) + 2)
                eng.indirect_dma_start(
                    out=xg[:, p], out_offset=None, in_=h_rows,
                    in_offset=bass.IndirectOffsetOnAxis(ap=row_of[:, 0, base + t:base + t + 1], axis=0),
                    bounds_check=T - 1, oob_is_err=False).then_inc(m.rows[p], 16)

            def scatter(m, t, base):
                p = t % 2
                eng.wait_ge(m.d_took, 2 * (t + 1))
                eng.indirect_dma_start(
                    out=pair_rows, out_offset=bass.IndirectOffsetOnAxis(ap=row_of[:, 1, base + t:base + t + 1], axis=0),
                    in_=ys[:, p], in_offset=None,
                    bounds_check=TOP_K * T - 1, oob_is_err=False).then_inc(m.sent[p], 16)

            def tokens(m, n, base):
                for t in range(n + 4):
                    if base == 0 and t == TAB0:
                        eng.wait_ge(tab_ready, 2)
                    if t < n:
                        gather(m, t, base)
                    if t >= 4:
                        scatter(m, t - 4, base)

            eng.wait_ge(tab_ready, 1)
            eng.wait_ge(hrow_out, 48)
            eng.wait_ge(xg_clear, 2)
            tokens(main, E, 0)
            crowded = eng.value_load(most[0:1, 0:1], min_val=0, max_val=T)
            with eng.If(crowded > P):
                eng.wait_ge(o_tab_took, 1)
                for p in range(2):
                    eng.wait_ge(main.sent[p], 16 * (E // 2))
                tokens(over, 2 * E, E)
                for p in range(2):
                    eng.wait_ge(over.sent[p], 16 * E)
            for p in range(2):
                eng.wait_ge(main.sent[p], 16 * (E // 2))

        @block.tensor
        def _(eng):
            mm = nc.tensor.matmul

            def bank_a(n):
                if not isinstance(n, int) or n >= 4:
                    eng.wait_ge(a_took, n - 3)

            def open_a(*name):
                n = ja[name]
                bank_a(n)
                return bank[n % 4]

            def open_v(*name):
                n = jv[name]
                if n >= 4:
                    eng.wait_ge(v_took, n - 3)
                return bank[4 + n % 4]

            def norm_part(k, c):
                ps = open_a("norm", k) if c == 0 else bank[ja["norm", k] % 4]
                eng.wait_ge(sq_done, k * KT + c + 1)
                last = mm(ps[:, 0:T], ones, sq[:, c], start=(c == 0), stop=(c == KT - 1))
                if c == KT - 1:
                    last.then_inc(a_full, 1)

            eng.wait_ge(ld_k, 16)
            for ft in range(KT):
                ps = open_a("xT", ft)
                for i, (t0, n) in enumerate(TOK):
                    if ft == 0:
                        eng.wait_ge(ld_x[i], 16)
                    last = nc.tensor.transpose(ps[:, t0:t0 + n], xtok[0:n, i, ft * P:(ft + 1) * P], ident[0:n, 0:n])
                last.then_inc(a_full, 1)
            eng.wait_ge(ld_prm, 16 * 9)
            nc.tensor.transpose(open_v("prm")[:, 0:R_N], prow[0:R_N], ident[0:R_N, 0:R_N]).then_inc(v_full, 1)
            for ft in range(KT):
                norm_part(0, ft)
            def proj_tile(slot, j, first, n_bank, very_first=False):
                w = W[:, slot].rearrange("p (k c) -> p k c", k=KT)
                bank_a(first + j)
                ps = bank[(n_bank + j) % 4]
                for k in range(KT):
                    if very_first:
                        eng.wait_ge(norm_done, k + 1)
                    last = mm(ps[:, 0:T], w[:, k, j * P:(j + 1) * P], hT[:, k], start=(k == 0), stop=(k == KT - 1))
                last.then_inc(a_full, 1)

            def proj_group(g):
                eng.wait_ge(w_slot[g % 2], 16 * (g // 2 + 1))
                for j in range(4):
                    n = ja["proj", 4 * g]
                    proj_tile(g % 2, j, n, n, g == 0 and j == 0)

            proj_group(0)
            eng.wait_ge(drow_ready, 1)
            nc.tensor.transpose(open_v("prmD")[:, 0:KT], drow[0:KT], ident[0:KT, 0:KT]).then_inc(v_full, 1)
            ps = open_v("cst")
            eng.wait_ge(ld_p, 32)
            for c in range(CT):
                last = nc.tensor.transpose(ps[:, 24 * c:24 * c + 24], crow[0:24, c * P:(c + 1) * P], ident[0:24, 0:24])
            last.then_inc(v_full, 1)
            for g in range(1, 3):
                proj_group(g)
            eng.wait_ge(ld_s, 48)
            ps = open_v("dt")
            for i, (t0, n) in enumerate(TOK):
                for k in range(KT):
                    last = mm(ps[0:n, H * i:H * i + H], hT[:, k, t0:t0 + n], wdt[:, k], start=(k == 0), stop=(k == KT - 1))
            last.then_inc(v_full, 1)
            proj_group(3)

            eng.wait_ge(silu_done, CT)
            ps = open_v("bcs")
            for j in range(4):
                last = nc.tensor.transpose(ps[0:NS, j * P:(j + 1) * P], CV[:, KT + j, NP_:T], ident)
            last.then_inc(v_full, 1)
            for g in range(G):
                ps = open_v("cb", g)
                mm(ps[:, 0:NP_], CV[:, KT + g, 0:P], CV[:, KT + G + g, 0:NP_], start=True, stop=True)
                mm(ps[:, NP_:384], CV[:, KT + g, P:NP_], CV[:, KT + G + g, P:NP_], start=True, stop=True
                   ).then_inc(v_full, 1)
            eng.wait_ge(dtx_ready, 2)
            ps = open_v("dts")
            for k, src in enumerate((dtx, eax)):
                for f in range(KT):
                    c = (k * KT + f) * NS
                    last = nc.tensor.transpose(ps[:, c:c + NS], src[:, f * P:(f + 1) * P], ident[0:NS, 0:NS])
            last.then_inc(v_full, 1)
            ps = open_a("btok")
            for tt in range(2):
                for g in range(G):
                    last = nc.tensor.transpose(ps[:, (2 * tt + g) * P:(2 * tt + g + 1) * P],
                                               CV[:, KT + g, tt * P:(tt + 1) * P], ident)
            last.then_inc(a_full, 1)
            ps = open_a("w")
            eng.wait_ge(dt_ready, 1)
            after = K[:, K_AFTER:K_AFTER + P]
            mm(ps[:, 0:H], after, av[:, 0], start=True, stop=False)
            mm(ps[:, 0:H], ones, av[:, 1], start=False, stop=True)
            mm(ps[:, H:2 * H], after, av[:, 1], start=True, stop=True).then_inc(a_full, 1)
            for i in range(3):
                ps = open_a("tail", i)
                for j in range(4):
                    last = nc.tensor.transpose(ps[0:11, j * P:(j + 1) * P], PR[:, 4 * i + j, NP_ - 3:T], ident)
                last.then_inc(a_full, 1)
            for tt in range(2):
                for half in range(2):
                    ps = open_v("xs", tt, half)
                    for j in range(4):
                        last = nc.tensor.transpose(ps[:, j * P:(j + 1) * P],
                                                   CV[:, 4 * half + j, tt * P:(tt + 1) * P], ident)
                    last.then_inc(v_full, 1)

            with eng.Fori(0, 2) as it:
                for g in range(2):
                    n = ja["proj", 16 + 4 * g]
                    eng.wait_ge(w_slot[g], it * 16 + 48)
                    for j in range(4):
                        proj_tile(g, j, it * 8 + n, n)
            proj_group(8)

            def diff(h):
                ps = open_a("diff", h)
                eng.wait_ge(am_ready, 2)
                causal = K[:, K_CAUSAL:K_CAUSAL + P]
                mm(ps[:, 0:NP_], AM[:, 0, h], K[:, K_CAUSAL:K_CAUSAL + NP_], start=True, stop=False, skip_group_check=True)
                mm(ps[:, P:NP_], av[:, 1, h:h + 1].to_broadcast([P, P]), causal, start=False, stop=True,
                   skip_group_check=True)
                mm(ps[:, NP_:384], AM[:, 1, h], causal, start=True, stop=True, skip_group_check=True).then_inc(a_full, 1)

            def y_head(h):
                ps = bank[4 + jv["y", h // 2] % 4] if h % 2 else open_v("y", h // 2)
                eng.wait_ge(m_ready, h + 1)
                r = slice(HD * (h % 2), HD * (h % 2) + HD)
                c = slice(HD * h, HD * h + HD)
                m = EM[:, h % 4]
                mm(ps[r, 0:NP_], xdt[:, 0, c], m[:, 0:NP_], start=True, stop=False, skip_group_check=True)
                last = mm(ps[r, P:NP_], xdt[:, 1, c], m[:, NP_:384], start=False, stop=True, skip_group_check=True)
                if h % 2:
                    last.then_inc(v_full, 1)

            for h in range(H + 2):
                if h < H:
                    diff(h)
                if h >= 2:
                    y_head(h - 2)
            eng.wait_ge(xw_ready, 2)
            for i in range(2):
                ps = open_a("st", i)
                for j in range(4):
                    f = 4 * i + j
                    for tt in range(2):
                        last = mm(ps[:, j * P:(j + 1) * P], xw[:, tt, f * P:(f + 1) * P],
                                  btok[:, tt, (f // 4) * N:(f // 4 + 1) * N], start=(tt == 0), stop=(tt == 1))
                last.then_inc(a_full, 1)

            for tt in range(2):
                for half in range(2):
                    ps = open_a("vtok", tt, half)
                    for j in range(4):
                        last = nc.tensor.transpose(ps[:, j * P:(j + 1) * P],
                                                   PR[:, P_V + 4 * half + j, tt * P:(tt + 1) * P], ident)
                    last.then_inc(a_full, 1)
            for half in range(2):
                ps = open_a("vs", half)
                for j in range(4):
                    last = nc.tensor.transpose(ps[0:NS, j * P:(j + 1) * P], PR[:, P_V + 4 * half + j, NP_:T], ident)
                last.then_inc(a_full, 1)

            def levels(h):
                qk, hl = QK[h // 2 % 2], h % 2
                eng.wait_ge(qk_ready, 16 * (h // 2 + 1))
                for tt in range(2):
                    tk = slice(tt * P, (tt + 1) * P)
                    for b in range(2):
                        ps = open_v("lv", h, tt, b)
                        for j in range(4):
                            a = 4 * b + j
                            if a < LEVELS:
                                x = y = qk[:, hl, a, tk]
                            else:
                                x, y = KK[:, h, tk], PR[:, P_Q + h, tk]
                            last = mm(ps[:, j * P:(j + 1) * P], x, y, start=True, stop=True)
                        last.then_inc(v_full, 1)
                ps = open_v("off", h)
                mm(ps[:, 0:P], qk[:, hl, 7, 0:P], qk[:, hl, 7, P:NP_], start=True, stop=True).then_inc(v_full, 1)

            def decode_out(b):
                ps = open_v("os", b)
                for h in range(HH):
                    eng.wait_ge(s2_new, HH * b + h + 1)
                    last = mm(ps[:, h:h + 1], S2[:, b % 2, h], PR[:, P_Q + h, NP_ + b:NP_ + b + 1], start=True, stop=True)
                last.then_inc(v_full, 1)

            def head_out(h):
                hl = h % 2
                hc = slice(h * P, (h + 1) * P)
                ps = open_a("klt", h)
                eng.wait_ge(kl_ready, h // 2 + 1)
                for tt in range(2):
                    last = nc.tensor.transpose(ps[:, tt * P:(tt + 1) * P], KL[h // 2 % 2][:, hl, tt * P:(tt + 1) * P], ident)
                last.then_inc(a_full, 1)
                ps = open_a("o", h)
                eng.wait_ge(at_ready, 2 * (h + 1))
                eng.wait_ge(v_took, jv["off", h] + 1)
                mm(ps[:, 0:NP_], vtok[:, 0, hc], AT[:, hl, 0:NP_], start=True, stop=False, skip_group_check=True)
                mm(ps[:, P:NP_], vtok[:, 1, hc], AT[:, hl, NP_:384], start=False, stop=True, skip_group_check=True
                   ).then_inc(a_full, 1)
                ps = open_a("sth", h)
                eng.wait_ge(a_took, ja["klt", h] + 1)
                for tt in range(2):
                    last = mm(ps[:, 0:DV], klt[:, hl, tt], vtok[:, tt, hc], start=(tt == 0), stop=(tt == 1))
                last.then_inc(a_full, 1)

            for h in range(HH):
                levels(h)
                if h:
                    decode_out(h - 1)
                if h == Y_NORM_AT:
                    for g in range(G):
                        ps = open_a("yn", g)
                        eng.wait_ge(sq_m, 1)
                        for j in range(4):
                            last = mm(ps[:, 0:T], ones, ysq[:, 4 * g + j], start=(j == 0), stop=(j == 3))
                        last.then_inc(a_full, 1)
                g = 9 + h // 2
                if h % 2 == 0:
                    eng.wait_ge(w_slot[g % 2], 16 * (g // 2 + 1))
                for j in range(2):
                    if j and h:
                        head_out(h - 1)
                    jw = 2 * (h % 2) + j
                    n = ja["proj", P_Z + 2 * h + j] - jw
                    proj_tile(g % 2, jw, n, n)
            head_out(HH - 1)
            decode_out(HH - 1)

            def mix(c, ks):
                g = c // 2
                s = (13 + g) % 2
                if 0 in ks:
                    if c % 2 == 0:
                        eng.wait_ge(w_slot[s], 16 * ((13 + g) // 2 + 1))
                    eng.wait_ge(mixed, KT)
                    ps = open_v("mix", c)
                ps = bank[4 + jv["mix", c] % 4]
                w = W[:, s].rearrange("p (k c) -> p k c", k=16)
                for k in ks:
                    if c == 0 and k >= KT:
                        eng.wait_ge(mixed, k + 1)
                    x = PR[:, k] if k < KT else PR[:, P_F + k - KT]
                    last = mm(ps[:, 0:T], w[:, k, (c % 2) * P:(c % 2) * P + P], x, start=(k == 0), stop=(k == 15))
                if 15 in ks:
                    last.then_inc(v_full, 1)

            for c in range(4):
                mix(c, range(KT))
            for h in range(HH):
                ps = open_a("on", h)
                eng.wait_ge(sq_m, 2 + h // 4)
                mm(ps[:, 0:T], ones, osq[:, h], start=True, stop=True).then_inc(a_full, 1)
            for c in range(4):
                mix(c, range(KT, 16))
            for c in range(4, KT):
                mix(c, range(16))
                norm_part(1, c - 4)
            for c in range(4, KT):
                norm_part(1, c)

            eng.wait_ge(ld_r, 64)
            ps = open_v("rt")
            for i, (t0, n) in enumerate(TOK):
                for k in range(KT):
                    if i == 0:
                        eng.wait_ge(norm_done, KT + k + 1)
                    last = mm(ps[0:n, 20 * i:20 * i + 20], hT[:, k, t0:t0 + n], wr[:, k], start=(k == 0), stop=(k == KT - 1))
            last.then_inc(v_full, 1)
            for i, (t0, n) in enumerate(TOK):
                for half in range(2):
                    ps = open_a("ht", i, half)
                    for j in range(4):
                        last = nc.tensor.transpose(ps[0:n, j * P:(j + 1) * P], hT[:, 4 * half + j, t0:t0 + n], ident)
                    last.then_inc(a_full, 1)
            eng.wait_ge(mt_ready, 3)
            ps = open_v("cnt")
            for i in range(4):
                c = slice(E * i, E * i + E)
                for k in range(min(i + 1, 3)):
                    last = mm(ps[:, c], ones if k < i else K[:, K_CAUSAL:K_CAUSAL + P], Mt[:, k],
                              start=(k == 0), stop=(k == min(i, 2)))
            last.then_inc(v_full, 1)

            def table(ps, first, turns, ready, used_, done):
                for t in range(first, turns):
                    eng.wait_ge(ready, t + 1)
                    for i in range(3):
                        last = mm(ps[:, RV * (t - first):RV * (t - first + 1)], OH[:, t % OH_SLOTS, i], rv[:, i, t % E], start=(i == 0), stop=(i == 2))
                    last.then_inc(used_ if t < turns - 1 else done, 1)

            table(open_v("tab", 0), 0, TAB0, oh_ready, oh_used, v_full)
            table(open_v("tab", 1), TAB0, E, oh_ready, oh_used, v_full)

            def gate(m, t, h, p, wait=True):
                wg = EW[p][:, 0].rearrange("p (k c) -> p k c", k=KT)
                eng.wait_ge(m.x_took, t * 2 + 2)
                if wait:
                    eng.wait_ge(m.t_took, t - 1)
                eng.wait_ge(m.wg[p], h * 16 + 16)
                for k in range(KT):
                    last = mm(bank[p][:, :], xgT[:, p, k], wg[:, k], start=(k == 0), stop=(k == KT - 1))
                last.then_inc(m.g_full, 1)

            def turn_rows(m, t, h, p):
                eng.wait_ge(m.rows[p], h * 16 + 16)
                for half in range(2):
                    for j in range(4):
                        c = slice((4 * half + j) * P, (4 * half + j + 1) * P)
                        last = nc.tensor.transpose(bank[2 + half][:, j * P:(j + 1) * P], xg[:, p, c], ident)
                    last.then_inc(m.x_full, 1)

            def up(m, t, h, p, wait=True):
                wu = EW[p][:, 1].rearrange("p (k c) -> p k c", k=KT)
                if wait:
                    eng.wait_ge(m.u_took, t - 1)
                eng.wait_ge(m.wu[p], h * 16 + 16)
                for k in range(KT):
                    last = mm(bank[4 + p][:, :], xgT[:, p, k], wu[:, k], start=(k == 0), stop=(k == KT - 1))
                last.then_inc(m.u_full, 1)

            def down(m, t, h, p, wait=True):
                wd = EW[p][:, 2].rearrange("p (k c) -> p k c", k=4)
                eng.wait_ge(m.t_took, t + 1)
                eng.wait_ge(m.wd[p], h * 16 + 16)
                for half in range(2):
                    if wait:
                        eng.wait_ge(m.d_took, t * 2 - 1 + half)
                    for k in range(4):
                        last = mm(bank[6 + half][:, :], actT[:, p, k], wd[:, k, 512 * half:512 * half + 512],
                                  start=(k == 0), stop=(k == 3))
                    last.then_inc(m.d_full, 1)

            def turn_act(m, t, h, p):
                eng.wait_ge(m.u_took, t + 1)
                for k in range(4):
                    last = nc.tensor.transpose(bank[p][:, k * P:(k + 1) * P], act[:, p, k * P:(k + 1) * P], ident)
                last.then_inc(m.t_full, 1)

            def experts(m, n):
                turn_rows(m, 0, 0, 0)
                gate(m, 0, 0, 0, wait=False)
                turn_rows(m, 1, 0, 1)
                up(m, 0, 0, 0, wait=False)
                turn_act(m, 0, 0, 0)
                gate(m, 1, 0, 1, wait=False)
                turn_rows(m, 2, 1, 0)
                up(m, 1, 0, 1, wait=False)
                down(m, 0, 0, 0, wait=False)
                turn_act(m, 1, 0, 1)
                with eng.Fori(1, n // 2 - 1) as it:
                    t = it * 2
                    gate(m, t, it, 0)
                    turn_rows(m, t + 1, it, 1)
                    up(m, t, it, 0)
                    down(m, t - 1, it - 1, 1)
                    turn_act(m, t, it, 0)
                    gate(m, t + 1, it, 1)
                    turn_rows(m, t + 2, it + 1, 0)
                    up(m, t + 1, it, 1)
                    down(m, t, it, 0)
                    turn_act(m, t + 1, it, 1)
                t, h = n - 2, n // 2 - 1
                gate(m, t, h, 0)
                turn_rows(m, t + 1, h, 1)
                up(m, t, h, 0)
                down(m, t - 1, h - 1, 1)
                turn_act(m, t, h, 0)
                gate(m, t + 1, h, 1)
                up(m, t + 1, h, 1)
                down(m, t, h, 0)
                turn_act(m, t + 1, h, 1)
                down(m, t + 1, h, 1)
                eng.wait_ge(m.d_took, 2 * n)
                eng.wait_ge(m.t_took, n)

            eng.wait_ge(a_took, ja["ht", 2, 1] + 1)
            eng.wait_ge(v_took, jv["tab", 1] + 1)
            experts(main, E)
            eng.wait_ge(tab_ready, 1)
            crowded = eng.value_load(most[0:1, 0:1], min_val=0, max_val=T)
            with eng.If(crowded > P):
                table(bank[4], 0, 2 * E, o_oh_ready, o_oh_used, o_tab)
                eng.wait_ge(o_tab_took, 1)
                experts(over, 2 * E)
                eng.wait_ge(wp_again, 80)
            eng.wait_ge(ld_pp, 48)
            for c in range(2):
                ps = open_a("pT", c)
                for i, (t0, n) in enumerate(TOK):
                    last = nc.tensor.transpose(ps[:, t0:t0 + n], ptok[0:n, i, c * P:(c + 1) * P], ident[0:n, 0:n])
                last.then_inc(a_full, 1)
            eng.wait_ge(a_took, ja["pT", 1] + 1)
            for c in range(KT):
                ps = open_a("pp", c)
                for k in range(2):
                    last = mm(ps[:, 0:T], wpp[:, k, c * P:(c + 1) * P], pT[:, k], start=(k == 0), stop=(k == 1))
                last.then_inc(a_full, 1)
            for ft in range(KT):
                ps = open_v("yt", ft)
                eng.wait_ge(acc_ready, 3)
                for i, (t0, n) in enumerate(TOK):
                    last = nc.tensor.transpose(ps[:, t0:t0 + n], acc[0:n, i, ft * P:(ft + 1) * P], ident[0:n, 0:n])
                last.then_inc(v_full, 1)
            for c in range(KT):
                norm_part(2, c)

            eng.wait_ge(ld_pg, 32)
            for c in range(KT):
                w = WP[:, c // 4].rearrange("p (k c) -> p k c", k=KT)
                ps = open_a("pg", c)
                for k in range(KT):
                    if c == 0:
                        eng.wait_ge(norm_done, 2 * KT + k + 1)
                    last = mm(ps[:, 0:T], w[:, k, (c % 4) * P:(c % 4 + 1) * P], hT[:, k], start=(k == 0), stop=(k == KT - 1))
                last.then_inc(a_full, 1)
                if c > 4:
                    norm_part(3, c - 5)
            for c in range(3, KT):
                norm_part(3, c)
            for i, (t0, n) in enumerate(TOK):
                for half in range(2):
                    ps = open_a("out", i, half)
                    if i == 0:
                        eng.wait_ge(norm_done, 3 * KT + 4 * half + 4)
                    for j in range(4):
                        last = nc.tensor.transpose(ps[0:n, j * P:(j + 1) * P], hT[:, 4 * half + j, t0:t0 + n], ident)
                    last.then_inc(a_full, 1)

        @block.scalar
        def _(eng):
            activation = nc.scalar.activation
            def full(*name):
                n = ja[name]
                eng.wait_ge(a_full, n + 1)
                return bank[n % 4]

            for r, name, rows in ((R_CW, "conv_w", 48), (R_CB, "conv_b", 12), (R_SN, "ssd_norm_w", 8),
                                  (R_HN, "hg_norm_w", 8), (R_MIX, "norm_mix_w", 8), (R_FFN, "norm_ffn_w", 8),
                                  (R_PLE, "norm_ple_w", 8)):
                src = ins[name][0]
                src = (src.rearrange("k (c p) -> (k c) p", p=P) if name == "conv_w"
                       else src.rearrange("(c p) -> c p", p=P))
                eng.dma_start(prow[r:r + rows], src).then_inc(ld_prm, 16)
            eng.dma_start(prow[R_FIN:R_FIN + 8], ins["final_norm_w"].rearrange("(c p) -> c p", p=P)).then_inc(ld_prm, 16)
            eng.dma_start(prow[R_LB:R_LB + 16], ins["lb_logits"].rearrange("r (c p) -> (r c) p", p=P)).then_inc(ld_prm, 16)

            def root(k):
                activation(rstd[:, 1], full("norm", k)[:, 0:T], ACT.Sqrt, scale=1.0 / D, bias=eps).then_inc(a_took, 1)

            def square(c, sem_, count):
                eng.wait_ge(sem_, count)
                activation(sq[:, c], xT[:, c], ACT.Square).then_inc(sq_done, 1)

            eng.wait_ge(ld_k, 16)
            for ft in range(KT):
                ps = full("xT", ft)[:, 0:T]
                activation(sq[:, ft], ps, ACT.Square).then_inc(sq_done, 1)
                activation(xT[:, ft], ps, ACT.Copy).then_inc(a_took, 1)
            root(0)
            eng.wait_ge(lb_in, 2)
            activation(lbt, lbt, ACT.Exp).then_inc(lb_exp, 1)
            eng.wait_ge(ld_s, 48)
            activation(aneg, alog, ACT.Exp).then_inc(lb_exp, 1)

            def proj(n, func=ACT.Copy):
                activation(PR[:, n], full("proj", n)[:, 0:T], func).then_inc(a_took, 1)

            def conv_silu(c):
                eng.wait_ge(conv_done, c + 1)
                activation(CV[:, c], CV[:, c], ACT.Silu).then_inc(silu_done, 1)

            for n in range(CT):
                proj(n)
                if n >= 2:
                    conv_silu(n - 2)
            for c in (CT - 2, CT - 1):
                conv_silu(c)
            eng.wait_ge(sp, 1)
            activation(dt2, dt1, ACT.Exp, scale=-1.0).then_inc(sp, 1)
            eng.wait_ge(sp, 3)
            activation(dt4, dt3, ACT.Ln).then_inc(sp, 1)
            eng.wait_ge(dt_ready, 1)
            activation(ea[0:NS], av[0:NS, 2], ACT.Exp).then_inc(ea_ready, 1)
            for n in range(P_Q, P_Q + 4):
                proj(n)
            activation(btok[:, :, :].rearrange("p a b -> p (a b)"), full("btok")[:, :], ACT.Copy).then_inc(a_took, 1)
            activation(wdec[:, :, :].rearrange("p a b -> p (a b)"), full("w")[:, 0:2 * H], ACT.Exp).then_inc(a_took, 1)
            for i in range(3):
                activation(tail[0:11, i * 512:(i + 1) * 512], full("tail", i)[0:11, :], ACT.Copy).then_inc(a_took, 1)

            def f_gates(h):
                ps = full("proj", P_F + h)[:, 0:T]
                activation(KK[:, h], ps, ACT.Sigmoid, scale=-1.0).then_inc(hg_sig, 1)
                activation(PR[:, P_F + h], ps, ACT.Sigmoid).then_inc(a_took, 1)

            eng.wait_ge(v_full, jv["dts"] + 1)
            for n in range(P_Q + 4, P_V + 4):
                if P_F <= n < P_V:
                    f_gates(n - P_F)
                else:
                    proj(n)
                b = n - (P_Q + 5)
                if not 0 <= b < NS:
                    continue
                if b == 0:
                    eng.wait_ge(xds_ready, 1)
                if b >= 2:
                    eng.wait_ge(s1_new, KT * (b - 1))
                eng.wait_ge(bcb_in[b % 4], 16 * (b // 4 + 1))
                for f in range(KT):
                    activation(U1[:, b % 2, f], BCb[b % 4][:, (f // 4) * N:(f // 4 + 1) * N], ACT.Copy,
                               scale=xds[:, b, f:f + 1]).then_inc(u1_ready, 1)
            eng.wait_ge(s1_new, NS * KT)
            for n in range(P_V + 4, P_V + 8):
                proj(n)
            for h in range(H):
                if h >= 4:
                    eng.wait_ge(v_full, jv["y", (h - 4) // 2] + 1)
                activation(EM[:, h % 4], full("diff", h)[:, 0:384], ACT.Exp).then_inc(a_took, 1)
            for i in range(2):
                activation(stage[:, 4 * i:4 * i + 4].rearrange("p a b -> p (a b)"), full("st", i)[:, :],
                           ACT.Copy).then_inc(a_took, 1)
            eng.wait_ge(tail_out, 32)
            eng.wait_ge(bcs_out, 16)
            for tt in range(2):
                for half in range(2):
                    activation(vtok[:, tt, 512 * half:512 * half + 512], full("vtok", tt, half)[:, :],
                               ACT.Copy).then_inc(a_took, 1)
            eng.wait_ge(v_took, jv["y", KT - 1] + 1)
            for half in range(2):
                activation(vss[:, 512 * half:512 * half + 512], full("vs", half)[0:NS, :], ACT.Copy).then_inc(a_took, 1)

            def decode_kv(b):
                eng.wait_ge(vb_in[b % 2], 16 * (b // 2 + 1))
                for h in range(HH):
                    x = vb[:, b % 2, h * DV:(h + 1) * DV]
                    activation(x, x, ACT.Copy, scale=KK[:, h, NP_ + b:NP_ + b + 1]).then_inc(u2_ready, 1)

            def head_take(h):
                hl = h % 2
                if h == 0:
                    eng.wait_ge(st_out, 16)
                activation(klt[:, hl].rearrange("p a b -> p (a b)"), full("klt", h)[:, 0:NP_], ACT.Copy).then_inc(a_took, 1)
                activation(PR[:, P_F + h, 0:NP_], full("o", h)[:, 0:NP_], ACT.Copy).then_inc(a_took, 1)
                if h == 0:
                    eng.wait_ge(vs_out, 16)
                activation(stage_h[:, h], full("sth", h)[:, 0:DV], ACT.Copy).then_inc(a_took, 1)

            eng.wait_ge(hg_fk, 2 * HH)
            decode_kv(0)
            for h in range(HH):
                if h == Y_NORM_AT:
                    eng.wait_ge(y_raw, 1)
                    activation(ysq, PR[:, 0:KT], ACT.Square).then_inc(sq_m, 1)
                    for g in range(G):
                        activation(rstd[:, g], full("yn", g)[:, 0:T], ACT.Ln, scale=1.0 / (SD // G), bias=eps
                                   ).then_inc(a_took, 1)
                    eng.wait_ge(a_took, ja["yn", 1] + 1)
                    activation(rstd[:, :, :], rstd[:, :, :], ACT.Exp, scale=-0.5).then_inc(sd_m, 1)
                proj(P_Z + 2 * h, ACT.Silu)
                if h:
                    head_take(h - 1)
                proj(P_Z + 2 * h + 1, ACT.Silu)
                if h < HH - 1:
                    decode_kv(h + 1)
            head_take(HH - 1)
            eng.wait_ge(v_took, jv["os", HH - 1] + 1)
            eng.wait_ge(a_took, ja["sth", HH - 1] + 1)
            for i in range(2):
                activation(osq[:, 4 * i:4 * i + 4], PR[:, P_F + 4 * i:P_F + 4 * i + 4], ACT.Square).then_inc(sq_m, 1)
            for h in range(HH):
                activation(ms[:, h], full("on", h)[:, 0:T], ACT.Ln, scale=1.0 / DV, bias=eps).then_inc(a_took, 1)
            eng.wait_ge(a_took, ja["on", HH - 1] + 1)
            for i in range(2):
                activation(ms[:, 4 * i:4 * i + 4], ms[:, 4 * i:4 * i + 4], ACT.Exp, scale=-0.5).then_inc(sd_m, 1)
            for c in range(KT):
                square(c, v_took, jv["mix", c] + 1)
            root(1)
            def turned_rows(m, t, p):
                for half in range(2):
                    eng.wait_ge(m.x_full, t * 2 + (half + 1))
                    activation(xgT[:, p, 4 * half:4 * half + 4].rearrange("p k c -> p (k c)"), bank[2 + half][:, :],
                               ACT.Copy).then_inc(m.x_took, 1)

            def silu(m, t, p, wait=True):
                eng.wait_ge(m.g_full, t + 1)
                if wait:
                    eng.wait_ge(m.u_took, t - 1)
                activation(sil[:, p], bank[p][:, :], ACT.Silu).then_inc(m.g_took, 1)

            def turned_act(m, t, p):
                eng.wait_ge(m.t_full, t + 1)
                activation(actT[:, p].rearrange("p k c -> p (k c)"), bank[p][:, :], ACT.Copy).then_inc(m.t_took, 1)

            def experts(m, n):
                turned_rows(m, 0, 0)
                for t in range(2):
                    silu(m, t, t, wait=False)
                    turned_rows(m, t + 1, 1 - t)
                    turned_act(m, t, t)
                with eng.Fori(1, n // 2 - 1) as it:
                    for p in range(2):
                        t = it * 2 + p
                        silu(m, t, p)
                        turned_rows(m, t + 1, 1 - p)
                        turned_act(m, t, p)
                silu(m, n - 2, 0)
                turned_rows(m, n - 1, 1)
                turned_act(m, n - 2, 0)
                silu(m, n - 1, 1)
                turned_act(m, n - 1, 1)

            eng.wait_ge(r_in, 1)
            activation(rs[:, 1], rs[:, 0], ACT.Exp).then_inc(r_exp, 1)
            for i, (t0, n) in enumerate(TOK):
                if i == 1:
                    eng.wait_ge(r_in, 2)
                    activation(rs[:, 9], rs[:, 8], ACT.Exp).then_inc(r_exp, 1)
                for half in range(2):
                    activation(htok[0:n, i, 512 * half:512 * half + 512], full("ht", i, half)[0:n, :],
                               ACT.Copy).then_inc(a_took, 1)
                eng.wait_ge(a_took, ja["ht", i, 1] + 1)
                eng.dma_start(h_rows[t0:t0 + n], htok[0:n, i]).then_inc(hrow_out, 16)
            experts(main, E)
            eng.wait_ge(tab_ready, 1)
            crowded = eng.value_load(most[0:1, 0:1], min_val=0, max_val=T)
            with eng.If(crowded > P):
                experts(over, 2 * E)
            for c in range(2):
                activation(pT[:, c], full("pT", c)[:, 0:T], ACT.Copy).then_inc(a_took, 1)
            for c in range(KT):
                activation(ple_in[:, c], full("pp", c)[:, 0:T], ACT.Copy).then_inc(a_took, 1)
            eng.wait_ge(hrow_out, 48)
            for c in range(KT):
                square(c, v_took, jv["yt", c] + 1)
            root(2)
            for c in range(KT):
                if c >= 2:
                    square(c - 2, x_new, c - 1)
                activation(gs[:, c % 2], full("pg", c)[:, 0:T], ACT.Sigmoid).then_inc(a_took, 1)
            for c in (KT - 2, KT - 1):
                square(c, x_new, c + 1)
            root(3)
            for i, (t0, n) in enumerate(TOK):
                for half in range(2):
                    activation(ostage[0:n, i, 512 * half:512 * half + 512], full("out", i, half)[0:n, :],
                               ACT.Copy).then_inc(a_took, 1)

        @block.vector
        def _(eng):
            own = {dve: 0, o_dve: 0}

            def link(ins_, chain=dve):
                own[chain] += 1
                ins_.then_inc(chain, 1)
                eng.wait_ge(chain, own[chain])

            def full(*name):
                n = jv[name]
                eng.wait_ge(v_full, n + 1)
                return bank[4 + n % 4]

            def took(*name):
                eng.wait_ge(v_took, jv[name] + 1)

            def tt(out, a, b, op=ALU.mult):
                return nc.vector.tensor_tensor(out, a, b, op)

            def ts(out, a, s1, op0, s2=None, op1=None):
                if op1 is None:
                    return nc.vector.tensor_scalar(out, a, s1, None, op0)
                return nc.vector.tensor_scalar(out, a, s1, s2, op0, op1)

            def stt(out, a, s, b, op0, op1):
                return nc.vector.scalar_tensor_tensor(out, a, s, b, op0, op1)

            def col(r):
                return prm[:, r:r + 1]

            def spread(x, n):
                rows = x.shape[0]
                return x.rearrange("p (h o) -> p h o", o=1).to_broadcast([rows, x.shape[1], n])

            def norm(k, row):
                eng.wait_ge(a_took, ja["norm", k] + 1)
                link(nc.vector.reciprocal(rstd[:, 0], rstd[:, 1]))
                for ft in range(KT):
                    stt(hT[:, ft], xT[:, ft], col(row + ft), rstd[:, 0], ALU.mult, ALU.mult).then_inc(norm_done, 1)

            nc.vector.tensor_copy(prm[:, 0:R_N], full("prm")[:, 0:R_N]).then_inc(v_took, 1)
            took("prm")
            norm(0, R_MIX)
            eng.wait_ge(ld_p, 32)
            nc.vector.tensor_copy(drow[0:KT].rearrange("f (h p) -> f h p", h=2), spread(dpair[0:KT], HD)
                                  ).then_inc(drow_ready, 1)
            l0, l1 = prm[:, R_LB:R_LB + HH], prm[:, R_LB + HH:R_LB + 2 * HH]
            link(tt(lbe[:, 0], l0, l1, ALU.max))
            tt(lbt[:, 0], l0, lbe[:, 0], ALU.subtract).then_inc(lb_in, 1)
            tt(lbt[:, 1], l1, lbe[:, 0], ALU.subtract).then_inc(lb_in, 1)
            nc.vector.tensor_copy(prm[:, R_N:R_N + KT], full("prmD")[:, 0:KT]).then_inc(v_took, 1)
            nc.vector.tensor_copy(convu.rearrange("p c b k -> p (c b k)"), full("cst")[:, 0:288]).then_inc(v_took, 1)
            took("cst")
            eng.wait_ge(lb_exp, 2)
            link(tt(lbe[:, 1], lbt[:, 0], lbt[:, 1], ALU.add))
            link(nc.vector.reciprocal(lbe[:, 2], lbe[:, 1]))
            tt(lb, lbt[:, 0], lbe[:, 2])
            link(tt(oml, lbt[:, 1], lbe[:, 2]))
            for c in range(CT):
                eng.wait_ge(a_took, ja["proj", c] + 1)
                raw, out = PR[:, c], CV[:, c]
                link(ts(out, raw, col(R_CW + 3 * CT + c), ALU.mult, col(R_CB + c), ALU.add))
                old = convu[:, c].rearrange("p b k -> p k b")
                for k in range(3):
                    s = 3 - k
                    stt(out[:, s:NP_], raw[:, 0:NP_ - s], col(R_CW + k * CT + c), out[:, s:NP_], ALU.mult, ALU.add)
                    last = stt(out[:, NP_:T], old[:, k], col(R_CW + k * CT + c), out[:, NP_:T], ALU.mult, ALU.add)
                    if k < 2:
                        link(last)
                last.then_inc(conv_done, 1)
            link(nc.vector.memset(dtr, 0.0))
            ps = full("dt")
            link(tt(dtr[:, 0:2], ps[:, 0:2 * H].rearrange("p (t h) -> p t h", h=H),
                    dtb.rearrange("p (o h) -> p o h", o=1).to_broadcast([P, 2, H]), ALU.add))
            tt(dtr[0:NS, 2], ps[0:NS, 2 * H:3 * H], dtb[0:NS], ALU.add).then_inc(v_took, 1)
            took("dt")
            link(ts(dt2, dtr, -1.0, ALU.mult))
            tt(dt1, dt2, dtr, ALU.max).then_inc(sp, 1)
            eng.wait_ge(sp, 2)
            ts(dt3, dt2, 1.0, ALU.add).then_inc(sp, 1)
            eng.wait_ge(sp, 4)
            link(ts(dt1, dt3, 1.0, ALU.is_equal))
            link(ts(dt3, dt3, -1.0, ALU.add))
            link(tt(dt3, dt3, dt1, ALU.add))
            link(tt(dt4, dt4, dt1, ALU.add))
            link(nc.vector.reciprocal(dtv, dt3))
            link(tt(dt4, dt4, dt2))
            link(tt(dt4, dt4, dtv))
            link(stt(dtv, dtr, 0.0, dt4, ALU.max, ALU.add))
            stt(av, dtv, -1.0, aneg.rearrange("p (o h) -> p o h", o=1).to_broadcast([P, 3, H]),
                ALU.mult, ALU.mult).then_inc(dt_ready, 1)
            eng.wait_ge(dt_ready, 1)
            nc.vector.tensor_copy(dtx.rearrange("p (h q) -> p h q", q=HD), spread(dtv[0:NS, 2], HD)).then_inc(dtx_ready, 1)
            eng.wait_ge(ea_ready, 1)
            nc.vector.tensor_copy(eax.rearrange("p (h q) -> p h q", q=HD), spread(ea[0:NS], HD)).then_inc(dtx_ready, 1)
            after = K[:, K_AFTER:K_AFTER + P].rearrange("p (o s) -> p o s", o=1).to_broadcast([P, H, P])
            nc.vector.tensor_copy(bcs, full("bcs")[0:NS, :]).then_inc(v_took, 1)
            for g in range(G):
                tt(CBm[:, g], full("cb", g)[:, 0:384], K[:, K_CAUSAL:K_CAUSAL + 384]).then_inc(v_took, 1)
            ps = full("dts")
            link(nc.vector.tensor_copy(DX, ps[:, 0:64].rearrange("p (f b) -> p b f", f=KT)))
            nc.vector.tensor_copy(EX, ps[:, 64:128].rearrange("p (f b) -> p b f", f=KT)).then_inc(v_took, 1)
            took("dts")
            tt(xds, CV[:, 0:KT, NP_:T].rearrange("p f b -> p b f"), DX).then_inc(xds_ready, 1)
            for i in range(2):
                for half in range(2):
                    tt(xdt[:, i, 512 * half:512 * half + 512].rearrange("p (h q) -> p h q", q=HD),
                       full("xs", i, half)[:, :].rearrange("p (h q) -> p h q", q=HD),
                       spread(dtv[:, i, 8 * half:8 * half + 8], HD)).then_inc(v_took, 1)
            for i in range(2):
                tt(AM[:, i], after, spread(av[:, i], P)).then_inc(am_ready, 1)
            took("xs", 1, 1)
            eng.wait_ge(a_took, ja["w"] + 1)
            for i in range(2):
                tt(xw[:, i].rearrange("p (h q) -> p h q", q=HD), xdt[:, i].rearrange("p (h q) -> p h q", q=HD),
                   spread(wdec[:, i], HD)).then_inc(xw_ready, 1)

            for b in range(NS):
                s = b % 2
                eng.wait_ge(s1_in[b % 4], 16 * (b // 4 + 1))
                eng.wait_ge(bcb_in[b % 4], 16 * (b // 4 + 1))
                for f in range(KT):
                    eng.wait_ge(u1_ready, b * KT + f + 1)
                    st = S1[:, b % 4, f]
                    stt(st, st, EX[:, b, f:f + 1], U1[:, s, f], ALU.mult, ALU.add).then_inc(u1_used, 1)
                for f in range(KT):
                    eng.wait_ge(u1_used, b * KT + f + 1)
                    nc.vector.tensor_tensor_reduce(
                        U1[:, s, f], S1[:, b % 4, f], BCb[b % 4][:, (G + f // 4) * N:(G + f // 4 + 1) * N], 1.0, 0.0,
                        ALU.mult, ALU.add, yss[:, b, f:f + 1]).then_inc(s1_new, 1)
            eng.wait_ge(s1_new, NS * KT)
            link(tt(DX, CV[:, 0:KT, NP_:T].rearrange("p f b -> p b f"),
                    prm[:, R_N:R_N + KT].rearrange("p (o f) -> p o f", o=1).to_broadcast([P, NS, KT])))
            eng.wait_ge(a_took, ja["tail", 2] + 1)
            link(tt(PR[:, 0:KT, NP_:T].rearrange("p f b -> p b f"), yss, DX, ALU.add))

            def forget(h):
                eng.wait_ge(hg_sig, h + 1)
                eng.wait_ge(a_took, ja["proj", P_F + h] + 1)
                if h:
                    eng.wait_ge(hg_fk, 2 * h)
                ts(KK[:, h], KK[:, h], oml[:, h:h + 1], ALU.mult).then_inc(hg_fk, 1)
                ts(PR[:, P_F + h], PR[:, P_F + h], oml[:, h:h + 1], ALU.mult, lb[:, h:h + 1], ALU.add).then_inc(hg_fk, 1)

            def halves(x, s):
                y = x.rearrange("p h (n w s) -> p h n w s", w=2, s=s)
                return y[:, :, :, 0], y[:, :, :, 1]

            def last_of(x, s):
                return x[:, :, :, s - 1:s].to_broadcast([P, 2, NP_ // (2 * s), s])

            def tree(pair, first=0, stop=8):
                h = slice(2 * pair, 2 * pair + 2)
                f2 = PR[:, P_F + 2 * pair:P_F + 2 * pair + 2, 0:NP_]
                q2 = PR[:, P_Q + 2 * pair:P_Q + 2 * pair + 2, 0:NP_]
                k2 = KK[:, h, 0:NP_]
                qk = QK[pair % 2]
                if pair >= 2 and first == 0:
                    eng.wait_ge(v_full, jv["off", 2 * pair - 3] + 1)
                if first == 0:
                    nc.vector.tensor_copy(R, f2)
                    link(nc.vector.memset(L, 1.0))
                for a in range(first, stop):
                    s = 2 ** a
                    ql, qr = halves(q2, s)
                    kl, kr = halves(k2, s)
                    Rl, Rr = halves(R, s)
                    Ll, Lr = halves(L, s)
                    ol, orr = halves(qk[:, :, a], s)
                    tt(ol, kl, Ll).then_inc(qk_ready, 1)
                    if a:
                        eng.wait_ge(dve, own[dve])
                    own[dve] += 1
                    tt(Ll, Ll, last_of(Rr, s)).then_inc(dve, 1)
                    tt(orr, qr, Rr).then_inc(qk_ready, 1)
                    eng.wait_ge(dve, own[dve])
                    if a < 7:
                        own[dve] += 1
                        tt(Rr, Rr, last_of(Rl, s)).then_inc(dve, 1)
                if stop == 8:
                    if pair >= 2:
                        eng.wait_ge(a_full, ja["klt", 2 * pair - 3] + 1)
                    tt(KL[pair % 2], k2, L).then_inc(kl_ready, 1)

            for h in range(2):
                forget(h)
            eng.wait_ge(hg_fk, 4)
            for s in range(4):
                eng.wait_ge(s1_out[s], 16 * 2)
            tree(0)
            for h in range(2, HH):
                forget(h)

            def y_take(f):
                stt(PR[:, f, 0:NP_], CV[:, f, 0:NP_], col(R_N + f), full("y", f)[:, 0:NP_], ALU.mult, ALU.add
                    ).then_inc(v_took, 1)

            for h in range(H):
                eng.wait_ge(a_took, ja["diff", h] + 1)
                tt(EM[:, h % 4], EM[:, h % 4], CBm[:, h // 8]).then_inc(m_ready, 1)
                if h % 2 and h >= 3:
                    y_take(h // 2 - 1)
            y_take(KT - 1)

            eng.wait_ge(a_full, ja["st", 1] + 1)
            eng.wait_ge(st_out, 16)
            eng.wait_ge(hg_fk, 2 * HH)

            def mask(h, i, b):
                r = 2 * h + i - 1
                if b == 0 and r > 0:
                    eng.wait_ge(at_ready, r)
                tt(LVt[:, i, 4 * b:4 * b + 4].rearrange("p a b -> p (a b)"), full("lv", h, i, b)[:, :],
                   K[:, K_LM + 512 * b:K_LM + 512 * b + 512]).then_inc(v_took, 1)

            def level_sum(h, i):
                took("lv", h, i, 1)
                nc.vector.tensor_reduce(AT[:, h % 2, 256 * i:256 * i + P], LVt[:, i].rearrange("p a c -> p c a"),
                                        AX.X, ALU.add).then_inc(at_ready, 1)

            y = PR[:, 0:KT]
            o = PR[:, P_F:P_F + HH]
            for h in range(HH):
                mask(h, 0, 0)
                mask(h, 0, 1)
                mask(h, 1, 0)
                if h >= 2:
                    eng.wait_ge(a_full, ja["o", h - 2] + 1)
                level_sum(h, 0)
                mask(h, 1, 1)
                nc.vector.tensor_copy(AT[:, h % 2, P:2 * P], full("off", h)[:, 0:P]).then_inc(v_took, 1)
                level_sum(h, 1)
                if h:
                    nc.vector.tensor_copy(o[:, :, NP_ + h - 1], full("os", h - 1)[:, 0:HH]).then_inc(v_took, 1)
                eng.wait_ge(s2_in[h % 2], 16 * (h // 2 + 1))
                for k in range(HH):
                    eng.wait_ge(u2_ready, h * HH + k + 1)
                    st = S2[:, h % 2, k]
                    stt(st, st, PR[:, P_F + k, NP_ + h:NP_ + h + 1], vb[:, h % 2, k * DV:(k + 1) * DV],
                        ALU.mult, ALU.add).then_inc(s2_new, 1)
                if h < HH - 2:
                    tree(h // 2 + 1, 4 * (h % 2), 4 * (h % 2) + 4)
                if h == Y_NORM_AT - 2:
                    eng.wait_ge(a_took, ja["proj", P_Z + KT - 1] + 1)
                    tt(y, y, PR[:, P_Z:P_Z + KT]).then_inc(y_raw, 1)
                if h == HH - 1:
                    eng.wait_ge(sd_m, 1)
                    eng.wait_ge(y_raw, 1)
                    for f in range(KT):
                        stt(y[:, f], y[:, f], col(R_SN + f), rstd[:, f // 4], ALU.mult, ALU.mult).then_inc(mixed, 1)
            nc.vector.tensor_copy(o[:, :, T - 1], full("os", HH - 1)[:, 0:HH]).then_inc(v_took, 1)

            for h in range(HH):
                if h % 4 == 0:
                    eng.wait_ge(sq_m, 2 + h // 4)
                    eng.wait_ge(a_took, ja["proj", P_G + KT - 1] + 1)
                last = stt(o[:, h], o[:, h], col(R_HN + h), PR[:, P_G + h], ALU.mult, ALU.mult)
            link(last)
            for h in range(HH):
                if h % 4 == 0:
                    eng.wait_ge(sd_m, 2 + h // 4)
                tt(o[:, h], o[:, h], ms[:, h]).then_inc(mixed, 1)
            for c in range(KT):
                tt(xT[:, c], xT[:, c], full("mix", c)[:, 0:T], ALU.add).then_inc(v_took, 1)
            norm(1, R_FFN)

            def bc(x, n=4):
                return x.rearrange("p (t o) -> p t o", o=1).to_broadcast([P, 3, n])

            def red(out, x, op):
                link(nc.vector.tensor_reduce(out, x, AX.X, op))

            def first_max(out, x, tmp, m):
                red(m, x, ALU.max)
                link(tt(tmp, x, bc(m), ALU.is_equal))
                link(tt(tmp, tmp, w4))
                red(m, tmp, ALU.max)
                link(tt(out, tmp, bc(m), ALU.is_equal))

            w4 = K[:, K_W4:K_W4 + 4].rearrange("p (o e) -> p o e", o=1).to_broadcast([P, 3, 4])
            link(nc.vector.memset(rt[:, :, :], 0.0))
            eng.wait_ge(mixers_done, 1)
            for i in range(3):
                link(nc.vector.memset(Mt[:, i], 0.0))
            ps = full("rt")
            link(nc.vector.tensor_copy(rt[:, 0:2], ps[:, 0:40].rearrange("p (t c) -> p t c", c=20)))
            nc.vector.tensor_copy(rt[0:NS, 2], ps[0:NS, 40:60]).then_inc(v_took, 1)
            took("rt")
            lg = rt[:, :, 0:4]
            red(r1[:, 0], lg, ALU.max)
            tt(rs[:, 0], lg, bc(r1[:, 0]), ALU.subtract).then_inc(r_in, 1)
            link(tt(rs[:, 3], lg, rb[:, 0:4].rearrange("p (o e) -> p o e", o=1).to_broadcast([P, 3, 4]), ALU.add))
            ohg = rs[:, 5]
            first_max(ohg, rs[:, 3], rs[:, 4], r1[:, 3])
            eng.wait_ge(r_exp, 1)
            red(r1[:, 1], rs[:, 1], ALU.add)
            link(nc.vector.reciprocal(r1[:, 2], r1[:, 1]))
            link(tt(rs[:, 2], rs[:, 1], bc(r1[:, 2])))
            link(tt(rs[:, 6], rs[:, 2], ohg))
            red(r1[:, 5], rs[:, 6], ALU.add)
            g4 = gates[:, :, :].rearrange("p t (g e) -> p t g e", g=EG)
            ohb = ohg.rearrange("p t (g o) -> p t g o", o=1).to_broadcast([P, 3, EG, EPG])
            link(tt(g4, rt[:, :, 4:20].rearrange("p t (g e) -> p t g e", g=EG), ohb))
            red(rs[:, 7], g4.rearrange("p t g e -> p t e g"), ALU.add)
            link(tt(g4, rb[:, 4:20].rearrange("p (o g e) -> p o g e", o=1, g=EG).to_broadcast([P, 3, EG, EPG]), ohb))
            red(rs[:, 14], g4.rearrange("p t g e -> p t e g"), ALU.add)
            red(r1[:, 6], rs[:, 7], ALU.max)
            tt(rs[:, 8], rs[:, 7], bc(r1[:, 6]), ALU.subtract).then_inc(r_in, 1)
            link(tt(rs[:, 11], rs[:, 7], rs[:, 14], ALU.add))
            first_max(rs[:, 12], rs[:, 11], rs[:, 4], r1[:, 3])
            link(stt(rs[:, 13], rs[:, 12], -BIG, rs[:, 11], ALU.mult, ALU.add))
            first_max(rs[:, 15], rs[:, 13], rs[:, 4], r1[:, 3])
            link(tt(rs[:, 16], rs[:, 12], rs[:, 15], ALU.add))
            eng.wait_ge(r_exp, 2)
            red(r1[:, 7], rs[:, 9], ALU.add)
            link(nc.vector.reciprocal(r1[:, 0], r1[:, 7]))
            link(tt(rs[:, 10], rs[:, 9], bc(r1[:, 0])))
            link(tt(rs[:, 10], rs[:, 10], rs[:, 16]))
            red(r1[:, 1], rs[:, 10], ALU.add)
            link(nc.vector.reciprocal(r1[:, 2], r1[:, 1]))
            link(tt(r1[:, 2], r1[:, 2], r1[:, 5]))
            link(tt(rs[:, 10], rs[:, 10], bc(r1[:, 2])))
            link(tt(g4, ohb, rs[:, 10].rearrange("p t (o e) -> p t o e", o=1).to_broadcast([P, 3, EG, EPG])))
            chosen = rs[:, 16].rearrange("p t (o e) -> p t o e", o=1).to_broadcast([P, 3, EG, EPG])
            for i, (t0, n) in enumerate(TOK):
                tt(Mt[0:n, i].rearrange("p (g e) -> p g e", g=EG), ohb[0:n, i], chosen[0:n, i]).then_inc(mt_ready, 1)
            tokid = K[:, K_TOK:K_TOK + 3]
            nc.vector.tensor_copy(rv[:, :, :, 0], K[:, K_TOK:K_TOK + 1].rearrange("p (o c) -> p o c", o=1)
                                  .to_broadcast([P, 3, E]))
            for i, (t0, n) in enumerate(TOK):
                nc.vector.memset(rv[:, i, :, 1], float(t0))
            nc.vector.memset(rv[:, :, :, 6:RV], 1.0)
            ts(rv[:, :, :, 2].rearrange("p t (g e) -> p t g e", g=EG),
               rs[:, 15].rearrange("p t (o e) -> p t o e", o=1).to_broadcast([P, 3, EG, EPG]), float(T), ALU.mult)
            link(nc.vector.tensor_copy(rv[:, :, :, 3], gates[:, :, :]))
            link(tt(grest[:, :, :], gates[:, :, :], rv[:, :, :, 3], ALU.subtract))
            link(nc.vector.tensor_copy(rv[:, :, :, 4], grest[:, :, :]))
            link(tt(rv[:, :, :, 5], grest[:, :, :], rv[:, :, :, 4], ALU.subtract))
            ps = full("cnt")
            eng.wait_ge(mt_ready, 3)
            tt(slot1[:, :, :], ps[:, 0:3 * E].rearrange("p (t e) -> p t e", e=E), Mt[:, :, :])
            nc.vector.tensor_reduce(most[:, :], ps[:, 3 * E:4 * E], AX.X, ALU.max).then_inc(v_took, 1)
            took("cnt")

            def one_hots(start, turns, first, ready, used_, uncounted=OH_SLOTS + 99):
                for t in range(start, turns):
                    c = (first + t) // E
                    before = t - OH_SLOTS
                    if before >= 0 and before != uncounted:
                        eng.wait_ge(used_, before + (1 if before < uncounted else 0))
                    tt(OH[:, t % OH_SLOTS], K[:, K_IOTA + P * c:K_IOTA + P * c + P].rearrange("p (o s) -> p o s", o=1)
                       .to_broadcast([P, 3, P]),
                       slot1[:, :, t % E:t % E + 1].to_broadcast([P, 3, P]), ALU.is_equal).then_inc(ready, 1)

            def tables(ps, turns, first):
                return nc.vector.tensor_copy(tabf[:, first:first + turns].rearrange("p t c -> p (t c)"),
                                             ps[:, 0:RV * turns])

            def row_numbers(turns, first, chain):
                f = tabf[:, first:first + turns]
                tt(f[:, :, 3], f[:, :, 3], f[:, :, 4], ALU.add)
                tt(f[:, :, 0], f[:, :, 0], f[:, :, 1], ALU.add)
                link(ts(f[:, :, 6], f[:, :, 6], -FAR, ALU.mult, FAR, ALU.add), chain)
                link(tt(f[:, :, 0], f[:, :, 0], f[:, :, 6], ALU.add), chain)
                nc.vector.tensor_copy(row_of[:, 0, first:first + turns], f[:, :, 0])
                link(tt(f[:, :, 3], f[:, :, 3], f[:, :, 5], ALU.add), chain)
                return tt(row_of[:, 1, first:first + turns], f[:, :, 0], f[:, :, 2], ALU.add)

            one_hots(0, TAB0 + 1, 0, oh_ready, oh_used)
            tables(full("tab", 0), TAB0, 0).then_inc(v_took, 1)
            took("tab", 0)
            row_numbers(TAB0, 0, dve).then_inc(tab_ready, 1)
            one_hots(TAB0 + 1, E, 0, oh_ready, oh_used, TAB0 - 1)
            tables(full("tab", 1), E - TAB0, TAB0).then_inc(v_took, 1)
            took("tab", 1)
            row_numbers(E - TAB0, TAB0, dve).then_inc(tab_ready, 1)
            eng.wait_ge(tab_ready, 2)

            def mul(m, t, p, base):
                eng.wait_ge(m.u_full, t + 1)
                eng.wait_ge(m.g_took, t + 1)
                stt(act[:, p], sil[:, p], tabf[:, ds(t + base, 1), 3], bank[4 + p][:, :], ALU.mult, ALU.mult
                    ).then_inc(m.u_took, 1)

            def result(m, t, h, p, wait=True):
                for half in range(2):
                    eng.wait_ge(m.d_full, t * 2 + (1 + half))
                    if wait and not half:
                        eng.wait_ge(m.sent[p], h * 16)
                    nc.vector.tensor_copy(ys[:, p, 512 * half:512 * half + 512], bank[6 + half][:, :]).then_inc(m.d_took, 1)

            def experts(m, n, base):
                mul(m, 0, 0, base)
                mul(m, 1, 1, base)
                result(m, 0, 0, 0, wait=False)
                mul(m, 2, 0, base)
                result(m, 1, 0, 1, wait=False)
                mul(m, 3, 1, base)
                result(m, 2, 1, 0)
                with eng.Fori(2, n // 2) as it:
                    t = it * 2
                    mul(m, t, 0, base)
                    result(m, t - 1, it - 1, 1)
                    mul(m, t + 1, 1, base)
                    result(m, t, it, 0)
                result(m, n - 1, n // 2 - 1, 1)

            experts(main, E, 0)
            crowded = eng.value_load(most[0:1, 0:1], min_val=0, max_val=T)
            with eng.If(crowded > P):
                one_hots(0, 2 * E, E, o_oh_ready, o_oh_used)
                eng.wait_ge(o_tab, 1)
                link(tables(bank[4], 2 * E, E), o_dve)
                row_numbers(2 * E, E, o_dve).then_inc(o_tab_took, 1)
                eng.wait_ge(o_tab_took, 1)
                for p in range(2):
                    eng.wait_ge(main.sent[p], 16 * (E // 2))
                experts(over, 2 * E, E)
            eng.wait_ge(pair_in, 64)
            for i, (t0, n) in enumerate(TOK):
                tt(acc[0:n, i], pairs[0:n, i, 0], pairs[0:n, i, 1], ALU.add).then_inc(acc_ready, 1)
            for ft in range(KT):
                tt(xT[:, ft], xT[:, ft], full("yt", ft)[:, 0:T], ALU.add).then_inc(v_took, 1)
            norm(2, R_PLE)

            for c in range(KT):
                eng.wait_ge(a_took, ja["pg", c] + 1)
                link(tt(gs[:, c % 2], gs[:, c % 2], ple_in[:, c]))
                tt(xT[:, c], xT[:, c], gs[:, c % 2], ALU.add).then_inc(x_new, 1)
            norm(3, R_FIN)

_INS = ["x_prompt", "x_sample", "state_ssm", "state_conv", "state_hgrn", "p_prompt", "p_sample", "norm_mix_w",
        "w_in", "conv_w", "conv_b", "dt_bias", "a_log", "d_skip", "ssd_norm_w", "lb_logits", "hg_norm_w",
        "w_out", "norm_ffn_w", "w_router_group", "b_router_group", "w_router_expert", "b_router_expert",
        "w_exp_gate", "w_exp_up", "w_exp_down", "norm_ple_w", "w_ple_gate", "w_ple_proj", "final_norm_w"]
_OUTS = [(1, NP_, D), (NS, 1, D), (1, 1, H, HD, N), (1, 1, 3, CONV), (1, 1, HH, DK, DV),
         (1, NS, H, HD, N), (1, NS, 3, CONV), (1, NS, HH, DK, DV)]

def kernel(**inputs):
    import concourse.bacc as bacc
    from concourse.bass_utils import run_bass_kernel_spmd

    nc = bacc.Bacc("TRN2", target_bir_lowering=False, num_devices=1)
    arrays, ins = {}, {}
    for name in _INS:
        x = np.ascontiguousarray(inputs[name])
        arrays[f"in_{name}"] = x
        ins[name] = nc.dram_tensor(f"in_{name}", x.shape, mybir.dt.from_np(x.dtype), kind="ExternalInput").ap()
    arrays["constants"] = constants()
    consts = nc.dram_tensor("constants", (P, K_N), F32, kind="ExternalInput").ap()
    outs = [nc.dram_tensor(f"out_{i}", shape, F32, kind="ExternalOutput").ap() for i, shape in enumerate(_OUTS)]
    build(nc, ins, outs, consts)
    r = run_bass_kernel_spmd(nc, [arrays], core_ids=[0])
    return tuple(r.results[0][f"out_{i}"] for i in range(len(_OUTS)))
```
